# Optimizing a Trainium2 kernel written in Bass

```python
import jax
import jax.numpy as jnp
from jax import lax
import numpy as np

D_MODEL = 1024
BATCH = 1
SEQ = 256
DEPTH = 2
DEC_BATCH = 8
DEC_SEQ = 8
PAST_LEN = 256
PAGE_SIZE = 128

N_EVEN = (DEPTH + 1) // 2
N_ODD = DEPTH // 2
MIX_HALF = D_MODEL // 2
POOL_WINDOWS = (2, 4, 8, 16)
N_POOL_GROUPS = len(POOL_WINDOWS)
POOL_GROUP = MIX_HALF // N_POOL_GROUPS
POOL_BUF = max(POOL_WINDOWS) - 1
HEAD_DIM = 64
N_HEADS = MIX_HALF // HEAD_DIM
FORGET_BIAS = 3.0
Q_BLOCK = 128
CONV_WIDTH = 31
CONV_BUF = CONV_WIDTH - 1
N_MEM = 256
X_HEADS = 4
X_HEAD_DIM = 128
X_WIDTH = X_HEADS * X_HEAD_DIM
D_FF = 2816
N_EXPERTS = 8
TOP_K = 2
D_FF_EXPERT = 3584
EPS = 1e-6
IN_EVEN = 4 * MIX_HALF + N_HEADS
IN_ODD = 5 * MIX_HALF

kernel_name = 'hybrid_pool_fox_conformer_stickbreak_decode_step'

def rmsnorm(x, g):
    xf = x.astype(jnp.float32)
    y = xf * lax.rsqrt(jnp.mean(xf * xf, axis=-1, keepdims=True) + EPS)
    return (y * g.astype(jnp.float32)).astype(x.dtype)

def layernorm(x, g, b):
    xf = x.astype(jnp.float32)
    mu = jnp.mean(xf, axis=-1, keepdims=True)
    var = jnp.mean(jnp.square(xf - mu), axis=-1, keepdims=True)
    y = (xf - mu) * lax.rsqrt(var + EPS)
    return (y * g.astype(jnp.float32) + b.astype(jnp.float32)).astype(x.dtype)

def gather_pages(pool, page_table):
    rows = pool[page_table]
    return rows.reshape(page_table.shape[0], -1, *pool.shape[2:])

def sweep_query_blocks(block_fn, qs, q_pos):
    L = q_pos.shape[0]
    qb = min(Q_BLOCK, L)
    nb = -(-L // qb)
    pad = nb * qb - L

    def prep(a):
        a = jnp.pad(a, [(0, 0), (0, pad)] + [(0, 0)] * (a.ndim - 2))
        a = a.reshape(a.shape[0], nb, qb, *a.shape[2:])
        return jnp.moveaxis(a, 1, 0)

    qs_b = tuple(prep(a) for a in qs)
    pos_b = jnp.pad(q_pos, (0, pad), mode='edge').reshape(nb, qb)
    out = lax.map(lambda args: block_fn(*args), (*qs_b, pos_b))
    out = jnp.moveaxis(out, 0, 1)
    out = out.reshape(out.shape[0], nb * qb, *out.shape[3:])
    return out[:, :L]

def fox_attention(q, k, v, Fq, Fk, q_pos, k_pos):
    scale = HEAD_DIM ** -0.5
    FkT = jnp.swapaxes(Fk, 1, 2)[:, :, None, :]

    def block(qb, fqb, pb):
        s = jnp.einsum('bqhd,bkhd->bhqk', qb, k, preferred_element_type=jnp.float32) * scale
        s = s + jnp.swapaxes(fqb, 1, 2)[..., None] - FkT
        mask = k_pos[None, :] <= pb[:, None]
        p = jax.nn.softmax(jnp.where(mask, s, -jnp.inf), axis=-1)
        return jnp.einsum('bhqk,bkhd->bqhd', p.astype(v.dtype), v)

    return sweep_query_blocks(block, (q, Fq), q_pos)

def stick_breaking_attention(q, k, v, q_pos, k_pos):
    scale = HEAD_DIM ** -0.5

    def block(qb, pb):
        z = jnp.einsum('bqhd,bkhd->bhqk', qb, k, preferred_element_type=jnp.float32) * scale
        mask = k_pos[None, :] < pb[:, None]
        log_not = jnp.where(mask, jax.nn.log_sigmoid(-z), 0.0)
        csum = jnp.cumsum(log_not, axis=-1)
        log_a = jax.nn.log_sigmoid(z) + csum[..., -1:] - csum
        a = jnp.where(mask, jnp.exp(log_a), 0.0)
        return jnp.einsum('bhqk,bkhd->bqhd', a.astype(v.dtype), v)

    return sweep_query_blocks(block, (q,), q_pos)

def pool_mixer(p, prefix, start_pos, w_grp, scale):
    B, L, _ = p.shape
    full = jnp.concatenate([prefix, p], axis=1)
    c = jnp.pad(jnp.cumsum(full.astype(jnp.float32), axis=1), ((0, 0), (1, 0), (0, 0)))
    pos = start_pos + jnp.arange(L)
    means = []
    for g, w in enumerate(POOL_WINDOWS):
        sl = slice(g * POOL_GROUP, (g + 1) * POOL_GROUP)
        wsum = c[:, POOL_BUF + 1:, sl] - c[:, POOL_BUF + 1 - w:POOL_BUF + 1 - w + L, sl]
        count = jnp.minimum(pos + 1, w).astype(jnp.float32)
        means.append(wsum / count[None, :, None])
    mean = jnp.concatenate(means, axis=-1).astype(p.dtype)
    d = (mean - p).reshape(B, L, N_POOL_GROUPS, POOL_GROUP)
    y = jnp.einsum('blgc,gcd->blgd', d, w_grp).reshape(B, L, MIX_HALF)
    return y * scale, full[:, -POOL_BUF:]

def conv_module(a, gate, prefix, conv_w, conv_b, ln_g, ln_b):
    u = a * jax.nn.sigmoid(gate)
    full = jnp.concatenate([prefix, u], axis=1)
    y = lax.conv_general_dilated(full, conv_w[:, None, :], window_strides=(1,), padding='VALID',
                                 dimension_numbers=('NWC', 'WIO', 'NWC'),
                                 feature_group_count=MIX_HALF) + conv_b
    y = jax.nn.silu(layernorm(y, ln_g, ln_b))
    return y, full[:, -CONV_BUF:]

def even_mixer(h, past_k, past_v, past_logf, pool_prefix, w_in, b_f, w_pool_grp, pool_scale, g_fq, g_fk, w_out):
    B, L, _ = h.shape
    P = past_k.shape[1]
    z = h @ w_in
    p, q, k, v, fl = jnp.split(z, [MIX_HALF, 2 * MIX_HALF, 3 * MIX_HALF, 4 * MIX_HALF], axis=-1)
    y_a, pool_state = pool_mixer(p, pool_prefix, P, w_pool_grp, pool_scale)
    q = rmsnorm(q.reshape(B, L, N_HEADS, HEAD_DIM), g_fq)
    k = rmsnorm(k.reshape(B, L, N_HEADS, HEAD_DIM), g_fk)
    v = v.reshape(B, L, N_HEADS, HEAD_DIM)
    logf = jax.nn.log_sigmoid(fl.astype(jnp.float32) + b_f.astype(jnp.float32))
    k_all = jnp.concatenate([past_k, k], axis=1)
    v_all = jnp.concatenate([past_v, v], axis=1)
    F = jnp.cumsum(jnp.concatenate([past_logf.astype(jnp.float32), logf], axis=1), axis=1)
    y_b = fox_attention(q, k_all, v_all, F[:, P:], F, P + jnp.arange(L), jnp.arange(P + L))
    y = jnp.concatenate([y_a, y_b.reshape(B, L, MIX_HALF)], axis=-1) @ w_out
    return y, (k, v, logf.astype(h.dtype), pool_state)

def odd_mixer(h, past_k, past_v, conv_prefix, w_in, conv_w, conv_b, ln_g, ln_b, w_out):
    B, L, _ = h.shape
    P = past_k.shape[1]
    z = h @ w_in
    a, g, q, k, v = jnp.split(z, [MIX_HALF, 2 * MIX_HALF, 3 * MIX_HALF, 4 * MIX_HALF], axis=-1)
    y_c, conv_state = conv_module(a, g, conv_prefix, conv_w, conv_b, ln_g, ln_b)
    q = q.reshape(B, L, N_HEADS, HEAD_DIM)
    k = k.reshape(B, L, N_HEADS, HEAD_DIM)
    v = v.reshape(B, L, N_HEADS, HEAD_DIM)
    k_all = jnp.concatenate([past_k, k], axis=1)
    v_all = jnp.concatenate([past_v, v], axis=1)
    y_d = stick_breaking_attention(q, k_all, v_all, P + jnp.arange(L), jnp.arange(P + L))
    y = jnp.concatenate([y_c, y_d.reshape(B, L, MIX_HALF)], axis=-1) @ w_out
    return y, (k, v, conv_state)

def mem_keys_values(mem, w_ck, w_cv, g_ck):
    B, M, _ = mem.shape
    k = rmsnorm((mem @ w_ck).reshape(B, M, X_HEADS, X_HEAD_DIM), g_ck)
    v = (mem @ w_cv).reshape(B, M, X_HEADS, X_HEAD_DIM)
    return k, v

def cross_attention(h, mem_k, mem_v, w_cq, g_cq, w_co):
    B, L, _ = h.shape
    q = rmsnorm((h @ w_cq).reshape(B, L, X_HEADS, X_HEAD_DIM), g_cq)
    s = jnp.einsum('blhd,bmhd->bhlm', q, mem_k, preferred_element_type=jnp.float32) * X_HEAD_DIM ** -0.5
    p = jax.nn.softmax(s, axis=-1)
    o = jnp.einsum('bhlm,bmhd->blhd', p.astype(mem_v.dtype), mem_v).reshape(B, L, X_WIDTH)
    return o @ w_co

def swiglu(h, w_gate, w_up, w_down):
    return (jax.nn.silu(h @ w_gate) * (h @ w_up)) @ w_down

def moe_swiglu(h, w_router, b_router, we_gate, we_up, we_down):
    logits = (h @ w_router).astype(jnp.float32) + b_router.astype(jnp.float32)
    top_val, top_idx = lax.top_k(logits, TOP_K)
    gates = jax.nn.softmax(top_val, axis=-1)
    combine = jnp.sum(jax.nn.one_hot(top_idx, N_EXPERTS, dtype=jnp.float32) * gates[..., None], axis=-2)
    combine = combine.astype(h.dtype)
    out = jnp.zeros_like(h)
    for e in range(N_EXPERTS):
        out = out + combine[..., e:e + 1] * swiglu(h, we_gate[e], we_up[e], we_down[e])
    return out

def decoder_stack(x, mem_kv, fox_past, sb_past, pool_prefix, conv_prefix, W):
    new = {name: [] for name in ('fox_k', 'fox_v', 'fox_logf', 'sb_k', 'sb_v', 'pool', 'conv')}
    for layer in range(DEPTH):
        i = layer // 2
        h = rmsnorm(x, W['norm_mix'][layer])
        if layer % 2 == 0:
            y, (k, v, lf, ps) = even_mixer(h, *fox_past[i], pool_prefix[i], W['w_in_e'][i], W['b_f'][i],
                                           W['w_pool_grp'][i], W['pool_scale'][i], W['g_fq'][i],
                                           W['g_fk'][i], W['w_out_e'][i])
            new['fox_k'].append(k)
            new['fox_v'].append(v)
            new['fox_logf'].append(lf)
            new['pool'].append(ps)
        else:
            y, (k, v, cs) = odd_mixer(h, *sb_past[i], conv_prefix[i], W['w_in_o'][i], W['conv_w'][i],
                                      W['conv_b'][i], W['ln_g'][i], W['ln_b'][i], W['w_out_o'][i])
            new['sb_k'].append(k)
            new['sb_v'].append(v)
            new['conv'].append(cs)
        x = x + y
        x = x + cross_attention(rmsnorm(x, W['norm_cross'][layer]), *mem_kv[layer],
                                W['w_cq'][layer], W['g_cq'][layer], W['w_co'][layer])
        h = rmsnorm(x, W['norm_ffn'][layer])
        if layer % 2 == 0:
            x = x + swiglu(h, W['w_gate'][i], W['w_up'][i], W['w_down'][i])
        else:
            x = x + moe_swiglu(h, W['w_router'][i], W['b_router'][i], W['we_gate'][i],
                               W['we_up'][i], W['we_down'][i])
    return x, new

def setup_inputs(seed: int = 0) -> dict:
    key = jax.random.key(seed)
    keys = jax.random.split(key, 48)
    idx = iter(range(48))

    def nrm(shape, scale=1.0):
        return scale * jax.random.normal(keys[next(idx)], shape, jnp.float32)

    def gain(shape):
        return 1.0 + nrm(shape, 0.05)

    n_pages = PAST_LEN // PAGE_SIZE
    used = DEC_BATCH * n_pages
    n_pool = used + max(1, used // 4)
    D = D_MODEL
    x_prompt = nrm((BATCH, SEQ, D))
    x_sample = nrm((DEC_BATCH, DEC_SEQ, D))
    cache_fox_k = nrm((N_EVEN, n_pool, PAGE_SIZE, N_HEADS, HEAD_DIM))
    cache_fox_v = nrm((N_EVEN, n_pool, PAGE_SIZE, N_HEADS, HEAD_DIM))
    cache_fox_logf = jax.nn.log_sigmoid(FORGET_BIAS + nrm((N_EVEN, n_pool, PAGE_SIZE, N_HEADS)))
    cache_sb_k = nrm((N_ODD, n_pool, PAGE_SIZE, N_HEADS, HEAD_DIM))
    cache_sb_v = nrm((N_ODD, n_pool, PAGE_SIZE, N_HEADS, HEAD_DIM))
    cache_mem_k = nrm((DEPTH, DEC_BATCH, N_MEM, X_HEADS, X_HEAD_DIM))
    cache_mem_v = nrm((DEPTH, DEC_BATCH, N_MEM, X_HEADS, X_HEAD_DIM))
    state_pool = nrm((N_EVEN, DEC_BATCH, POOL_BUF, MIX_HALF))
    state_conv = nrm((N_ODD, DEC_BATCH, CONV_BUF, MIX_HALF), 0.5)
    page_table = jax.random.permutation(keys[next(idx)], n_pool)[:used].reshape(DEC_BATCH, n_pages).astype(jnp.int32)
    mem_prompt = nrm((BATCH, N_MEM, D))
    return {
        'x_prompt': x_prompt, 'x_sample': x_sample,
        'cache_fox_k': cache_fox_k, 'cache_fox_v': cache_fox_v, 'cache_fox_logf': cache_fox_logf,
        'cache_sb_k': cache_sb_k, 'cache_sb_v': cache_sb_v,
        'cache_mem_k': cache_mem_k, 'cache_mem_v': cache_mem_v,
        'state_pool': state_pool, 'state_conv': state_conv,
        'page_table': page_table, 'mem_prompt': mem_prompt,
        'norm_mix': gain((DEPTH, D)), 'norm_cross': gain((DEPTH, D)), 'norm_ffn': gain((DEPTH, D)),
        'w_cq': nrm((DEPTH, D, X_WIDTH), D ** -0.5), 'w_ck': nrm((DEPTH, D, X_WIDTH), D ** -0.5),
        'w_cv': nrm((DEPTH, D, X_WIDTH), D ** -0.5), 'w_co': nrm((DEPTH, X_WIDTH, D), X_WIDTH ** -0.5),
        'g_cq': gain((DEPTH, X_HEAD_DIM)), 'g_ck': gain((DEPTH, X_HEAD_DIM)),
        'w_in_e': nrm((N_EVEN, D, IN_EVEN), D ** -0.5), 'b_f': FORGET_BIAS + nrm((N_EVEN, N_HEADS), 0.1),
        'w_pool_grp': nrm((N_EVEN, N_POOL_GROUPS, POOL_GROUP, POOL_GROUP), POOL_GROUP ** -0.5),
        'pool_scale': gain((N_EVEN, MIX_HALF)),
        'g_fq': gain((N_EVEN, HEAD_DIM)), 'g_fk': gain((N_EVEN, HEAD_DIM)),
        'w_out_e': nrm((N_EVEN, 2 * MIX_HALF, D), (2 * MIX_HALF) ** -0.5),
        'w_gate': nrm((N_EVEN, D, D_FF), D ** -0.5), 'w_up': nrm((N_EVEN, D, D_FF), D ** -0.5),
        'w_down': nrm((N_EVEN, D_FF, D), D_FF ** -0.5),
        'w_in_o': nrm((N_ODD, D, IN_ODD), D ** -0.5),
        'conv_w': nrm((N_ODD, CONV_WIDTH, MIX_HALF), CONV_WIDTH ** -0.5),
        'conv_b': nrm((N_ODD, MIX_HALF), 0.01),
        'ln_g': gain((N_ODD, MIX_HALF)), 'ln_b': nrm((N_ODD, MIX_HALF), 0.01),
        'w_out_o': nrm((N_ODD, 2 * MIX_HALF, D), (2 * MIX_HALF) ** -0.5),
        'w_router': nrm((N_ODD, D, N_EXPERTS), D ** -0.5), 'b_router': nrm((N_ODD, N_EXPERTS), 0.01),
        'we_gate': nrm((N_ODD, N_EXPERTS, D, D_FF_EXPERT), D ** -0.5),
        'we_up': nrm((N_ODD, N_EXPERTS, D, D_FF_EXPERT), D ** -0.5),
        'we_down': nrm((N_ODD, N_EXPERTS, D_FF_EXPERT, D), D_FF_EXPERT ** -0.5),
    }

def reference(x_prompt, x_sample, cache_fox_k, cache_fox_v, cache_fox_logf, cache_sb_k, cache_sb_v,
              cache_mem_k, cache_mem_v, state_pool, state_conv, page_table, mem_prompt,
              norm_mix, norm_cross, norm_ffn, w_cq, w_ck, w_cv, w_co, g_cq, g_ck,
              w_in_e, b_f, w_pool_grp, pool_scale, g_fq, g_fk, w_out_e, w_gate, w_up, w_down,
              w_in_o, conv_w, conv_b, ln_g, ln_b, w_out_o, w_router, b_router, we_gate, we_up, we_down):
    W = dict(norm_mix=norm_mix, norm_cross=norm_cross, norm_ffn=norm_ffn, w_cq=w_cq, w_co=w_co,
             g_cq=g_cq, w_in_e=w_in_e, b_f=b_f, w_pool_grp=w_pool_grp, pool_scale=pool_scale,
             g_fq=g_fq, g_fk=g_fk, w_out_e=w_out_e, w_gate=w_gate, w_up=w_up, w_down=w_down,
             w_in_o=w_in_o, conv_w=conv_w, conv_b=conv_b, ln_g=ln_g, ln_b=ln_b, w_out_o=w_out_o,
             w_router=w_router, b_router=b_router, we_gate=we_gate, we_up=we_up, we_down=we_down)

    B = x_prompt.shape[0]
    dt = x_prompt.dtype
    empty_kv = jnp.zeros((B, 0, N_HEADS, HEAD_DIM), dt)
    empty_lf = jnp.zeros((B, 0, N_HEADS), dt)
    mem_kv_p = [mem_keys_values(mem_prompt, w_ck[l], w_cv[l], g_ck[l]) for l in range(DEPTH)]
    fox_past_p = [(empty_kv, empty_kv, empty_lf) for _ in range(N_EVEN)]
    sb_past_p = [(empty_kv, empty_kv) for _ in range(N_ODD)]
    pool_prefix_p = [jnp.zeros((B, POOL_BUF, MIX_HALF), dt) for _ in range(N_EVEN)]
    conv_prefix_p = [jnp.zeros((B, CONV_BUF, MIX_HALF), dt) for _ in range(N_ODD)]
    y_prompt, sp = decoder_stack(x_prompt, mem_kv_p, fox_past_p, sb_past_p, pool_prefix_p, conv_prefix_p, W)

    mem_kv_s = [(cache_mem_k[l], cache_mem_v[l]) for l in range(DEPTH)]
    fox_past_s = [(gather_pages(cache_fox_k[i], page_table), gather_pages(cache_fox_v[i], page_table),
                   gather_pages(cache_fox_logf[i], page_table)) for i in range(N_EVEN)]
    sb_past_s = [(gather_pages(cache_sb_k[i], page_table), gather_pages(cache_sb_v[i], page_table))
                 for i in range(N_ODD)]
    pool_prefix_s = [state_pool[i] for i in range(N_EVEN)]
    conv_prefix_s = [state_conv[i] for i in range(N_ODD)]
    y_sample, ss = decoder_stack(x_sample, mem_kv_s, fox_past_s, sb_past_s, pool_prefix_s, conv_prefix_s, W)

    return (y_prompt, y_sample,
            jnp.stack(sp['fox_k']), jnp.stack(sp['fox_v']), jnp.stack(sp['fox_logf']),
            jnp.stack(sp['sb_k']), jnp.stack(sp['sb_v']),
            jnp.stack(sp['pool']), jnp.stack(sp['conv']),
            jnp.stack([kv[0] for kv in mem_kv_p]), jnp.stack([kv[1] for kv in mem_kv_p]),
            jnp.stack(ss['fox_k']), jnp.stack(ss['fox_v']), jnp.stack(ss['fox_logf']),
            jnp.stack(ss['sb_k']), jnp.stack(ss['sb_v']),
            jnp.stack(ss['pool']), jnp.stack(ss['conv']))


_drawn_inputs = setup_inputs


def setup_inputs(seed=0):
    import zlib

    import numpy as np

    out = dict(_drawn_inputs(seed))
    spreads = {}
    factors = {'g_cq': 4.062, 'g_fq': 3.007, 'ln_b': 8.0, 'conv_b': 3.138, 'b_router': 4.037}
    for name, (base, spread) in spreads.items():
        noise = np.random.default_rng([zlib.crc32(name.encode()), seed]).standard_normal(out[name].shape)
        drawn = base * np.exp(spread * noise) if base else spread * noise
        out[name] = jnp.asarray(drawn.astype(out[name].dtype))
    for name, factor in factors.items():
        out[name] = (out[name] * factor).astype(out[name].dtype)
    return out
```

```python
from contextlib import ExitStack

import concourse.bass as bass
from concourse import mybir
import numpy as np

F32 = mybir.dt.float32
I32 = mybir.dt.int32
U32 = mybir.dt.uint32
F32R = mybir.dt.float32r
ALU = mybir.AluOpType
ACT = mybir.ActivationFunctionType
AX = mybir.AxisListType.X

P = 128
D = 1024
KD = D // P
SEQ = 256
NB, NS = 8, 8
PAST = 256
NPG = 2
HALF = 512
NH, HD = 8, 64
NCH = HALF // P
XH, XHD = 4, 128
NMEM = 256
DFF = 2816
NE = 8
DFE = 3584
EPS = 1e-6
WINDOWS = (2, 4, 8, 16)
PBUF = 15
CW = 31
CBUF = 30
NSAMP = NB * NS
T = SEQ + NSAMP
TILES = 3
ROWS = (P, P, NSAMP)
RING = 3
SLOT = 4096
XSLOTS = 7
FB = 512
STAGES = DFE // FB
PRODUCTS = [(0, 0), (1, 0)] + [b for j in range(1, STAGES) for b in ((0, j), (1, j), (2, j - 1))] + [(2, STAGES - 1)]
PIECES = [(m, j, q) for m, j in PRODUCTS for q in range(2)]
NPIECE = len(PIECES)
PIECE = SLOT // 2
PRING = 7
CAP = P
ROUNDS = -(-T // CAP)
NEG = -1e30
PSEG = PBUF + SEQ
SSEG = PBUF + NS
PFLAT = PSEG + NB * SSEG
CSEG = CBUF + SEQ
DSEG = CBUF + NS
CFLAT = CSEG + NB * DSEG


def constants():
    i, j = np.arange(P)[:, None], np.arange(P)[None, :]
    rb, rs = (np.arange(P) // 64)[:, None], (np.arange(P) % NS)[:, None]
    nb, ns = (np.arange(NSAMP) // NS), (np.arange(NSAMP) % NS)
    upto = (i <= j).astype(np.float32)
    one = np.ones((P, P), np.float32)
    own = [(nb[None, :] == 2 * g + rb) for g in range(4)]
    pad = lambda a: np.concatenate([a, np.zeros((P - a.shape[0], a.shape[1]), a.dtype)])
    parts = {
        "ident": np.eye(P, dtype=np.float32),
        "minus_half": np.full((P, 1), -0.5, np.float32),
        "upto": upto,
        "before": (i < j).astype(np.float32),
        "neg_upto": np.concatenate([-upto, -one], 1),
        "ones": one,
        "after": (i > j).astype(np.float32),
        "zeros": 0 * one,
        "causal": np.where(j <= i, 0, NEG).astype(np.float32),
        "new_upto": pad(-((nb[:, None] == nb[None, :]) & (ns[:, None] <= ns[None, :])).astype(np.float32)),
        "own_upto": pad(np.concatenate([((nb[:, None] == 2 * g + b) & (ns[:, None] <= np.arange(NS)[None, :]))
                                        for g in range(4) for b in range(2)], 1).astype(np.float32)),
        "own": pad(np.concatenate([(nb[:, None] == 2 * g + b) for g in range(4) for b in range(2)], 1)
                   .astype(np.float32)),
        "strict": (j < i).astype(np.float32),
        "new_causal": np.concatenate([np.where(o & (ns[None, :] <= rs), 0, NEG) for o in own], 1)
                        .astype(np.float32),
        "new_strict": np.concatenate([(o & (ns[None, :] < rs)) for o in own], 1).astype(np.float32),
        "inv_count": np.tile(np.concatenate([1.0 / np.minimum(np.arange(16) + 1, w) for w in WINDOWS])
                             .astype(np.float32), (P, 1)),
        "iota": np.tile(np.arange(P, dtype=np.float32), (P, 1)),
    }
    at, n = {}, 0
    for name, a in parts.items():
        at[name] = (n, a.shape[1])
        n += a.shape[1]
    return np.concatenate(list(parts.values()), 1).astype(np.float32), at


class Marks:

    def __init__(self, nc, ctx, known):
        self.nc, self.ctx, self.known = nc, ctx, known
        self.sems, self.table, self.count = {}, {}, {}

    def sem(self, name):
        if name not in self.sems:
            self.sems[name] = self.ctx.enter_context(self.nc.semaphore("m_" + name))
        return self.sems[name]

    def sets(self, name, *index, by=1):
        self.count[name] = self.count.get(name, 0) + by
        self.table[(name, *index)] = self.count[name]
        return self.sem(name), by

    def at(self, name, *index):
        return self.sem(name), self.known.get((name, *index), 1)

    def has(self, name, *index):
        return (name, *index) in self.known


class Banks:

    def __init__(self, known):
        self.known, self.table, self.n = known, {}, 0

    def open(self, *key):
        b, use = self.n % 8, self.n // 8
        self.n += 1
        self.table[key] = (b, use + 1)
        return b, use

    def of(self, *key):
        return self.known.get(key, (0, 1))

    def uses(self, b):
        return (self.n - b + 7) // 8


def units():
    out = []
    for l in range(2):
        out += [("mk", l, t) for t in range(2)]
        out += [(k, l, t) for k in ("q", "k") for t in range(TILES)]
        out += [("cq", l, t) for t in range(TILES)]
    return out


UNITS = units()
UNIT = {u: n for n, u in enumerate(UNITS)}


def decoder_step(nc, a, o, known):
    ctx = ExitStack()
    with ctx:
        marks = Marks(nc, ctx, known.get("marks", {}))
        banks = Banks(known.get("banks", {}))
        releases = known.get("releases", {})
        released = {}
        sets, at = marks.sets, marks.at

        at_byte, width = {}, {}

        def sb(name, cols, dt=F32):
            at_byte[name], width[name] = -(-nc.sbuf_base // 32) * 32, cols
            return ctx.enter_context(nc.sbuf_tensor(name, [P, cols], dt))

        def rounded(name):
            return nc.alloc_sbuf_tensor_at(name + "_r", [P, width[name]], F32R, offset=at_byte[name])

        def sem(name):
            return ctx.enter_context(nc.semaphore(name))

        small_ring = sb("small_ring", RING * SLOT)
        big = sb("big", (XSLOTS - RING) * SLOT)
        slots = [small_ring[:, s * SLOT:(s + 1) * SLOT] for s in range(RING)]
        slots += [big[:, s * SLOT:(s + 1) * SLOT] for s in range(XSLOTS - RING)]
        kT = big[:, 0:4096].rearrange("p (c b k) -> p c b k", c=NCH, b=4)
        vC = big[:, 4096:8192].rearrange("p (b g c) -> p b g c", b=4, g=NPG)
        qbd = big[:, 8192:12288]
        knat = big[:, 12288:14336].rearrange("p (s c) -> p s c", s=4)
        lb = big[:, 14336:16384].rearrange("p (b g c) -> p b g c", b=NB, g=NPG)

        x = sb("x", TILES * D)[:, :].rearrange("p (t d) -> p t d", t=TILES)
        hbuf = sb("h", TILES * D)
        h = hbuf[:, :].rearrange("p (t d) -> p t d", t=TILES)
        yT = hbuf[:, 0:8 * T].rearrange("p (c t) -> p c t", c=8)
        mem = hbuf[:, 0:2 * D].rearrange("p (t d) -> p t d", t=2)
        hTbuf = sb("hT", KD * T)
        hT = hTbuf[:, :].rearrange("p (c t) -> p c t", c=KD)
        lr = hTbuf[:, 0:2048].rearrange("p (t h c) -> p t h c", t=2, h=NH)
        poolF = big[:, 0:NCH * PFLAT].rearrange("p (c t) -> p c t", c=NCH)
        pool_new = big[:, NCH * PFLAT:NCH * (PFLAT + NSAMP)].rearrange("p (c t) -> p c t", c=NCH)
        conv_at = 4096
        conv = big[:, conv_at:conv_at + NCH * T].rearrange("p (c t) -> p c t", c=NCH)
        convF = big[:, conv_at + NCH * T:conv_at + NCH * (T + CFLAT)].rearrange("p (c t) -> p c t", c=NCH)
        conv_new = big[:, conv_at + NCH * (T + CFLAT):conv_at + NCH * (T + CFLAT + NSAMP)] \
            .rearrange("p (c t) -> p c t", c=NCH)
        taps = hbuf[:, 0:NSAMP * CW]
        squares = big[:, conv_at + NCH * T:conv_at + 2 * NCH * T].rearrange("p (c t) -> p c t", c=NCH)
        qz_t = sb("qz", NCH * 2 * SEQ)
        qz = qz_t[:, :].rearrange("p (c z t) -> p c z t", c=NCH, z=2)
        kN_t = sb("kN", NCH * T)
        kN = kN_t[:, :].rearrange("p (c t) -> p c t", c=NCH)
        v_t = sb("v", TILES * HALF)
        v = v_t[:, :].rearrange("p (t c) -> p t c", t=TILES)
        kM_t = sb("kM", XH * NMEM)
        kM = kM_t[:, :].rearrange("p (c t) -> p c t", c=XH)
        vM_t = sb("vM", 2 * HALF)
        vM = vM_t[:, :].rearrange("p (t c) -> p t c", t=2)
        S_t = sb("S", 640)
        L_t = sb("L", 640)
        Pr_t = sb("Pr", 1024)
        PT_t = sb("PT", 1024)
        stick_S = [hTbuf[:, 384 * i:384 * i + 384] for i in range(4)]
        stick_L = [big[:, 14336 + 384 * i:14336 + 384 * i + 384] for i in range(4)]
        stick_P = [Pr_t[:, 0:384], Pr_t[:, 512:896], hTbuf[:, 1536:1920], hTbuf[:, 1920:2304]]
        S = [S_t[:, 0:320], S_t[:, 320:640]]
        L = [L_t[:, 0:320], L_t[:, 320:640]]
        Pr = [Pr_t[:, 0:512], Pr_t[:, 512:1024]]
        PT = [PT_t[:, 0:512], PT_t[:, 512:1024]]
        nbuf = [S_t[:, 0:512], L_t[:, 0:512]]
        gain = sb("gain", D)
        ctab, cat = constants()
        cbuf = sb("consts", ctab.shape[1])

        def C(name, lo=0, n=None):
            s, w = cat[name]
            return cbuf[:, s + lo:s + lo + (w - lo if n is None else n)]

        ident = C("ident")
        hg = sb("hg", 2 * (2 * HD + 2 * XHD))
        g_fq, g_fk = hg[:, 0:64], hg[:, 64:128]
        g_cq = [hg[:, 128:256], hg[:, 256:384]]
        hg2 = sb("hg2", XHD)
        g_ck = [hg[:, 384:512], hg2[:, :]]
        bf8 = sb("bf8", 2 * NH)
        b_f, b_r = bf8[:, 0:8], bf8[:, 8:16]
        wfl = sb("wfl", KD * NH)[:, :].rearrange("p (k n) -> p k n", k=KD)
        wrt = sb("wrt", KD * NE)[:, :].rearrange("p (k n) -> p k n", k=KD)
        wpg = sb("wpg", NCH * P)[:, :].rearrange("p (g n) -> p g n", g=NCH)
        chan_t = sb("chan", (4 + CW) * NCH)
        chan = chan_t[:, :].rearrange("p (c n) -> p n c", c=NCH)
        cw = chan[:, 4:4 + CW, :]
        pt = sb("pt", 16, I32)
        lf = sb("lf", 6 * 8)
        lf_y = lf[:, 0:24].rearrange("p (t h) -> p t h", t=3)
        logf = lf[:, 24:48].rearrange("p (t h) -> p t h", t=3)
        lfw = sb("lfw", 3 * 24)
        lf_a, lf_e, lf_l = (lfw[:, 24 * i:24 * i + 24].rearrange("p (t h) -> p t h", t=3) for i in range(3))
        lfp = sb("lfp", 16 * 8)[:, :].rearrange("p (b g h) -> p b g h", b=NB, g=NPG)
        Fq = sb("Fq", 16)[:, :].rearrange("p (t h) -> p t h", t=2)
        ln1_t = gain[:, 0:512]
        ln2_t = gain[:, 512:1024]
        route = sb("route", 9 * 24 + 24)
        lg, m8, pk1, pk2, picked, gates, posr = (route[:, 24 * i:24 * i + 24].rearrange("p (t e) -> p t e", t=3)
                                                 for i in range(7))
        idx = sb("idx", 24, U32)[:, :].rearrange("p (t e) -> p t e", t=3)
        idxf = route[:, 168:192].rearrange("p (t e) -> p t e", t=3)
        gw = route[:, 192:216].rearrange("p (t e) -> p t e", t=3)
        rcol = route[:, 216:222]
        cmax = route[:, 222:223]
        cmax_i = sb("cmax_i", 1, I32)
        ffn_s, ffn_hid = S, L
        ring_r, big_r, PT_r = rounded("small_ring"), rounded("big"), rounded("PT")
        moe_x = [t[:, 0:1024].rearrange("p (k c) -> p k c", k=KD) for t in (rounded("hT"), rounded("kM"))]
        moe_P = hTbuf[:, 1024:1408].rearrange("p (t c) -> p t c", t=3)
        moe_G = hTbuf[:, 1408:1792].rearrange("p (t c) -> p t c", t=3)
        moe_GT = hTbuf[:, 1792:2176]
        moe_y = qz_t[:, 0:1024]
        moe_hid = [qz_t[:, 1024:1536], qz_t[:, 1536:2048]]
        moe_sg = Pr
        moe_hidT = [PT_r[:, 0:512], PT_r[:, 512:1024]]

        def pieces_of(small, large):
            return [(small if s < RING else large)[:, (s % RING if s < RING else s - RING) * SLOT + q * PIECE:][:, 0:PIECE]
                    for s in (1, 2, 3, 4, 5, 6, 0) for q in range(2)]

        raw = pieces_of(small_ring, big)[:PRING]
        low = pieces_of(ring_r, big_r)[:PRING]
        high = pieces_of(ring_r, big_r)[PRING:]
        nst = sb("nst", 4 * TILES)
        n_ss, n_ms, n_rs = (nst[:, TILES * i:TILES * i + TILES] for i in range(3))
        lnst = sb("lnst", 2 * TILES)
        ln_var, ln_rs = lnst[:, 0:TILES], lnst[:, TILES:2 * TILES]
        ust = sb("ust", 2 * 24)
        u_ss = [ust[:, 24 * i:24 * i + 8] for i in range(2)]
        u_ms = [ust[:, 24 * i + 8:24 * i + 16] for i in range(2)]
        u_rs = [ust[:, 24 * i + 16:24 * i + 24] for i in range(2)]
        ast = sb("ast", 4 * 6)
        a_nm = [ast[:, 6 * i:6 * i + 2] for i in range(4)]
        a_sm = [ast[:, 6 * i + 2:6 * i + 4] for i in range(4)]
        a_rc = [ast[:, 6 * i + 4:6 * i + 6] for i in range(4)]

        bank = [ctx.enter_context(nc.psum_tensor(f"bank{b}", [P, 512], F32)) for b in range(8)]
        full = [sem(f"bank{b}_full") for b in range(8)]
        free = [sem(f"bank{b}_free") for b in range(8)]
        raw_full = [sem(f"raw{s}_full") for s in range(PRING)]
        moe_hi, moe_lo, moe_used, moe_xhi, moe_hThi = (sem("moe_" + n) for n in (
            "weights_hi", "weights_lo", "weights_used", "tokens_hi", "hiddenT_hi"))
        slot_full = [sem(f"slot{s}_full") for s in range(XSLOTS)]
        knat_full = [sem(f"knat{s}_full") for s in range(4)]
        ffn_gate, ffn_up, ffn_silu, ffn_h, ffn_down = (sem("ffn_" + n) for n in ("gate", "up", "silu", "h", "down"))
        (moe_sel, moe_gathered, moe_xT, moe_silu, moe_h, moe_tr, moe_hT, moe_yc,
         moe_scattered, moe_added, moe_GTr, moe_GTc, moe_zero, moe_scatteredE, moe_addedE) = (
            sem("moe_" + n) for n in (
                "selection", "gathered", "tokensT", "silu", "hidden", "transposed", "hiddenT", "output",
                "scattered", "added", "gatesT_psum", "gatesT", "zeroed", "scattered_last",
                "added_last"))
        moe_col, moe_cleared, moe_shift = sem("moe_columns"), sem("moe_cleared"), sem("moe_shifted")
        conv_p, conv_s = sem("conv_prompt_tap"), sem("conv_sample_sum")

        def used(n, m, j):
            return moe_used, n * NPIECE + (2 * PRODUCTS.index((m, j)) + 2)

        def taken(*key):
            b, use = banks.of(*key)
            return free[b], use

        def view(ap, offset, dims):
            return bass.AP(ap.tensor, ap.offset + offset, [list(ap.ap[0])] + dims)

        def spread(src):
            return bass.AP(src.tensor, src.offset, [[0, P]] + [list(d) for d in src.ap])

        def w_stream():
            for l in range(2):
                yield ("ck", l), a["w_ck"][l].rearrange("(k p) n -> p k n", p=P)
                yield ("cv", l), a["w_cv"][l].rearrange("(k p) n -> p k n", p=P)
                w = a["w_in_e" if l == 0 else "w_in_o"][0].rearrange("(k p) n -> p k n", p=P)
                for n, name in ((1, "q"), (2, "k"), (3, "v"), (0, "p")) if l == 0 else \
                        ((0, "a"), (1, "g"), (2, "q"), (3, "k"), (4, "v")):
                    yield (name, l), w[:, :, n * HALF:(n + 1) * HALF]
                w = a["w_out_e" if l == 0 else "w_out_o"][0].rearrange("(k p) n -> p k n", p=P)
                for hf in range(2):
                    yield ("wo", l, hf), w[:, :, hf * HALF:(hf + 1) * HALF]
                yield ("cq", l), a["w_cq"][l].rearrange("(k p) n -> p k n", p=P)
                yield ("co", l), a["w_co"][l].rearrange("(k p) n -> p k n", p=P)

        stream = list(w_stream())
        place = {key: (n % RING, n // RING) for n, (key, _) in enumerate(stream)}
        FBLK = DFF // 256
        n0 = next(n for n, (key, _) in enumerate(stream) if key[1] == 1)
        extra = [2 * (FBLK // 2 + 1), 2 * (FBLK // 2), 0]

        def uses_before(s, n):
            return len([m for m in range(n) if m % RING == s])

        def slot_of(key):
            s, use = place[key]
            n = next(m for m, (k, _) in enumerate(stream) if k == key)
            return s, use + 1 + (extra[s] if n >= n0 else 0)


        ZSEQ = [[(k, t) for k in ("q", "k", "v") for t in range(TILES)]] * 2
        block = ctx.enter_context(nc.Block())

        @block.tensor
        def _(pe):
            mm = nc.tensor.matmul
            tr = nc.tensor.transpose

            def open_bank(*key):
                b, use = banks.open(*key)
                if use:
                    pe.wait_ge(free[b], use)
                return b

            def slot(key):
                s, n = slot_of(key)
                pe.wait_ge(slot_full[s], 16 * n)
                return slots[s]

            def release(key, *last):
                released[key] = last

            def to_channel_major(j, src_ready, src, dst_tiles):
                for t in dst_tiles:
                    pe.wait_ge(*at(*src_ready(t)))
                    for kh in range(2):
                        b = open_bank("tc", j, t, kh)
                        for k in range(4):
                            ins = tr(bank[b][:, k * P:k * P + ROWS[t]],
                                     src[0:ROWS[t], t, (4 * kh + k) * P:(4 * kh + k + 1) * P],
                                     ident[0:ROWS[t], 0:ROWS[t]])
                        ins.then_inc(full[b], 1)

            def token_product(key, xT, w, nk, t, cols=HALF, col0=0):
                b = open_bank(*key)
                t0 = t * P
                for k in range(nk):
                    ins = mm(bank[b][0:ROWS[t], 0:cols], xT[:, k, t0:t0 + ROWS[t]], w[:, k, col0:col0 + cols],
                             start=k == 0, stop=k == nk - 1)
                ins.then_inc(full[b], 1)

            def unit_transpose(u):
                rows = ROWS[UNITS[u][2]]
                pe.wait_ge(*at("unit", u))
                b = open_bank("ut", u)
                for c in range(4):
                    ins = tr(bank[b][:, c * P:c * P + rows], nbuf[u % 2][0:rows, c * P:(c + 1) * P],
                             ident[0:rows, 0:rows])
                ins.then_inc(full[b], 1)

            def wait_hT(j):
                for t in range(TILES):
                    for kh in range(2):
                        pe.wait_ge(*taken("tc", j, t, kh))

            def memory_keys_values(l):
                to_channel_major(("mem", l), lambda t: ("mem_in", l), mem, range(2))
                for t in range(2):
                    for kh in range(2):
                        pe.wait_ge(*taken("tc", ("mem", l), t, kh))
                w = slot(("ck", l)).rearrange("p (k n) -> p k n", k=KD)
                for t in range(2):
                    token_product(("z", "mk", l, t), hT, w, KD, t)
                release(("ck", l), "z", "mk", l, 1)
                w = slot(("cv", l)).rearrange("p (k n) -> p k n", k=KD)
                for t in range(2):
                    token_product(("z", "mv", l, t), hT, w, KD, t)
                    unit_transpose(UNIT["mk", l, t])
                release(("cv", l), "z", "mv", l, 1)

            def cache_transpose(stage, hf, j):
                n = (stage * 2 + hf) * 8 + j
                pe.wait_ge(knat_full[j % 4], 16 * (n // 4 + 1))
                b = open_bank("kt", stage, hf, j)
                for c in range(4):
                    ins = tr(bank[b][:, c * P:(c + 1) * P], knat[:, j % 4, c * P:(c + 1) * P], ident)
                ins.then_inc(full[b], 1)

            def stick_scores(hd):
                c = hd // 2
                b = open_bank("s", 1, hd)
                for qt in range(2):
                    ins = mm(bank[b][:, qt * P:(2 * qt + 1) * P], qz[:, c, hd % 2, qt * P:(qt + 1) * P],
                             kN[:, c, 0:(qt + 1) * P], start=True, stop=True)
                ins.then_inc(full[b], 1)

            def layernorm_sums():
                pe.wait_ge(*at("conv"))
                b = open_bank("lmean")
                for c in range(NCH):
                    ins = mm(bank[b][:, 0:T], C("ones"), conv[:, c, :], start=c == 0, stop=c == NCH - 1)
                ins.then_inc(full[b], 1)
                pe.wait_ge(*at("cent_sq"))
                b = open_bank("lvar")
                for t in range(TILES):
                    for c in range(NCH):
                        ins = mm(bank[b][0:ROWS[t], t:t + 1], squares[:, c, t * P:t * P + ROWS[t]], C("ones", 0, 1),
                                 start=c == 0, stop=c == NCH - 1)
                ins.then_inc(full[b], 1)

            def layernorm_spread():
                pe.wait_ge(*at("ln_diag"))
                b = open_bank("lrs")
                for t in range(TILES):
                    ins = mm(bank[b][:, t * P:t * P + ROWS[t]], C("ones")[0:ROWS[t]],
                             S_t[0:ROWS[t], t * P:t * P + ROWS[t]], start=True, stop=True)
                ins.then_inc(full[b], 1)

            def prompt_scores(l, hd):
                c = hd // 2
                for qt in range(2):
                    nk = (qt + 1) * P
                    b = open_bank("s", l, hd, qt)
                    out = bank[b][:, 0:nk]
                    ins = mm(out, qz[:, c, hd % 2, qt * P:(qt + 1) * P], kN[:, c, 0:nk],
                             start=True, stop=l == 1)
                    if l == 0:
                        ins = mm(out, lr[:, 0, hd, :], C("neg_upto", 0, nk), start=False, stop=qt == 0)
                        if qt == 1:
                            ins = mm(out[:, P:2 * P], lr[:, 1, hd, :], C("neg_upto", 0, P),
                                     start=False, stop=True)
                    ins.then_inc(full[b], 1)

            def prompt_values(l, hd):
                probs = Pr[hd % 2] if l == 0 else stick_P[hd % 4]
                for qt in range(2):
                    pe.wait_ge(*(at("probs", 0, "p", hd, qt) if l == 0 else at("probs", 1, "p", hd)))
                    if qt == 0:
                        b = open_bank("pt", l, hd)
                    for kt in range(qt + 1):
                        ins = tr(bank[b][:, (qt + kt) * P:(qt + kt + 1) * P],
                                 probs[:, (qt + kt) * P:(qt + kt + 1) * P], ident)
                ins.then_inc(full[b], 1)
                pe.wait_ge(*taken("pt", l, hd))
                c = hd // 2
                if hd % 2 == 0:
                    prompt_values.b = open_bank("o", l, c)
                out = bank[prompt_values.b][:, (hd % 2) * SEQ:(hd % 2 + 1) * SEQ]
                mm(out, v[:, 0, c * P:(c + 1) * P], PT[hd % 2][:, 0:SEQ], start=True, stop=False)
                ins = mm(out[:, P:SEQ], v[:, 1, c * P:(c + 1) * P], PT[hd % 2][:, SEQ:SEQ + P],
                         start=False, stop=True)
                if hd % 2 == 1:
                    ins.then_inc(full[prompt_values.b], 1)

            def sample_scores(l, g):
                b = open_bank("ss", l, g)
                q = qbd.rearrange("p (g b c r) -> p g b c r", g=4, b=2, c=NCH)
                old, new = bank[b][:, 0:PAST], bank[b][:, PAST:PAST + NSAMP]
                for b2 in range(2):
                    for c in range(NCH):
                        mm(old, q[:, g, b2, c, :], kT[:, c, 2 * (g % 2) + b2, :],
                           start=(b2, c) == (0, 0), stop=l == 1 and (b2, c) == (1, 3))
                if l == 0:
                    for b2 in range(2):
                        for pg in range(NPG):
                            mm(old, lb[:, 2 * g + b2, pg, :], C("after" if pg == 0 else "ones", 0, 2 * P),
                               start=False, stop=False)
                    mm(old, ln1_t[0:NSAMP, g * P:(g + 1) * P], view(C("ones")[0:NSAMP], 0, [[0, 2], [1, P]]),
                       start=False, stop=True)
                for b2 in range(2):
                    for c in range(NCH):
                        ins = mm(new, q[:, g, b2, c, :], kN[:, c, SEQ:T],
                                 start=(b2, c) == (0, 0), stop=l == 1 and (b2, c) == (1, 3))
                if l == 0:
                    mm(new, ln1_t[0:NSAMP, g * P:(g + 1) * P], C("ones", 0, NSAMP)[0:NSAMP],
                       start=False, stop=False)
                    ins = mm(new, ln2_t[0:NSAMP, g * P:(g + 1) * P], C("new_upto")[0:NSAMP],
                             start=False, stop=True)
                ins.then_inc(full[b], 1)

            def sample_values(l, g):
                pe.wait_ge(*at("probs", l, "s", g))
                b = open_bank("pts", l, g)
                for kt in range(2):
                    tr(bank[b][:, kt * P:(kt + 1) * P], Pr[g % 2][:, kt * P:(kt + 1) * P], ident)
                ins = tr(bank[b][0:NSAMP, 2 * P:3 * P], Pr[g % 2][:, 2 * P:2 * P + NSAMP], ident)
                ins.then_inc(full[b], 1)
                pe.wait_ge(*taken("pts", l, g))
                pe.wait_ge(*at("v_in", 2 * l, g // 2))
                b = open_bank("os", l, g)
                for c in range(NCH):
                    for b2 in range(2):
                        out = bank[b][:, (2 * c + b2) * 16:(2 * c + b2 + 1) * 16]
                        r0 = b2 * 64 + c * 16
                        for pg in range(NPG):
                            mm(out, vC[:, 2 * (g % 2) + b2, pg, c * P:(c + 1) * P],
                               PT[g % 2][:, pg * P + r0:pg * P + r0 + 16], start=pg == 0, stop=False)
                        ins = mm(out, v[0:NSAMP, 2, c * P:(c + 1) * P],
                                 PT[g % 2][0:NSAMP, 2 * P + r0:2 * P + r0 + 16], start=False, stop=True)
                ins.then_inc(full[b], 1)

            def self_attention(l):
                stage = 2 * l
                for t in range(TILES):
                    for k in ("q", "k"):
                        pe.wait_ge(*taken("ut", UNIT[k, l, t]))
                    pe.wait_ge(*taken("z", "v", l, t))
                if l == 0:
                    pe.wait_ge(*at("lr", 0))
                if l == 0:
                    prompt_scores(l, 0)
                else:
                    for hd in range(4):
                        stick_scores(hd)
                    layernorm_sums()
                for hd in range(NH):
                    if l == 0 and hd + 1 < NH:
                        prompt_scores(l, hd + 1)
                    if l == 1 and hd % 2 == 0 and hd + 4 < NH:
                        stick_scores(hd + 4)
                        stick_scores(hd + 5)
                    cache_transpose(stage, 0, hd)
                    prompt_values(l, hd)
                    if l == 1 and hd == 1:
                        layernorm_spread()
                for hf in range(2):
                    if hf:
                        for j in range(8):
                            cache_transpose(stage, 1, j)
                    for j in range(8):
                        pe.wait_ge(*taken("kt", stage, hf, j))
                    if l == 0 and hf == 0:
                        pe.wait_ge(*at("lb", 0))
                    for g in (2 * hf, 2 * hf + 1):
                        sample_scores(l, g)
                    for g in (2 * hf, 2 * hf + 1):
                        sample_values(l, g)

            def out_projection(l):
                for c in range(NCH):
                    pe.wait_ge(*taken("os", l, c))
                    pe.wait_ge(*taken("o", l, c))
                    pe.wait_ge(*(taken("pm", c) if l == 0 else at("y_mix", c)))
                for hf in range(2):
                    w = slot(("wo", l, hf)).rearrange("p (k n) -> p k n", k=KD)
                    for t in range(TILES):
                        token_product(("wo", l, hf, t), yT, w, KD, t)
                    release(("wo", l, hf), "wo", l, hf, 2)

            def cross_attention(l):
                stage = 2 * l + 1
                w = slot(("cq", l)).rearrange("p (k n) -> p k n", k=KD)
                wait_hT(3 * l + 1)
                for t in range(TILES):
                    token_product(("z", "cq", l, t), hT, w, KD, t)
                    if t:
                        unit_transpose(UNIT["cq", l, t - 1])
                release(("cq", l), "z", "cq", l, 2)
                unit_transpose(UNIT["cq", l, 2])
                for t in range(TILES):
                    pe.wait_ge(*taken("ut", UNIT["cq", l, t]))
                for t in range(2):
                    pe.wait_ge(*taken("ut", UNIT["mk", l, t]))
                    pe.wait_ge(*taken("z", "mv", l, t))

                def scores(hd):
                    b = open_bank("cs", l, hd)
                    for qt in range(2):
                        ins = mm(bank[b][:, qt * NMEM:(qt + 1) * NMEM], kN[:, hd, qt * P:(qt + 1) * P],
                                 kM[:, hd, :], start=True, stop=True)
                    ins.then_inc(full[b], 1)

                def values(hd):
                    pe.wait_ge(*at("probs", l, "cp", hd))
                    b = open_bank("cpt", l, hd)
                    for kt in range(2):
                        for qt in range(2):
                            ins = tr(bank[b][:, (2 * kt + qt) * P:(2 * kt + qt + 1) * P],
                                     Pr[hd % 2][:, qt * NMEM + kt * P:qt * NMEM + (kt + 1) * P], ident)
                    ins.then_inc(full[b], 1)
                    pe.wait_ge(*taken("cpt", l, hd))
                    b = open_bank("co", l, hd)
                    for kt in range(2):
                        ins = mm(bank[b][:, 0:SEQ], vM[:, kt, hd * P:(hd + 1) * P],
                                 PT[hd % 2][:, kt * SEQ:(kt + 1) * SEQ], start=kt == 0, stop=kt == 1)
                    ins.then_inc(full[b], 1)

                scores(0)
                for hd in range(XH):
                    if hd + 1 < XH:
                        scores(hd + 1)
                    cache_transpose(stage, 0, 2 * hd)
                    cache_transpose(stage, 0, 2 * hd + 1)
                    values(hd)
                q = qbd.rearrange("p (g b h r) -> p g b h r", g=2, b=4, h=XH)
                for hf in range(2):
                    if hf:
                        for j in range(8):
                            cache_transpose(stage, 1, j)
                    for j in range(8):
                        pe.wait_ge(*taken("kt", stage, hf, j))
                    b = open_bank("css", l, hf)
                    for b4 in range(4):
                        for hd in range(XH):
                            ins = mm(bank[b][:, 0:NMEM], q[:, hf, b4, hd, :], kT[:, hd, b4, :],
                                     start=(b4, hd) == (0, 0), stop=(b4, hd) == (3, 3))
                    ins.then_inc(full[b], 1)
                    pe.wait_ge(*at("probs", l, "cs", hf))
                    b = open_bank("cpts", l, hf)
                    for kt in range(2):
                        ins = tr(bank[b][:, kt * P:(kt + 1) * P], Pr[hf][:, kt * P:(kt + 1) * P], ident)
                    ins.then_inc(full[b], 1)
                    pe.wait_ge(*taken("cpts", l, hf))
                    pe.wait_ge(*at("v_in", stage, hf))
                    b = open_bank("cos", l, hf)
                    for hd in range(XH):
                        for b4 in range(4):
                            out = bank[b][:, hd * 32 + b4 * 8:hd * 32 + b4 * 8 + 8]
                            for kt in range(2):
                                r0 = kt * P + b4 * 32 + hd * 8
                                ins = mm(out, vC[:, b4, kt, hd * P:(hd + 1) * P], PT[hf][:, r0:r0 + 8],
                                         start=kt == 0, stop=kt == 1)
                    ins.then_inc(full[b], 1)
                for hf in range(2):
                    pe.wait_ge(*taken("cos", l, hf))
                for hd in range(XH):
                    pe.wait_ge(*taken("co", l, hd))
                w = slot(("co", l)).rearrange("p (k n) -> p k n", k=4)
                for hf in range(2):
                    for t in range(TILES):
                        token_product(("wc", l, hf, t), yT, w, 4, t, col0=hf * HALF)
                release(("co", l), "wc", l, 1, 2)

            pe.wait_ge(*at("head_in"))
            memory_keys_values(0)
            pe.wait_ge(*at("const_in"))
            pe.wait_ge(*at("table_in"))
            b = open_bank("chan")
            for c in range(NCH):
                ins = tr(bank[b][:, c * (4 + CW):(c + 1) * (4 + CW)], PT[1][0:4 + CW, c * P:(c + 1) * P],
                         ident[0:4 + CW, 0:4 + CW])
            ins.then_inc(full[b], 1)
            to_channel_major(0, lambda t: ("h", 0, t), h, range(TILES))
            wait_hT(0)
            lag = 2
            for n, (k, t) in enumerate(ZSEQ[0]):
                if t == 0:
                    w = slot((k, 0)).rearrange("p (k n) -> p k n", k=KD)
                token_product(("z", k, 0, t), hT, w, KD, t)
                if t == 2:
                    release((k, 0), "z", k, 0, 2)
                if n >= lag and ZSEQ[0][n - lag][0] != "v":
                    unit_transpose(UNIT[ZSEQ[0][n - lag][0], 0, ZSEQ[0][n - lag][1]])
            b = open_bank("fl")
            for t in range(TILES):
                for k in range(KD):
                    ins = mm(bank[b][0:ROWS[t], 8 * t:8 * t + 8], hT[:, k, t * P:t * P + ROWS[t]], wfl[:, k, :],
                             start=k == 0, stop=k == KD - 1)
            ins.then_inc(full[b], 1)
            pe.wait_ge(*at("pre_in"))
            b = open_bank("pre")
            for g in range(NCH):
                ins = tr(bank[b][:, g * 120:(g + 1) * 120], PT[0][0:120, g * P:(g + 1) * P], ident[0:120, 0:120])
            ins.then_inc(full[b], 1)
            w = slot(("p", 0)).rearrange("p (k n) -> p k n", k=KD)
            for g in range(NCH):
                b = open_bank("p", g)
                for k in range(KD):
                    ins = mm(bank[b][:, 0:T], w[:, k, g * P:(g + 1) * P], hT[:, k, :],
                             start=k == 0, stop=k == KD - 1)
                ins.then_inc(full[b], 1)
            release(("p", 0), "p", NCH - 1)
            pe.wait_ge(*at("logf"))
            b = open_bank("Fq")
            mm(bank[b][:, 0:8], C("upto"), logf[:, 0, :], start=True, stop=True)
            mm(bank[b][:, 8:16], C("ones"), logf[:, 0, :], start=True, stop=False)
            mm(bank[b][:, 8:16], C("upto"), logf[:, 1, :], start=False, stop=True).then_inc(full[b], 1)
            pe.wait_ge(*taken("p", NCH - 1))
            for n, (src, rows) in enumerate((("p", P), ("s", NSAMP))):
                b = open_bank("pst", src)
                for g in range(NCH):
                    t_in = poolF[:, g, PBUF + P:PBUF + SEQ] if n == 0 else \
                        pool_new[:, g, :]
                    ins = tr(bank[b][0:rows, g * P:(g + 1) * P], t_in, ident)
                ins.then_inc(full[b], 1)
            for g in range(NCH):
                pe.wait_ge(*at("pool_d", g))
                b = open_bank("pm", g)
                mm(bank[b][:, 0:T], wpg[:, g, :], L_t[:, (g % 2) * T:(g % 2 + 1) * T],
                   start=True, stop=True).then_inc(full[b], 1)
            self_attention(0)
            out_projection(0)
            to_channel_major(1, lambda t: ("h", 1, t), h, range(TILES))
            cross_attention(0)
            to_channel_major(2, lambda t: ("h", 2, t), h, range(TILES))
            wait_hT(2)

            for b in range(8):
                pe.wait_ge(free[b], banks.uses(b))

            def gate_up(blk, f2, ff):
                w = slots[blk].rearrange("p (m k n) -> p m k n", m=2, k=KD)
                for m, (bk, read, done) in enumerate(((6, ffn_silu, ffn_gate), (7, ffn_h, ffn_up))):
                    pe.wait_ge(read, ff)
                    for k in range(KD):
                        ins = mm(bank[bk][:, 0:T], w[:, m, k, f2 * P:(f2 + 1) * P], hT[:, k, :],
                                 start=k == 0, stop=k == KD - 1)
                    ins.then_inc(done, 1)

            def down(blk, f2, ff, first=False, last=False):
                w = slots[3 + blk][:, 0:2 * D].rearrange("p (f n) -> p f n", f=2)
                pe.wait_ge(ffn_h, ff + 1)
                for hf in range(2):
                    for t in range(TILES):
                        ins = mm(bank[3 * hf + t][0:ROWS[t], :], ffn_hid[f2][:, t * P:t * P + ROWS[t]],
                                 w[:, f2, hf * HALF:(hf + 1) * HALF], start=first, stop=last)
                ins.then_inc(ffn_down, 1)

            def ffn_block(blk, i, gu_loads, down_loads, first=False):
                pe.wait_ge(slot_full[blk], gu_loads * 16)
                gate_up(blk, 0, i * 2)
                if not first:
                    down(1 - blk, 1, i * 2 - 1)
                gate_up(blk, 1, i * 2 + 1)
                pe.wait_ge(slot_full[3 + blk], down_loads * 16)
                down(blk, 0, i * 2, first=first)

            ub = [uses_before(s, n0) for s in range(2)]
            ffn_block(0, 0, ub[0] + 2, 1, first=True)
            with pe.Fori(0, FBLK // 2) as i:
                ffn_block(1, i * 2 + 1, i * 2 + (ub[1] + 2), i + 1)
                ffn_block(0, i * 2 + 2, i * 2 + (ub[0] + 4), i + 2)
            down(0, 1, DFF // P - 1, last=True)
            for hf in range(2):
                for t in range(TILES):
                    pe.wait_ge(*at("ffn_out", hf, t))

            memory_keys_values(1)
            to_channel_major(3, lambda t: ("h", 3, t), h, range(TILES))
            wait_hT(3)
            for m, name in enumerate("ag"):
                w = slot((name, 1)).rearrange("p (k n) -> p k n", k=KD)
                for c in range(NCH):
                    b = open_bank(name, c)
                    for k in range(KD):
                        ins = mm(bank[b][:, 0:T], w[:, k, c * P:(c + 1) * P], hT[:, k, :],
                                 start=k == 0, stop=k == KD - 1)
                    ins.then_inc(full[b], 1)
                release((name, 1), name, NCH - 1)
                if m == 0:
                    pe.wait_ge(*at("cpre_in"))
                    for n in range(2):
                        b = open_bank("cpre", n)
                        for c in range(NCH):
                            ins = tr(bank[b][:, c * 120:(c + 1) * 120], PT[n][0:120, c * P:(c + 1) * P],
                                     ident[0:120, 0:120])
                        ins.then_inc(full[b], 1)
            for n, (k, t) in enumerate(ZSEQ[1]):
                if t == 0:
                    w = slot((k, 1)).rearrange("p (k n) -> p k n", k=KD)
                token_product(("z", k, 1, t), hT, w, KD, t)
                if t == 2:
                    release((k, 1), "z", k, 1, 2)
                if n >= lag and ZSEQ[1][n - lag][0] != "v":
                    unit_transpose(UNIT[ZSEQ[1][n - lag][0], 1, ZSEQ[1][n - lag][1]])
            pe.wait_ge(*taken("a", NCH - 1))
            for n, (src, rows) in enumerate((("p", P), ("s", NSAMP))):
                b = open_bank("cst", src)
                for c in range(NCH):
                    t_in = convF[:, c, CBUF + P:CBUF + SEQ] if n == 0 else \
                        conv_new[:, c, :]
                    ins = tr(bank[b][0:rows, c * P:(c + 1) * P], t_in, ident)
                ins.then_inc(full[b], 1)
            self_attention(1)
            out_projection(1)
            to_channel_major(4, lambda t: ("h", 4, t), h, range(TILES))
            cross_attention(1)
            to_channel_major(5, lambda t: ("h", 5, t), h, range(TILES))
            wait_hT(5)

            b = open_bank("rt")
            for t in range(TILES):
                for k in range(KD):
                    ins = mm(bank[b][0:ROWS[t], 8 * t:8 * t + 8], hT[:, k, t * P:t * P + ROWS[t]], wrt[:, k, :],
                             start=k == 0, stop=k == KD - 1)
            ins.then_inc(full[b], 1)
            pe.wait_ge(*at("picked"))
            b = open_bank("rank")
            for t in range(TILES):
                for s in range(t + 1):
                    mm(bank[b][0:ROWS[t], 8 * t:8 * t + 8], C("before" if s == t else "ones")[0:ROWS[s], 0:ROWS[t]],
                       picked[0:ROWS[s], s, :], start=s == 0, stop=s == t)
            for s in range(TILES):
                ins = mm(bank[b][:, 24:32], C("ones")[0:ROWS[s], :], picked[0:ROWS[s], s, :],
                         start=s == 0, stop=s == TILES - 1)
            ins.then_inc(full[b], 1)
            for b in range(8):
                pe.wait_ge(free[b], banks.uses(b))

            def split_product(n, m, j, out, x_hi_lo, chunks):
                for q in range(2):
                    i = 2 * PRODUCTS.index((m, j)) + q
                    pe.wait_ge(moe_lo, n * NPIECE + (i + 1))
                    w = [t[i % PRING].rearrange("p (k n) -> p k n", k=chunks) for t in (high, low)]
                    for k in range(chunks):
                        kk = q * chunks + k
                        for xa, wa in ((0, 0), (1, 0), (0, 1)):
                            for dst, wcols in out(w[wa][:, k, :]):
                                ins = mm(dst, x_hi_lo[xa][kk], wcols,
                                         start=(m < 2 or j == 0) and kk == 0 and (xa, wa) == (0, 0),
                                         stop=(m < 2 or j == STAGES - 1) and kk == 2 * chunks - 1 and wa == 1)
                    ins.then_inc(moe_used, 1)

            def scatter(i, done):
                t, hf = i // 2, i % 2
                mm(bank[6 + i % 2][0:ROWS[t], :], moe_GT[:, t * P:t * P + ROWS[t]],
                   moe_y[:, hf * HALF:(hf + 1) * HALF], start=True, stop=True).then_inc(done, 1)

            def expert(n, r=None):
                if r is not None:
                    pe.wait_ge(moe_zero, r + 1)
                pe.wait_ge(moe_sel, n + 1)
                if r is not None:
                    pe.wait_ge(moe_addedE, r * 6)
                pe.wait_ge(moe_GTc, n)
                for half in range(2):
                    if half:
                        pe.wait_ge(moe_xT, n * 2 + 1)
                    for k in range(4):
                        for t in range(TILES):
                            ins = mm(bank[7][:, k * P:(k + 1) * P],
                                     h[0:ROWS[t], t, (4 * half + k) * P:(4 * half + k + 1) * P],
                                     moe_P[0:ROWS[t], t, :], start=t == 0, stop=t == TILES - 1)
                    ins.then_inc(moe_gathered, 1)
                pe.wait_ge(moe_xT, n * 2 + 2)

                def product(m, j):
                    pe.wait_ge(moe_silu if m == 0 else moe_h, n * STAGES + max(j - 1, 0))
                    split_product(n, m, j, lambda w: [(bank[2 * m + j % 2][:, :], w)],
                                  [[moe_x[i][:, k, :] for k in range(KD)] for i in range(2)], KD // 2)

                def hidden_transpose(j):
                    pe.wait_ge(moe_h, n * STAGES + (j + 1))
                    if j:
                        pe.wait_ge(moe_hT, n * STAGES + j)
                    else:
                        pe.wait_ge(moe_added, n * 6 + 5)
                    for c in range(4):
                        ins = tr(bank[6][:, c * P:(c + 1) * P], moe_hid[j % 2][:, c * P:(c + 1) * P], ident)
                    ins.then_inc(moe_tr, 1)

                def down_product(j):
                    pe.wait_ge(moe_hT, n * STAGES + (j + 1))
                    if j == 0:
                        pe.wait_ge(moe_yc, n * 2)
                    split_product(n, 2, j,
                                  lambda w: [(bank[4 + hf][:, :], w[:, hf * HALF:(hf + 1) * HALF]) for hf in range(2)],
                                  [[moe_hidT[i][:, k * P:(k + 1) * P] for k in range(4)] for i in range(2)], 2)

                product(0, 0)
                pe.wait_ge(moe_yc, n * 2)
                pe.wait_ge(moe_hT, n * STAGES)
                scatter(0, moe_scattered)
                scatter(1, moe_scattered)
                product(1, 0)
                pe.wait_ge(moe_added, n * 6 + 1)
                scatter(2, moe_scattered)
                pe.wait_ge(moe_added, n * 6 + 2)
                scatter(3, moe_scattered)
                product(0, 1)
                pe.wait_ge(moe_added, n * 6 + 3)
                scatter(4, moe_scattered)
                pe.wait_ge(moe_added, n * 6 + 4)
                scatter(5, moe_scattered)
                hidden_transpose(0)
                product(1, 1)
                down_product(0)
                pe.wait_ge(moe_added, n * 6 + 6)
                for t in range(TILES):
                    ins = tr(bank[7][:, t * P:t * P + ROWS[t]], moe_G[0:ROWS[t], t, :],
                             ident[0:ROWS[t], 0:ROWS[t]])
                ins.then_inc(moe_GTr, 1)
                for j in range(1, STAGES):
                    if j + 1 < STAGES:
                        product(0, j + 1)
                    hidden_transpose(j)
                    if j + 1 < STAGES:
                        product(1, j + 1)
                    down_product(j)

            def expert_round(r):
                if type(r) is int:
                    pe.wait_ge(moe_zero, r + 1)
                with pe.Fori(0, NE) as e:
                    expert(e + r * NE, None if type(r) is int else r)
                pe.wait_ge(moe_yc, r * 16 + 16)
                for i in range(6):
                    if i >= 2:
                        pe.wait_ge(moe_addedE, r * 6 + (i - 1))
                    else:
                        pe.wait_ge(*((moe_hT, (r + 1) * NE * STAGES) if i == 0 else (moe_GTc, (r + 1) * NE)))
                    scatter(i, moe_scatteredE)

            expert_round(0)
            pe.wait_ge(*at("cmax"))
            most = pe.value_load(cmax_i[0:1, 0:1])
            with pe.If(most > CAP):
                with pe.Fori(1, ROUNDS) as r:
                    expert_round(r)

        @block.sync
        def _(sp):
            def wait_group(*key):
                b, use = banks.of(*key)
                sp.wait_ge(full[b], use)

            def stream_load(n):
                key, src = stream[n]
                s = n % RING
                if n0 <= n < n0 + RING and s < 2:
                    sp.wait_ge(ffn_up, 2 * FBLK if s == 0 else 2 * (FBLK - 1))
                elif n >= RING:
                    wait_group(*releases.get(stream[n - RING][0], ("fl",)))
                dst = slots[s].rearrange("p (k n) -> p k n", k=src.shape[1])
                sp.dma_start(dst, src).then_inc(slot_full[s], 16)

            def page(i):
                return sp.value_load(pt[0:1, i:i + 1], min_val=0, max_val=a["cache_fox_k"].shape[1] - 1)

            def key_load(stage, hf, j):
                n = (stage * 2 + hf) * 8 + j
                if n >= 4:
                    m = n - 4
                    wait_group("kt", m // 16, m // 8 % 2, m % 8)
                l, b, g = stage // 2, 4 * hf + j // 2, j % 2
                if stage % 2 == 0:
                    src = a["cache_fox_k" if l == 0 else "cache_sb_k"][0][page(2 * b + g), :, :, :]
                else:
                    src = a["cache_mem_k"][l, b, g * P:(g + 1) * P]
                sp.dma_start(knat[:, j % 4, :], src.rearrange("s h d -> s (h d)")).then_inc(knat_full[j % 4], 16)

            def value_loads(stage, hf):
                l = stage // 2
                for j in range(8):
                    b, g = 4 * hf + j // 2, j % 2
                    if stage % 2 == 0:
                        src = a["cache_fox_v" if l == 0 else "cache_sb_v"][0][page(2 * b + g), :, :, :]
                    else:
                        src = a["cache_mem_v"][l, b, g * P:(g + 1) * P]
                    sp.dma_start(vC[:, j // 2, g, :], src.rearrange("s h d -> s (h d)")) \
                        .then_inc(*sets("v_in", stage, hf, by=16))

            sp.dma_start(cbuf[:, 0:P + 1], a["const_table"][:, 0:P + 1]).then_inc(*sets("head_in", by=16))
            sp.dma_start(mem, a["mem_prompt"][0].rearrange("(t p) d -> p t d", p=P)).then_inc(*sets("mem_in", 0, by=16))
            stream_load(0)
            sp.dma_start(x[:, 0:2, :], a["x_prompt"][0].rearrange("(t p) d -> p t d", p=P)).then_inc(*sets("x_in", by=16))
            sp.dma_start(x[0:NSAMP, 2, :], a["x_sample"].rearrange("b s d -> (b s) d")).then_inc(*sets("x_in", by=16))
            stream_load(1)
            sp.dma_start(PT[0][0:NB * PBUF, :], a["state_pool"][0].rearrange("b j c -> (b j) c")) \
                .then_inc(*sets("pre_in", by=16))
            sp.dma_start(cbuf[:, P + 1:], a["const_table"][:, P + 1:]).then_inc(*sets("table_in", by=16))
            for n in range(2, 5):
                stream_load(n)
            sp.wait_ge(*at("pt_in"))
            for j in range(16):
                sp.dma_start(lfp[:, j // 2, j % 2, :], a["cache_fox_logf"][0][page(j), :, :]) \
                    .then_inc(*sets("lfp_in", by=16))
            for l in range(2):
                base = 0 if l == 0 else n0
                st = 2 * l
                if l == 1:
                    wait_group("tc", 2, 2, 1)
                    sp.dma_start(mem, a["mem_prompt"][0].rearrange("(t p) d -> p t d", p=P)) \
                        .then_inc(*sets("mem_in", 1, by=16))
                    stream_load(n0)
                    stream_load(n0 + 1)
                    stream_load(n0 + 2)
                    for n in range(2):
                        sp.dma_start(PT[n][0:120, :],
                                     a["state_conv"][0, 4 * n:4 * n + 4].rearrange("b j c -> (b j) c")) \
                            .then_inc(*sets("cpre_in", by=16))
                    for n in range(3, 7):
                        stream_load(n0 + n)
                for j in range(4):
                    key_load(st, 0, j)
                if l == 0:
                    value_loads(st, 0)
                first = 5 if l == 0 else n0 + 7
                for n in range(first, first + (4 if l == 0 else 3)):
                    stream_load(n)
                for j in range(4, 8):
                    key_load(st, 0, j)
                if l == 1:
                    sp.wait_ge(*at("y_mix", NCH - 1))
                    value_loads(st, 0)
                for j in range(8):
                    key_load(st, 1, j)
                wait_group("os", l, 1)
                value_loads(st, 1)
                for j in range(4):
                    key_load(st + 1, 0, j)
                wait_group("os", l, 3)
                value_loads(st + 1, 0)
                stream_load(first + (4 if l == 0 else 3))
                for j in range(4, 8):
                    key_load(st + 1, 0, j)
                for j in range(8):
                    key_load(st + 1, 1, j)
                wait_group("cos", l, 0)
                value_loads(st + 1, 1)
                if l == 0:
                    wg = a["w_gate"][0].rearrange("(k p) (i n) -> i p k n", p=P, n=256)
                    wu = a["w_up"][0].rearrange("(k p) (i n) -> i p k n", p=P, n=256)
                    wd = a["w_down"][0].rearrange("(i f p) n -> i p f n", p=P, f=2)

                    def ffn_loads(blk, i):
                        half = slots[blk].rearrange("p (m k n) -> p m k n", m=2, k=KD)
                        sp.dma_start(half[:, 0], wg[i]).then_inc(slot_full[blk], 16)
                        sp.dma_start(half[:, 1], wu[i]).then_inc(slot_full[blk], 16)

                    def down_load(blk, i):
                        dst = slots[3 + blk][:, 0:2 * D].rearrange("p (f n) -> p f n", f=2)
                        sp.dma_start(dst, wd[i]).then_inc(slot_full[3 + blk], 16)

                    for blk in range(2):
                        m = max(n for n in range(n0) if n % RING == blk)
                        wait_group(*releases.get(stream[m][0], ("fl",)))
                        ffn_loads(blk, blk)
                    wait_group("cos", 0, 1)
                    for blk in range(2):
                        down_load(blk, blk)
                    with sp.Fori(0, FBLK // 2 - 1) as i:
                        for blk in range(2):
                            sp.wait_ge(ffn_up, i * 4 + 2 * (blk + 1))
                            ffn_loads(blk, i * 2 + (2 + blk))
                            sp.wait_ge(ffn_down, i * 4 + 2 * (blk + 1))
                            down_load(blk, i * 2 + (2 + blk))
                    sp.wait_ge(ffn_up, 2 * (FBLK - 2))
                    ffn_loads(0, FBLK - 1)
                    sp.wait_ge(ffn_down, 2 * (FBLK - 2))
                    down_load(0, FBLK - 1)

            eg = a["we_gate"][0].rearrange("e (k p) (j n) -> e j p k n", p=P, n=FB)
            eu = a["we_up"][0].rearrange("e (k p) (j n) -> e j p k n", p=P, n=FB)
            ed = a["we_down"][0].rearrange("e (j k p) n -> e j p k n", p=P, k=4)

            def expert_loads(e, n, first=False):
                for i, (m, j, q) in enumerate(PIECES):
                    if i >= PRING or not first:
                        sp.wait_ge(moe_used, n * NPIECE + (i + 1 - PRING))
                    elif i < 4:
                        wait_group(*releases.get(stream[max(p for p in range(len(stream))
                                                            if p % RING == 1 + i // 2)][0], ("fl",)))
                    else:
                        wait_group("cos", 1, 1)
                    w = (eg, eu, ed)[m]
                    chunks = 4 if m < 2 else 2
                    sp.dma_start(raw[i % PRING].rearrange("p (k n) -> p k n", k=chunks),
                                 w[e, j][:, q * chunks:(q + 1) * chunks, :]).then_inc(raw_full[i % PRING], 16)

            expert_loads(0, 0, first=True)
            with sp.Fori(1, NE) as e:
                expert_loads(e, e)
            sp.wait_ge(*at("cmax"))
            most = sp.value_load(cmax_i[0:1, 0:1])
            with sp.If(most > CAP):
                with sp.Fori(1, ROUNDS) as r:
                    with sp.Fori(0, NE) as e:
                        expert_loads(e, e + r * NE)
            sp.wait_ge(*at("x_final"))
            sp.dma_start(o["y_prompt"][0].rearrange("(t p) d -> p t d", p=P), x[:, 0:2, :]).then_inc(*sets("y_out", by=16))
            sp.dma_start(o["y_sample"].rearrange("b s d -> (b s) d"), x[0:NSAMP, 2, :]).then_inc(*sets("y_out", by=16))
            sp.wait_ge(*at("y_out"))

        @block.gpsimd
        def _(pool):
            tt, ts = nc.gpsimd.tensor_tensor, nc.gpsimd.tensor_scalar

            def after_group(*key):
                b, use = banks.of(*key)
                pool.wait_ge(full[b], use)

            pool.dma_start(pt[0:1, :], a["page_table"].rearrange("b g -> (b g)").rearrange("(o n) -> o n", o=1)) \
                .then_inc(*sets("pt_in", by=16))
            pool.dma_start(gain[:, :], spread(a["norm_mix"][0])).then_inc(*sets("gain", 0, by=16))
            nc.gpsimd.memset(qz_t[:, :], 0.0).then_inc(*sets("qz0"))
            nc.gpsimd.memset(qbd, 0.0).then_inc(*sets("qbd0", 0))
            nc.gpsimd.memset(big[:, 14336:16384], 0.0).then_inc(*sets("lb0"))
            pool.wait_ge(*at("head_in"))

            def unit_power(u):
                kind, l, t = UNITS[u]
                hd = HD if kind in "qk" else XHD
                nh = HALF // hd
                i = u % 2
                r = ROWS[t]
                pool.wait_ge(*at("u_ss", u))
                ts(u_ms[i][0:r, 0:nh], u_ss[i][0:r, 0:nh], 1.0 / hd, EPS, ALU.mult, ALU.add) \
                    .then_inc(*sets("u_ms", u))
                pool.wait_ge(*at("u_ms", u))
                tt(u_rs[i][0:r, 0:nh], u_ms[i][0:r, 0:nh], view(C("minus_half")[0:r], 0, [[0, nh]]), ALU.pow) \
                    .then_inc(*sets("u_rs", u))

            def unit_store(u, dst):
                pool.wait_ge(*at("unit", u))
                pool.dma_start(dst, nbuf[u % 2][0:ROWS[UNITS[u][2]], :]).then_inc(*sets(f"u_out{u % 2}", u, by=16))

            def norm_power(j):
                for t in range(TILES):
                    r = ROWS[t]
                    pool.wait_ge(*at("n_ss", j, t))
                    ts(n_ms[0:r, t:t + 1], n_ss[0:r, t:t + 1], 1.0 / D, EPS, ALU.mult, ALU.add) \
                        .then_inc(*sets("n_ms", j, t))
                    pool.wait_ge(*at("n_ms", j, t))
                    tt(n_rs[0:r, t:t + 1], n_ms[0:r, t:t + 1], C("minus_half", 0, 1)[0:r], ALU.pow) \
                        .then_inc(*sets("n_rs", j, t))

            def gain_load(j):
                src = a[("norm_mix", "norm_cross", "norm_ffn")[j % 3]][j // 3]
                pool.wait_ge(*at("h", j - 1, 2))
                pool.dma_start(gain[:, :], spread(src)).then_inc(*sets("gain", j, by=16))

            def memory(l):
                for t in range(2):
                    u = UNIT["mk", l, t]
                    unit_power(u)
                    unit_store(u, o["mem_k_p"][l, 0, t * P:(t + 1) * P].rearrange("s h d -> s (h d)"))
                for t in range(2):
                    pool.wait_ge(*taken("z", "mv", l, t))
                    pool.dma_start(o["mem_v_p"][l, 0, t * P:(t + 1) * P].rearrange("s h d -> s (h d)"), vM[:, t, :]) \
                        .then_inc(*sets("vM_out", l, t, by=16))

            def new_rows(name, t):
                if t < 2:
                    return o[name + "_p"][0, 0, t * P:(t + 1) * P].rearrange("s h d -> s (h d)")
                return o[name + "_s"][0].rearrange("b s h d -> (b s) (h d)")

            def state_stores(l, name, nbuf_, src):
                pool.wait_ge(*taken("pst" if l == 0 else "cst", "p"))
                pool.dma_start(o[name + "_p"][0, 0], PT[0][P - nbuf_:P, :]).then_inc(*sets("state_out", l, by=16))
                pool.wait_ge(*taken("pst" if l == 0 else "cst", "s"))
                for b in range(NB):
                    pool.dma_start(o[name + "_s"][0, b, nbuf_ - NS:nbuf_], PT[1][b * NS:(b + 1) * NS, :]) \
                        .then_inc(*sets("state_out", l, by=16))
                pool.dma_start(o[name + "_s"][0, :, 0:nbuf_ - NS], a[src][0, :, NS:nbuf_]) \
                    .then_inc(*sets("old_state_out", by=16))

            memory(0)
            pool.wait_ge(*at("const_in"))
            ts(hg[:, 0:64], hg[:, 0:64], HD ** -0.5, None, ALU.mult).then_inc(*sets("scaled_gain"))
            for l in range(2):
                ts(g_cq[l], g_cq[l], XHD ** -0.5, None, ALU.mult).then_inc(*sets("scaled_gain"))
            norm_power(0)
            for n, (k, t) in enumerate(ZSEQ[0]):
                if k != "v":
                    unit_power(UNIT[k, 0, t])
                if k == "k":
                    unit_store(UNIT[k, 0, t], new_rows("fox_k", t))
                if k == "v":
                    pool.wait_ge(*taken("z", "v", 0, t))
                    pool.dma_start(new_rows("fox_v", t), v[0:ROWS[t], t, :]).then_inc(*sets("v_out", 0, by=16))
            pool.wait_ge(*at("lb0"))
            pool.wait_ge(*at("lfp_in"))
            lfp_ap = lfp[:, 0, 0, :]
            for b2 in range(2):
                for pg in range(NPG):
                    nc.gpsimd.tensor_copy(
                        view(lb[:, 0, 0, :], (b2 * NPG + pg) * P + b2 * 64, [[2 * NPG * P, 4], [8, 8], [1, 8]]),
                        view(lfp_ap, (b2 * NPG + pg) * 8, [[2 * NPG * 8, 4], [1, 8], [0, 8]])) \
                        .then_inc(*sets("lb", 0))
            pool.wait_ge(*at("logf"))
            pool.wait_ge(*at("h", 0, 2))
            r = NSAMP
            for g in range(4):
                spread_f = view(logf[0:r, 2, :], 0, [[0, 2], [1, 8], [0, 8]])
                out1 = ln1_t[0:r, g * P:(g + 1) * P].rearrange("p (b h s) -> p b h s", b=2, h=8)
                out2 = ln2_t[0:r, g * P:(g + 1) * P].rearrange("p (b h s) -> p b h s", b=2, h=8)
                tt(out1, spread_f, view(C("own_upto")[0:r], g * 16, [[8, 2], [0, 8], [1, 8]]), ALU.mult) \
                    .then_inc(*sets("lb", 0))
                tt(out2, spread_f, view(C("own")[0:r], g * 2, [[1, 2], [0, 8], [0, 8]]), ALU.mult) \
                    .then_inc(*sets("lb", 0))
            pool.dma_start(o["fox_logf_p"][0, 0].rearrange("(t p) h -> p t h", p=P), logf[:, 0:2, :]) \
                .then_inc(*sets("logf_out", by=16))
            pool.dma_start(o["fox_logf_s"][0].rearrange("b s h -> (b s) h"), logf[0:NSAMP, 2, :]) \
                .then_inc(*sets("logf_out", by=16))
            state_stores(0, "pool", PBUF, "state_pool")
            for l in range(2):
                if l == 1:
                    pool.wait_ge(*at("ln_var"))
                    tt(ln_rs, ln_var, view(C("minus_half"), 0, [[0, TILES]]), ALU.pow).then_inc(*sets("ln_rs"))
                after_group("ss", l, 3)
                gain_load(3 * l + 1)
                nc.gpsimd.memset(qbd, 0.0).then_inc(*sets("qbd0", 2 * l + 1))
                norm_power(3 * l + 1)
                for t in range(TILES):
                    unit_power(UNIT["cq", l, t])
                gain_load(3 * l + 2)
                after_group("css", l, 1)
                if l == 0:
                    nc.gpsimd.memset(qbd, 0.0).then_inc(*sets("qbd0", 2))
                norm_power(3 * l + 2)
                if l == 0:
                    gain_load(3)
                    memory(1)
                    norm_power(3)
                    pool.wait_ge(*taken("chan"))
                    for n in range(2):
                        pool.wait_ge(*taken("cpre", n))
                    for c in range(NCH):
                        pool.wait_ge(*taken("a", c))
                        if c:
                            pool.wait_ge(conv_s, c)
                        tt(taps.rearrange("p (b s j) -> p b s j", b=NB, s=NS),
                           view(convF[:, c, :], CSEG, [[DSEG, NB], [1, NS], [1, CW]]),
                           view(cw[:, 0, c:c + 1], 0, [[0, NB], [0, NS], [1, CW]]), ALU.mult).then_inc(*sets("taps", c))
                        if c == 1:
                            unit_store(UNIT["k", 1, 0], new_rows("sb_k", 0))
                    for t in (1, 2):
                        unit_store(UNIT["k", 1, t], new_rows("sb_k", t))
                    for t in range(TILES):
                        pool.wait_ge(*taken("z", "v", 1, t))
                        pool.dma_start(new_rows("sb_v", t), v[0:ROWS[t], t, :]).then_inc(*sets("v_out", 1, by=16))
                    state_stores(1, "conv", CBUF, "state_conv")
            for name in ("u_out0", "u_out1", "vM_out", "v_out", "state_out", "old_state_out", "logf_out"):
                pool.wait_ge(marks.sem(name), marks.count[name])


        @block.scalar
        def _(act):
            A = nc.scalar.activation

            def take(*key):
                b, use = banks.of(*key)
                act.wait_ge(full[b], use)
                return b

            def copy(out, in_):
                return A(out, in_, ACT.Copy)

            def to_hT(j, tiles):
                for t in tiles:
                    b = take("tc", j, t, 0)
                    copy(hT[:, 0:4, t * P:t * P + ROWS[t]],
                         bank[b][:, :].rearrange("p (k c) -> p k c", k=4)[:, :, 0:ROWS[t]]).then_inc(free[b], 1)

            def unit_squares(u):
                kind, l, t = UNITS[u]
                if l == 1 and kind in "qk":
                    return
                b = take("z", kind, l, t)
                if u >= 2 and not (UNITS[u - 2][1] == 1 and UNITS[u - 2][0] in "qk"):
                    act.wait_ge(*at("u_ss", u - 2))
                A(Pr[u % 2][0:ROWS[t], :], bank[b][0:ROWS[t], :], ACT.Square).then_inc(*sets("u_sq", u))

            def unit_spread(u):
                kind, l, t = UNITS[u]
                b = take("ut", u)
                src = bank[b][:, :].rearrange("p (c r) -> p c r", c=4)[:, :, 0:ROWS[t]]
                if kind == "k":
                    ins = copy(kN[:, :, t * P:t * P + ROWS[t]], src)
                elif kind == "mk":
                    ins = copy(kM[:, :].rearrange("p c t -> p c t")[:, :, t * P:(t + 1) * P], src)
                elif kind == "q" and t < 2:
                    if t == 0 and l == 0:
                        act.wait_ge(*at("qz0"))
                    copy(qz[0:64, :, 0, t * P:(t + 1) * P], src[0:64])
                    ins = copy(qz[64:P, :, 1, t * P:(t + 1) * P], src[64:P])
                elif kind == "q":
                    act.wait_ge(*at("qbd0", 2 * l))
                    for z in range(2):
                        for b2 in range(2):
                            ins = copy(view(qbd[64 * z:64 * z + 64], b2 * (NCH * P + 64) + 8 * z,
                                            [[2 * NCH * P, 4], [P + 16, NCH], [1, NS]]),
                                       view(bank[b][64 * z:64 * z + 64, :], b2 * 8, [[16, 4], [P, NCH], [1, NS]]))
                elif t < 2:
                    ins = copy(kN[:, :, t * P:(t + 1) * P], src)
                else:
                    act.wait_ge(*at("qbd0", 2 * l + 1))
                    for g in range(2):
                        ins = copy(view(qbd, g * 16 * P, [[XH * P + 32, 4], [P + 8, XH], [1, NS]]),
                                   view(bank[b][:, :], g * 32, [[8, 4], [P, XH], [1, NS]]))
                ins.then_inc(free[b], 1)

            def norm_squares(j):
                for t in range(TILES):
                    act.wait_ge(*(at("x_in") if j == 0 else at("x", j, t)))
                    if j:
                        act.wait_ge(*at("n_rs", j - 1, t))
                    if j or t:
                        act.wait_ge(*at("n_ss", *((j, t - 1) if t else (j - 1, 2))))
                    A(Pr_t[0:ROWS[t], :], x[0:ROWS[t], t, :], ACT.Square,
                      accum_out=n_ss[0:ROWS[t], t:t + 1]).then_inc(*sets("n_ss", j, t))

            def memory(l):
                to_hT(("mem", l), range(2))
                for t in range(2):
                    unit_squares(UNIT["mk", l, t])
                for t in range(2):
                    b = take("z", "mv", l, t)
                    if l == 1:
                        act.wait_ge(*at("vM_out", 0, 1))
                    copy(vM[:, t, :], bank[b][:, :]).then_inc(free[b], 1)
                    unit_spread(UNIT["mk", l, t])

            def inputs(l):
                for n, (k, t) in enumerate(ZSEQ[l]):
                    if k == "v":
                        b = take("z", "v", l, t)
                        if l == 1:
                            act.wait_ge(*at("v_out", 0))
                        copy(v[0:ROWS[t], t, :], bank[b][0:ROWS[t], :]).then_inc(free[b], 1)
                    else:
                        unit_squares(UNIT[k, l, t])
                    if n >= 2 and ZSEQ[l][n - 2][0] != "v":
                        unit_spread(UNIT[ZSEQ[l][n - 2][0], l, ZSEQ[l][n - 2][1]])

            def keys_out(stage, hf, js):
                for j in js:
                    if j % 2 == 0:
                        b = take("kt", stage, hf, j)
                        copy(kT[:, :, j // 2, (j % 2) * P:(j % 2 + 1) * P],
                             bank[b][:, :].rearrange("p (c k) -> p c k", c=4)).then_inc(free[b], 1)

            def head_out(l, hd):
                keys_out(2 * l, 0, [hd])
                b = take("pt", l, hd)
                if hd == 0:
                    act.wait_ge(*at("state_out", l))
                copy(PT[hd % 2][:, 0:3 * P], bank[b][:, 0:3 * P]).then_inc(free[b], 1)
                if hd % 2:
                    c = hd // 2
                    b = take("o", l, c)
                    copy(yT[0:64, 4 + c, 0:SEQ], bank[b][0:64, 0:SEQ])
                    copy(yT[64:P, 4 + c, 0:SEQ], bank[b][64:P, SEQ:2 * SEQ]).then_inc(free[b], 1)

            def sample_out(l, g):
                b = take("pts", l, g)
                copy(PT[g % 2][:, 0:2 * P], bank[b][:, 0:2 * P])
                copy(PT[g % 2][0:NSAMP, 2 * P:3 * P], bank[b][0:NSAMP, 2 * P:3 * P]).then_inc(free[b], 1)
                b = take("os", l, g)
                for z in range(2):
                    ins = copy(view(yT[64 * z:64 * z + 64, 0, :], 4 * T + SEQ + 16 * g, [[T, NCH], [8, 2], [1, NS]]),
                               view(bank[b][64 * z:64 * z + 64, :], 8 * z, [[32, NCH], [16, 2], [1, NS]]))
                ins.then_inc(free[b], 1)

            def softmax_exp(key, i, src, dst, col=0):
                act.wait_ge(*at("neg_max", *key))
                return A(dst, src, ACT.Exp, bias=a_nm[i % 4][:, col:col + 1], accum_out=a_sm[i % 4][:, col:col + 1])

            def forget_attention():
                for i in range(2 * NH):
                    hd, qt = i // 2, i % 2
                    if hd >= 2:
                        b, use = banks.of("pt", 0, hd - 2)
                        act.wait_ge(full[b], use)
                    nk = (qt + 1) * P
                    if i >= 4:
                        act.wait_ge(*at("probs", 0, "p", (i - 4) // 2, i % 2))
                    softmax_exp((0, "p", hd, qt), i, S[i % 2][:, 0:nk], Pr[hd % 2][:, qt * P:qt * P + nk]) \
                        .then_inc(*sets("exp", 0, "p", hd, qt))
                    if i % 2 and i >= 3:
                        head_out(0, hd - 1)
                head_out(0, NH - 1)
                for hf in range(2):
                    if hf:
                        keys_out(0, 1, range(8))
                    for g in (2 * hf, 2 * hf + 1):
                        b, use = banks.of("ss", 0, g)
                        i = 2 * NH + g
                        k, n = ("pt", NH - 2 + g) if g < 2 else ("pts", g - 2)
                        b2, use2 = banks.of(k, 0, n)
                        act.wait_ge(full[b2], use2)
                        act.wait_ge(*(at("probs", 0, "p", NH - 2 + g // 2, g % 2) if g < 4 else at("probs", 0, "s", g - 4)))
                        softmax_exp((0, "s", g), i, bank[b][:, 0:T], Pr[g % 2][:, 0:T]) \
                            .then_inc(*sets("exp", 0, "s", g))
                    for g in (2 * hf, 2 * hf + 1):
                        sample_out(0, g)

            def stick_before(i, bkey, ukey, n, dst):
                b = take(*bkey)
                A(dst, bank[b][:, 0:n], ACT.Abs).then_inc(*sets("abs", *ukey))
                act.wait_ge(*at("abs", *ukey))
                A(dst, dst, ACT.Exp, scale=-1.0).then_inc(*sets("exp_abs", *ukey))
                act.wait_ge(*at("exp_abs", *ukey))
                A(L[i % 2][:, 0:n], dst, ACT.Ln, bias=1.0).then_inc(*sets("log1p", *ukey))

            def stick_exp(i, ukey, n, dst):
                act.wait_ge(*at("log_a", *ukey))
                A(dst, L[i % 2][:, 0:n], ACT.Exp, bias=a_nm[i % 4][:, 0:1]).then_inc(*sets("stick_exp", *ukey))

            def stick_attention():
                def log1p(pair):
                    heads = (2 * pair, 2 * pair + 1)
                    for hd in heads:
                        b = take("s", 1, hd)
                        A(stick_S[hd % 4], bank[b][:, 0:3 * P], ACT.Abs).then_inc(*sets("abs", hd))
                    for hd in heads:
                        act.wait_ge(*at("abs", hd))
                        A(stick_S[hd % 4], stick_S[hd % 4], ACT.Exp, scale=-1.0).then_inc(*sets("exp_abs", hd))
                    for hd in heads:
                        act.wait_ge(*at("exp_abs", hd))
                        A(stick_L[hd % 4], stick_S[hd % 4], ACT.Ln, bias=1.0).then_inc(*sets("log1p", hd))

                def weights(pair):
                    for hd in (2 * pair, 2 * pair + 1):
                        act.wait_ge(*at("log_a", hd))
                        for qt in range(2):
                            ins = A(stick_P[hd % 4][:, qt * P:(2 * qt + 1) * P],
                                    stick_L[hd % 4][:, qt * P:(2 * qt + 1) * P], ACT.Exp,
                                    bias=a_nm[hd % 4][:, qt:qt + 1])
                        ins.then_inc(*sets("stick_exp", hd))

                log1p(0)
                state_out("cst")
                act.wait_ge(*at("cent"))
                A(squares, conv, ACT.Square).then_inc(*sets("cent_sq"))
                log1p(1)
                for pair in range(NH // 2):
                    weights(pair)
                    if pair + 2 < NH // 2:
                        log1p(pair + 2)
                    head_out(1, 2 * pair)
                    head_out(1, 2 * pair + 1)
                    if pair == 1:
                        act.wait_ge(*at("scaled"))
                        for c in range(NCH):
                            A(yT[:, c, :], conv[:, c, :], ACT.Silu, bias=chan[:, 3, c:c + 1],
                              scale=chan[:, 2, c:c + 1]).then_inc(*sets("y_mix", c))
                for hf in range(2):
                    if hf:
                        keys_out(2, 1, range(8))
                    for g in (2 * hf, 2 * hf + 1):
                        k, n = ("pt", NH - 2 + g) if g < 2 else ("pts", g - 2)
                        b2, use2 = banks.of(k, 1, n)
                        act.wait_ge(full[b2], use2)
                        stick_before(g, ("ss", 1, g), ("s", g), T, Pr[g % 2][:, 0:T])
                    for g in (2 * hf, 2 * hf + 1):
                        stick_exp(g, ("s", g), T, Pr[g % 2][:, 0:T])
                    for g in (2 * hf, 2 * hf + 1):
                        sample_out(1, g)

            def cross_attention(l):
                stage = 2 * l + 1
                for t in range(TILES):
                    unit_squares(UNIT["cq", l, t])
                    if t:
                        unit_spread(UNIT["cq", l, t - 1])
                unit_spread(UNIT["cq", l, 2])

                def exps(hd):
                    b = take("cs", l, hd)
                    if hd >= 2:
                        b2, use2 = banks.of("cpt", l, hd - 2)
                        act.wait_ge(full[b2], use2)
                    for qt in range(2):
                        ins = softmax_exp((l, "cp", hd), hd, bank[b][:, qt * NMEM:(qt + 1) * NMEM],
                                          Pr[hd % 2][:, qt * NMEM:(qt + 1) * NMEM], qt)
                    ins.then_inc(*sets("exp", l, "cp", hd))

                exps(0)
                for hd in range(XH):
                    if hd + 1 < XH:
                        exps(hd + 1)
                    keys_out(stage, 0, [2 * hd, 2 * hd + 1])
                    b = take("cpt", l, hd)
                    copy(PT[hd % 2][:, :], bank[b][:, :]).then_inc(free[b], 1)
                    b = take("co", l, hd)
                    copy(yT[:, hd, 0:SEQ], bank[b][:, 0:SEQ]).then_inc(free[b], 1)
                for hf in range(2):
                    if hf:
                        keys_out(stage, 1, range(8))
                    b = take("css", l, hf)
                    softmax_exp((l, "cs", hf), hf, bank[b][:, 0:NMEM], Pr[hf][:, 0:NMEM]).then_inc(*sets("exp", l, "cs", hf))
                    b = take("cpts", l, hf)
                    copy(PT[hf][:, 0:2 * P], bank[b][:, 0:2 * P]).then_inc(free[b], 1)
                    b = take("cos", l, hf)
                    copy(view(yT[:, 0, :], SEQ + 32 * hf, [[T, XH], [1, 32]]),
                         bank[b][:, 0:P].rearrange("p (h r) -> p h r", h=XH)).then_inc(free[b], 1)

            def state_out(name):
                for n, (src, rows) in enumerate((("p", P), ("s", NSAMP))):
                    b = take(name, src)
                    copy(PT[n][0:rows, :], bank[b][0:rows, :]).then_inc(free[b], 1)

            def const_load(dst, src):
                act.dma_start(dst, src).then_inc(*sets("const_in", by=16))

            act.dma_start(hg[:, 384:512], spread(a["g_ck"][0])).then_inc(*sets("ck_gain_in", by=16))
            act.dma_start(hg2[:, :], spread(a["g_ck"][1])).then_inc(*sets("ck_gain_in", by=16))
            const_load(g_fq, spread(a["g_fq"][0]))
            const_load(hg[:, 64:128], spread(a["g_fk"][0]))
            for l in range(2):
                const_load(g_cq[l], spread(a["g_cq"][l]))
            const_load(b_f, spread(a["b_f"][0]))
            const_load(b_r, spread(a["b_router"][0]))
            const_load(wfl, a["w_in_e"][0].rearrange("(k p) n -> p k n", p=P)[:, :, 4 * HALF:4 * HALF + NH])
            const_load(wrt, a["w_router"][0].rearrange("(k p) n -> p k n", p=P))
            const_load(wpg, a["w_pool_grp"][0].rearrange("g c d -> c g d"))
            for n, name in enumerate(("pool_scale", "conv_b", "ln_g", "ln_b")):
                const_load(PT[1][n:n + 1, :], a[name])
            const_load(PT[1][4:4 + CW, :], a["conv_w"][0])
            memory(0)
            b = take("chan")
            copy(chan_t[:, :], bank[b][:, 0:(4 + CW) * NCH]).then_inc(free[b], 1)
            norm_squares(0)
            to_hT(0, range(TILES))
            inputs(0)
            act.wait_ge(*at("forget_abs"))
            A(lf_e, lf_a, ACT.Exp, scale=-1.0).then_inc(*sets("forget_exp"))
            act.wait_ge(*at("forget_exp"))
            A(lf_l, lf_e, ACT.Ln, bias=1.0).then_inc(*sets("forget_log"))
            for g in range(NCH):
                b = take("p", g)
                copy(poolF[:, g, PBUF:PSEG], bank[b][:, 0:SEQ])
                copy(pool_new[:, g, :], bank[b][:, SEQ:T])
                copy(view(poolF[:, g, :], PSEG + PBUF, [[SSEG, NB], [1, NS]]),
                     view(bank[b][:, :], SEQ, [[NS, NB], [1, NS]])).then_inc(free[b], 1)
            act.wait_ge(*at("logf"))
            for t in range(2):
                ins = copy(lr[:, t], view(logf[:, t, :], 0, [[1, NH], [0, P]]))
            ins.then_inc(*sets("lr", 0))
            state_out("pst")
            for g in range(NCH):
                b = take("pm", g)
                A(yT[:, g, :], bank[b][:, 0:T], ACT.Copy, scale=chan[:, 0, g:g + 1]).then_inc(free[b], 1)
            forget_attention()
            norm_squares(1)
            to_hT(1, range(TILES))
            cross_attention(0)
            norm_squares(2)
            to_hT(2, range(TILES))

            def ffn_silu_tile(f2, ff):
                act.wait_ge(ffn_gate, ff + 1)
                A(ffn_s[f2], bank[6][:, 0:T], ACT.Silu).then_inc(ffn_silu, 1)

            for f2 in range(2):
                ffn_silu_tile(f2, f2)
            with act.Fori(1, FBLK) as i:
                for f2 in range(2):
                    act.wait_ge(ffn_h, i * 2 + (f2 - 1))
                    ffn_silu_tile(f2, i * 2 + f2)

            memory(1)
            norm_squares(3)
            to_hT(3, range(TILES))
            for t in range(2):
                act.wait_ge(*at(f"u_out{UNIT['mk', 1, t] % 2}", UNIT["mk", 1, t]))
            for c in range(NCH):
                b = take("g", c)
                if c >= 2:
                    act.wait_ge(*taken("a", c - 2))
                A(S[c % 2], bank[b][:, 0:T], ACT.Sigmoid).then_inc(free[b], 1)
            inputs(1)
            stick_attention()
            norm_squares(4)
            to_hT(4, range(TILES))
            cross_attention(1)
            norm_squares(5)
            to_hT(5, range(TILES))
            act.wait_ge(*at("gap"))
            A(gw[:, :, 1:2], gw[:, :, 0:1], ACT.Exp).then_inc(*sets("gap_exp"))

            def expert(n):
                def weights_hi(b):
                    for i in (2 * b, 2 * b + 1):
                        act.wait_ge(raw_full[i % PRING], 16 * (n * (NPIECE // PRING) + (i // PRING + 1)))
                        copy(high[i % PRING], raw[i % PRING]).then_inc(moe_hi, 1)

                def silu(j):
                    act.wait_ge(*used(n, 0, j))
                    act.wait_ge(moe_h, n * STAGES + max(j - 1, 0))
                    A(moe_sg[j % 2], bank[j % 2][:, :], ACT.Silu).then_inc(moe_silu, 1)

                def hidden_hi(j):
                    act.wait_ge(moe_tr, n * STAGES + (j + 1))
                    if j:
                        act.wait_ge(*used(n, 2, j - 1))
                    else:
                        act.wait_ge(moe_used, n * NPIECE)
                    copy(moe_hidT[0], bank[6][:, :]).then_inc(moe_hThi, 1)

                weights_hi(0)
                for half in range(2):
                    act.wait_ge(moe_gathered, n * 2 + (half + 1))
                    copy(moe_x[0][:, 4 * half:4 * half + 4, :], bank[7][:, :].rearrange("p (k c) -> p k c", k=4)) \
                        .then_inc(moe_xhi, 1)
                weights_hi(1)
                for b, (m, j) in enumerate(PRODUCTS):
                    if b + 2 < len(PRODUCTS):
                        weights_hi(b + 2)
                    if m == 0:
                        silu(j)
                        if j:
                            hidden_hi(j - 1)
                hidden_hi(STAGES - 1)
                act.wait_ge(*used(n, 2, STAGES - 1))
                act.wait_ge(moe_scattered, n * 6 + 6)
                for hf in range(2):
                    copy(moe_y[:, hf * HALF:(hf + 1) * HALF], bank[4 + hf][:, :]).then_inc(moe_yc, 1)

            def expert_round(r):
                act.wait_ge(moe_zero, r + 1)
                with act.Fori(0, NE) as e:
                    expert(e + r * NE)
                act.wait_ge(moe_scatteredE, (r + 1) * 6)

            expert_round(0)
            act.wait_ge(*at("cmax"))
            most = act.value_load(cmax_i[0:1, 0:1])
            with act.If(most > CAP):
                with act.Fori(1, ROUNDS) as r:
                    expert_round(r)

        @block.vector
        def _(dve):
            V = nc.vector
            steps = [0]
            dve_step = sem("dve_step")

            def step(ins):
                ins.then_inc(dve_step, 1)
                steps[0] += 1
                dve.wait_ge(dve_step, steps[0])

            def take(*key):
                b, use = banks.of(*key)
                dve.wait_ge(full[b], use)
                return b

            def to_hT(j, tiles):
                for t in tiles:
                    b = take("tc", j, t, 1)
                    V.tensor_copy(hT[:, 4:8, t * P:t * P + ROWS[t]],
                                  bank[b][:, :].rearrange("p (k c) -> p k c", k=4)[:, :, 0:ROWS[t]]) \
                        .then_inc(free[b], 1)

            def unit(u):
                kind, l, t = UNITS[u]
                r = ROWS[t]
                i = u % 2
                nb = nbuf[i][0:r, :]
                if l == 1 and kind in "qk":
                    b = take("z", kind, l, t)
                    unit_buffer_free(u)
                    V.tensor_scalar(nb, bank[b][0:r, :], HD ** -0.5 if kind == "q" else 1.0, None, ALU.mult) \
                        .then_inc(*sets("unit", u))
                    dve.wait_ge(*at("unit", u))
                    freed(b)
                    return
                hd = HD if kind in "qk" else XHD
                nh = HALF // hd
                b, use = banks.of("z", kind, l, t)
                dve.wait_ge(*at("u_sq", u))
                if u >= 2 and ("u_rs", u - 2) in marks.known:
                    dve.wait_ge(*at("u_ms", u - 2))
                V.tensor_reduce(u_ss[i][0:r, 0:nh], Pr[i][0:r, :].rearrange("p (h d) -> p h d", h=nh), AX, ALU.add) \
                    .then_inc(*sets("u_ss", u))
                unit_buffer_free(u)
                dve.wait_ge(*at("u_rs", u))
                V.tensor_tensor(nb.rearrange("p (h d) -> p h d", h=nh),
                                bank[b][0:r, :].rearrange("p (h d) -> p h d", h=nh),
                                view(u_rs[i][0:r, 0:nh], 0, [[1, nh], [0, hd]]), ALU.mult).then_inc(free[b], 1)
                dve.wait_ge(free[b], use)
                g = {"q": g_fq, "k": g_fk, "cq": g_cq[l], "mk": g_ck[l]}[kind]
                V.tensor_tensor(nb.rearrange("p (h d) -> p h d", h=nh), nb.rearrange("p (h d) -> p h d", h=nh),
                                view(g[0:r, :], 0, [[0, nh], [1, hd]]), ALU.mult).then_inc(*sets("unit", u))

            def freed(b):
                dve.sem_inc(free[b], 1)

            def unit_buffer_free(u):
                if u >= 2:
                    take("ut", u - 2)
                    name = f"u_out{u % 2}"
                    last = max([w for w in range(u - 1) if (name, w) in marks.known], default=None)
                    if last is not None:
                        dve.wait_ge(*at(name, last))

            def norm(j):
                for t in range(TILES):
                    r = ROWS[t]
                    if t == 0:
                        dve.wait_ge(*at("gain", j))
                        if j:
                            last = {1: ("wo", 0, 1, 2), 2: ("wc", 0, 1, 2), 3: ("tc", ("mem", 1), 1, 1),
                                    4: ("wo", 1, 1, 2), 5: ("wc", 1, 1, 2)}[j]
                        else:
                            last = ("tc", ("mem", 0), 1, 1)
                        take(*last)
                    dve.wait_ge(*at("n_rs", j, t))
                    V.scalar_tensor_tensor(h[0:r, t, :], x[0:r, t, :], n_rs[0:r, t:t + 1], gain[0:r, :],
                                           ALU.mult, ALU.mult).then_inc(*sets("h", j, t))

            def residual(name, l, j):
                for hf in range(2):
                    for t in range(TILES):
                        b = take(name, l, hf, t)
                        xs = x[0:ROWS[t], t, hf * HALF:(hf + 1) * HALF]
                        V.tensor_tensor(xs, xs, bank[b][0:ROWS[t], :], ALU.add).then_inc(free[b], 1)
                        if hf == 1:
                            dve.wait_ge(*taken(name, l, 1, t))
                            dve.sem_inc(*sets("x", j, t))

            def keys_out(stage, hf, js):
                for j in js:
                    if j % 2:
                        b = take("kt", stage, hf, j)
                        V.tensor_copy(kT[:, :, j // 2, (j % 2) * P:(j % 2 + 1) * P],
                                      bank[b][:, :].rearrange("p (c k) -> p c k", c=4)).then_inc(free[b], 1)

            def normalize(key, i, probs, ncol=1):
                dve.wait_ge(*at("exp", *key))
                step(V.reciprocal(a_rc[i % 4][:, 0:ncol], a_sm[i % 4][:, 0:ncol]))
                if ncol == 1:
                    return V.tensor_scalar(probs, probs, a_rc[i % 4][:, 0:1], None, ALU.mult)
                p3 = probs.rearrange("p (q k) -> p q k", q=2)
                return V.tensor_tensor(p3, p3, view(a_rc[i % 4], 0, [[1, 2], [0, NMEM]]), ALU.mult)

            def forget_attention():
                def scores(i):
                    hd, qt = i // 2, i % 2
                    nk = (qt + 1) * P
                    b = take("s", 0, hd, qt)
                    if i >= 2:
                        dve.wait_ge(*at("exp", 0, "p", (i - 2) // 2, qt))
                    V.scalar_tensor_tensor(S[qt][:, 0:nk], bank[b][:, 0:nk], Fq[:, qt, hd:hd + 1],
                                           C("causal" if qt == 0 else "zeros", 0, nk), ALU.add, ALU.add).then_inc(free[b], 1)
                    dve.wait_ge(*taken("s", 0, hd, qt))
                    V.reduce_max(a_nm[i % 4][:, 0:1], S[qt][:, 0:nk], AX, negate=True) \
                        .then_inc(*sets("neg_max", 0, "p", hd, qt))

                def finish(i):
                    hd, qt = i // 2, i % 2
                    normalize((0, "p", hd, qt), i, Pr[hd % 2][:, qt * P:(2 * qt + 1) * P]) \
                        .then_inc(*sets("probs", 0, "p", hd, qt))

                for i in range(2 * NH):
                    scores(i)
                    if i >= 2:
                        finish(i - 2)
                    if i % 2 and i >= 3:
                        keys_out(0, 0, [i // 2 - 1])
                finish(2 * NH - 2)
                finish(2 * NH - 1)
                keys_out(0, 0, [NH - 1])
                for hf in range(2):
                    if hf:
                        keys_out(0, 1, range(8))
                    for g in (2 * hf, 2 * hf + 1):
                        b = take("ss", 0, g)
                        i = 2 * NH + g
                        new = bank[b][:, PAST:T]
                        step(V.tensor_tensor(new, new, C("new_causal", g * NSAMP, NSAMP), ALU.add))
                        V.reduce_max(a_nm[i % 4][:, 0:1], bank[b][:, 0:T], AX, negate=True) \
                            .then_inc(*sets("neg_max", 0, "s", g))
                    for g in (2 * hf, 2 * hf + 1):
                        normalize((0, "s", g), 2 * NH + g, Pr[g % 2][:, 0:T]).then_inc(*sets("probs", 0, "s", g))
                        freed(banks.of("ss", 0, g)[0])

            def stick(i, bkey, ukey, n, probs, masked, mask):
                b, use = banks.of(*bkey)
                dve.wait_ge(*at("log1p", *ukey))
                Sn, Ln = S[i % 2][:, 0:n], L[i % 2][:, 0:n]
                step(V.scalar_tensor_tensor(Sn, bank[b][:, 0:n], 0.0, Ln, ALU.max, ALU.add))
                m = Sn[:, masked:n]
                V.scalar_tensor_tensor(Ln, bank[b][:, 0:n], 0.0, Ln, ALU.min, ALU.subtract).then_inc(free[b], 1)
                step(V.tensor_tensor(m, m, mask, ALU.mult))
                step(V.tensor_tensor_scan(probs, Sn, Sn, 0.0, ALU.add, ALU.bypass))
                step(V.tensor_tensor(Ln, Ln, probs, ALU.add))
                V.tensor_scalar(a_nm[i % 4][:, 0:1], probs[:, n - 1:n], -1.0, None, ALU.mult) \
                    .then_inc(*sets("log_a", *ukey))

            def stick_finish(ukey, probs, masked, mask, key):
                dve.wait_ge(*at("stick_exp", *ukey))
                m = probs[:, masked:]
                V.tensor_tensor(m, m, mask, ALU.mult).then_inc(*sets("probs", 1, *key))

            def stick_attention():
                strict2 = view(C("strict"), 0, [[0, 2], [1, P]])

                def diagonal(a384):
                    return view(a384, 0, [[2 * P, 2], [1, P]])

                def log_weights(pair):
                    heads = (2 * pair, 2 * pair + 1)
                    for hd in heads:
                        b, _use = banks.of("s", 1, hd)
                        z, Sn, Ln = bank[b][:, 0:3 * P], stick_S[hd % 4], stick_L[hd % 4]
                        dve.wait_ge(*at("log1p", hd))
                        V.scalar_tensor_tensor(Sn, z, 0.0, Ln, ALU.max, ALU.add).then_inc(*sets("softplus", hd))
                        dve.wait_ge(*at("softplus", hd))
                        V.scalar_tensor_tensor(Ln, z, 0.0, Ln, ALU.min, ALU.subtract).then_inc(free[b], 1)
                    for hd in heads:
                        m = diagonal(stick_S[hd % 4])
                        V.tensor_tensor(m, m, strict2, ALU.mult).then_inc(*sets("masked", hd))
                    for hd in heads:
                        if hd >= 4:
                            take("pt", 1, hd - 4)
                        dve.wait_ge(*at("masked", hd))
                        V.tensor_tensor_scan(stick_P[hd % 4], stick_S[hd % 4], stick_S[hd % 4], 0.0,
                                             ALU.add, ALU.bypass).then_inc(*sets("summed", hd))
                    for hd in heads:
                        dve.wait_ge(*at("summed", hd))
                        V.tensor_scalar(a_nm[hd % 4][:, 0:2], view(stick_P[hd % 4], P - 1, [[2 * P, 2]]), -1.0, None,
                                        ALU.mult)
                        V.tensor_tensor(stick_L[hd % 4], stick_L[hd % 4], stick_P[hd % 4], ALU.add) \
                            .then_inc(*sets("log_a", hd))

                def finish(pair):
                    for hd in (2 * pair, 2 * pair + 1):
                        dve.wait_ge(*at("stick_exp", hd))
                        m = diagonal(stick_P[hd % 4])
                        V.tensor_tensor(m, m, strict2, ALU.mult).then_inc(*sets("probs", 1, "p", hd))

                log_weights(0)
                for u in (UNIT["k", 1, 1], UNIT["k", 1, 2]):
                    unit_buffer_free(u + 2)
                b = take("lvar")
                step(V.memset(ln_var, 1.0))
                V.tensor_scalar(ln_var[:, 0:2], bank[b][:, 0:2], 1.0 / HALF, EPS, ALU.mult, ALU.add)
                V.tensor_scalar(ln_var[0:NSAMP, 2:3], bank[b][0:NSAMP, 2:3], 1.0 / HALF, EPS, ALU.mult, ALU.add) \
                    .then_inc(free[b], 1)
                dve.wait_ge(*taken("lvar"))
                dve.sem_inc(*sets("ln_var"))
                log_weights(1)
                dve.wait_ge(*at("ln_rs"))
                for t in range(TILES):
                    r = ROWS[t]
                    ins = V.tensor_scalar(S_t[0:r, t * P:t * P + r], ident[0:r, 0:r], ln_rs[0:r, t:t + 1], None, ALU.mult)
                ins.then_inc(*sets("ln_diag"))
                for pair in range(NH // 2):
                    finish(pair)
                    if pair + 2 < NH // 2:
                        log_weights(pair + 2)
                    keys_out(2, 0, [2 * pair, 2 * pair + 1])
                    if pair == 0:
                        b = take("lrs")
                        V.tensor_tensor(conv, conv, view(bank[b][:, :], 0, [[0, NCH], [1, T]]), ALU.mult).then_inc(free[b], 1)
                        dve.wait_ge(*taken("lrs"))
                        dve.sem_inc(*sets("scaled"))
                for hf in range(2):
                    if hf:
                        keys_out(2, 1, range(8))
                    gs = (2 * hf, 2 * hf + 1)
                    for g in gs:
                        stick(g, ("ss", 1, g), ("s", g), T, Pr[g % 2][:, 0:T], PAST, C("new_strict", g * NSAMP, NSAMP))
                    for g in gs:
                        stick_finish(("s", g), Pr[g % 2][:, 0:T], PAST, C("new_strict", g * NSAMP, NSAMP), ("s", g))

            def cross_attention(l):
                stage = 2 * l + 1
                for t in range(TILES):
                    unit(UNIT["cq", l, t])

                def scores(hd):
                    b = take("cs", l, hd)
                    V.reduce_max(a_nm[hd % 4], bank[b][:, :].rearrange("p (q k) -> p q k", q=2), AX, negate=True) \
                        .then_inc(*sets("neg_max", l, "cp", hd))

                scores(0)
                for hd in range(XH):
                    if hd + 1 < XH:
                        scores(hd + 1)
                    normalize((l, "cp", hd), hd, Pr[hd % 2], 2).then_inc(*sets("probs", l, "cp", hd))
                    freed(banks.of("cs", l, hd)[0])
                    keys_out(stage, 0, [2 * hd, 2 * hd + 1])
                for hf in range(2):
                    if hf:
                        keys_out(stage, 1, range(8))
                    b = take("css", l, hf)
                    V.reduce_max(a_nm[hf][:, 0:1], bank[b][:, 0:NMEM], AX, negate=True) \
                        .then_inc(*sets("neg_max", l, "cs", hf))
                    normalize((l, "cs", hf), hf, Pr[hf][:, 0:NMEM]).then_inc(*sets("probs", l, "cs", hf))
                    freed(b)

            def memory(l):
                to_hT(("mem", l), range(2))
                for t in range(2):
                    unit(UNIT["mk", l, t])

            dve.wait_ge(*at("ck_gain_in"))
            step(V.memset(lf[:, :], 0.0))
            step(V.memset(route[:, :], 0.0))
            step(V.memset(poolF[:, :, 0:PBUF], 0.0))
            memory(0)
            norm(0)
            to_hT(0, range(TILES))
            dve.wait_ge(*at("scaled_gain"))
            dve.wait_ge(*at("const_in"))
            dve.wait_ge(*at("table_in"))
            for n, (k, t) in enumerate(ZSEQ[0]):
                if k != "v":
                    unit(UNIT[k, 0, t])
            b = take("fl")
            for t in range(TILES):
                r = ROWS[t]
                ins = V.tensor_tensor(lf_y[0:r, t, :], bank[b][0:r, 8 * t:8 * t + 8], b_f[0:r, :], ALU.add)
            ins.then_inc(free[b], 1)
            dve.wait_ge(*taken("fl"))
            V.scalar_tensor_tensor(lf_a, lf_y, -1.0, lf_y, ALU.mult, ALU.max).then_inc(*sets("forget_abs"))
            b = take("pre")
            V.tensor_copy(view(poolF[:, 0, :], PSEG, [[PFLAT, NCH], [SSEG, NB], [1, PBUF]]),
                          view(bank[b][:, :], 0, [[120, NCH], [PBUF, NB], [1, PBUF]])).then_inc(free[b], 1)
            dve.wait_ge(*at("forget_log"))
            V.scalar_tensor_tensor(logf, lf_y, 0.0, lf_l, ALU.min, ALU.subtract).then_inc(*sets("logf"))
            dve.wait_ge(*taken("pre"))
            for u in (UNIT["k", 0, 1], UNIT["k", 0, 2]):
                unit_buffer_free(u + 2)
            for g, w in enumerate(WINDOWS):
                dve.wait_ge(*taken("p", g))
                f = poolF[:, g, :]
                src, lo = f, 0
                for i in range(g + 1):
                    dst = (S_t[:, 0:PFLAT], Pr_t[:, 0:PFLAT])[i % 2]
                    d = 1 << i
                    step(V.tensor_tensor(dst[:, lo + d:], src[:, lo + d:], src[:, lo:PFLAT - d], ALU.add))
                    src, lo = dst, lo + d
                if g >= 2:
                    take("pm", g - 2)
                out = L_t[:, (g % 2) * T:(g % 2 + 1) * T]
                new = lambda q: view(q, PSEG + PBUF, [[SSEG, NB], [1, NS]])
                V.scalar_tensor_tensor(out[:, SEQ:T].rearrange("p (b s) -> p b s", b=NB), new(src), 1.0 / w, new(f),
                                       ALU.mult, ALU.subtract)
                V.scalar_tensor_tensor(out[:, 16:SEQ], src[:, PBUF + 16:PSEG], 1.0 / w, f[:, PBUF + 16:PSEG],
                                       ALU.mult, ALU.subtract)
                step(V.tensor_tensor(out[:, 0:16], src[:, PBUF:PBUF + 16], C("inv_count", 16 * g, 16), ALU.mult))
                V.tensor_tensor(out[:, 0:16], out[:, 0:16], f[:, PBUF:PBUF + 16], ALU.subtract) \
                    .then_inc(*sets("pool_d", g))
                dve.wait_ge(*at("pool_d", g))
            b = take("Fq")
            V.tensor_copy(Fq, bank[b][:, 0:16].rearrange("p (t h) -> p t h", t=2)).then_inc(free[b], 1)
            dve.wait_ge(*taken("Fq"))
            forget_attention()
            residual("wo", 0, 1)
            norm(1)
            to_hT(1, range(TILES))
            cross_attention(0)
            residual("wc", 0, 2)
            norm(2)
            to_hT(2, range(TILES))

            def ffn_mul(f2, ff):
                dve.wait_ge(ffn_up, ff + 1)
                dve.wait_ge(ffn_silu, ff + 1)
                V.tensor_tensor(ffn_hid[f2], ffn_s[f2], bank[7][:, 0:T], ALU.mult).then_inc(ffn_h, 1)

            for f2 in range(2):
                ffn_mul(f2, f2)
            with dve.Fori(1, FBLK) as i:
                for f2 in range(2):
                    dve.wait_ge(ffn_down, i * 2 + (f2 - 1))
                    ffn_mul(f2, i * 2 + f2)
            dve.wait_ge(ffn_down, 2 * FBLK)
            for hf in range(2):
                for t in range(TILES):
                    xs = x[0:ROWS[t], t, hf * HALF:(hf + 1) * HALF]
                    V.tensor_tensor(xs, xs, bank[3 * hf + t][0:ROWS[t], :], ALU.add).then_inc(*sets("ffn_out", hf, t))
            for t in range(TILES):
                dve.wait_ge(*at("ffn_out", 1, t))
                dve.sem_inc(*sets("x", 3, t))

            memory(1)
            norm(3)
            to_hT(3, range(TILES))
            step(V.memset(convF[:, :, 0:CBUF], 0.0))
            for n in range(2):
                b = take("cpre", n)
                V.tensor_copy(view(convF[:, 0, :], CSEG + 4 * n * DSEG, [[CFLAT, NCH], [DSEG, 4], [1, CBUF]]),
                              view(bank[b][:, :], 0, [[120, NCH], [CBUF, 4], [1, CBUF]])).then_inc(free[b], 1)
            for c in range(NCH):
                dve.wait_ge(*taken("g", c))
                b = take("a", c)
                V.tensor_tensor(convF[:, c, CBUF:CSEG], bank[b][:, 0:SEQ], S[c % 2][:, 0:SEQ], ALU.mult)
                V.tensor_tensor(conv_new[:, c, :], bank[b][:, SEQ:T], S[c % 2][:, SEQ:T], ALU.mult)
                V.tensor_tensor(view(convF[:, c, :], CSEG + CBUF, [[DSEG, NB], [1, NS]]),
                                view(bank[b][:, :], SEQ, [[NS, NB], [1, NS]]),
                                S[c % 2][:, SEQ:T].rearrange("p (b s) -> p b s", b=NB), ALU.mult).then_inc(free[b], 1)
            for n in range(2):
                dve.wait_ge(*taken("cpre", n))
            order = [UNIT[k, 1, t] for k, t in ZSEQ[1] if k != "v"]
            for c in range(NCH):
                dve.wait_ge(*taken("a", c))
                accp = conv[:, c, 0:SEQ]
                inp = lambda j: view(convF[:, c, :], j, [[1, SEQ]])
                V.tensor_scalar(accp, inp(0), cw[:, 0, c:c + 1], chan[:, 1, c:c + 1], ALU.mult, ALU.add) \
                    .then_inc(conv_p, 1)
                for j in range(1, CW):
                    dve.wait_ge(conv_p, c * CW + j)
                    V.scalar_tensor_tensor(accp, inp(j), cw[:, j, c:c + 1], accp, ALU.mult, ALU.add) \
                        .then_inc(conv_p, 1)
                for u in order[2 * c:2 * c + 2]:
                    unit(u)
                dve.wait_ge(*at("taps", c))
                V.tensor_reduce(conv[:, c, SEQ:T], taps.rearrange("p (t j) -> p t j", j=CW), AX, ALU.add) \
                    .then_inc(conv_s, 1)
                dve.wait_ge(conv_s, c + 1)
                V.tensor_scalar(conv[:, c, SEQ:T], conv[:, c, SEQ:T], chan[:, 1, c:c + 1], None, ALU.add) \
                    .then_inc(*sets("conv_bias", c))
            dve.wait_ge(*at("conv_bias", NCH - 1))
            dve.wait_ge(conv_p, NCH * CW)
            dve.sem_inc(*sets("conv"))
            b = take("lmean")
            V.scalar_tensor_tensor(conv, view(bank[b][:, :], 0, [[0, NCH], [1, T]]), -1.0 / HALF, conv, ALU.mult, ALU.add).then_inc(free[b], 1)
            dve.wait_ge(*taken("lmean"))
            dve.sem_inc(*sets("cent"))
            stick_attention()
            residual("wo", 1, 4)
            norm(4)
            to_hT(4, range(TILES))
            cross_attention(1)
            residual("wc", 1, 5)
            norm(5)
            to_hT(5, range(TILES))

            b = take("rt")
            for t in range(TILES):
                r = ROWS[t]
                ins = V.tensor_tensor(lg[0:r, t, :], bank[b][0:r, 8 * t:8 * t + 8], b_r[0:r, :], ALU.add)
            ins.then_inc(free[b], 1)
            dve.wait_ge(*taken("rt"))
            for t in range(TILES):
                ins = V.max(m8[:, t, :], lg[:, t, :])
            step(ins)
            for t in range(TILES):
                ins = V.max_index(idx[:, t, :], m8[:, t, :], lg[:, t, :])
            step(ins)
            V.tensor_tensor(gw[:, :, 0:1], m8[:, :, 1:2], m8[:, :, 0:1], ALU.subtract).then_inc(*sets("gap"))
            step(V.tensor_copy(idxf, idx))
            iota8 = view(C("iota"), 0, [[0, 3], [1, NE]])
            V.tensor_tensor(pk1, iota8, view(idxf[:, 0, :], 0, [[8, 3], [0, NE]]), ALU.is_equal)
            step(V.tensor_tensor(pk2, iota8, view(idxf[:, 0, :], 1, [[8, 3], [0, NE]]), ALU.is_equal))
            V.tensor_tensor(picked, pk1, pk2, ALU.add).then_inc(*sets("picked"))
            dve.wait_ge(*at("gap_exp"))
            step(V.tensor_scalar(gw[:, :, 2:3], gw[:, :, 1:2], 1.0, None, ALU.add))
            step(V.reciprocal(gw[:, :, 3:4], gw[:, :, 2:3]))
            step(V.tensor_tensor(gw[:, :, 4:5], gw[:, :, 3:4], gw[:, :, 1:2], ALU.mult))
            step(V.tensor_tensor(pk1, pk1, view(gw[:, 0, :], 3, [[8, 3], [0, NE]]), ALU.mult))
            step(V.tensor_tensor(pk2, pk2, view(gw[:, 0, :], 4, [[8, 3], [0, NE]]), ALU.mult))
            step(V.tensor_tensor(gates, pk1, pk2, ALU.add))
            b = take("rank")
            FAR = 1048576.0
            for t in range(TILES):
                r = ROWS[t]
                ins = V.scalar_tensor_tensor(posr[0:r, t, :], bank[b][0:r, 8 * t:8 * t + 8], FAR, picked[0:r, t, :],
                                             ALU.add, ALU.mult)
            step(ins)
            step(V.tensor_scalar(posr, posr, -FAR, None, ALU.add))
            V.reduce_max(cmax, bank[b][:, 24:32], AX).then_inc(free[b], 1)
            dve.wait_ge(*taken("rank"))
            V.tensor_copy(cmax_i[:, :], cmax).then_inc(*sets("cmax"))
            dve.wait_ge(*at("cmax"))

            def add_scattered(i, scattered, n, done):
                t, hf = i // 2, i % 2
                dve.wait_ge(scattered, n)
                xs = x[0:ROWS[t], t, hf * HALF:(hf + 1) * HALF]
                V.tensor_tensor(xs, xs, bank[6 + i % 2][0:ROWS[t], :], ALU.add).then_inc(done, 1)

            def expert(n, e):
                dve.wait_ge(moe_gathered, n * 2)
                dve.wait_ge(moe_GTr, n)
                V.tensor_copy(rcol[:, 0:3], posr[:, :, bass.ds(e, 1)].rearrange("p t e -> p (t e)")) \
                    .then_inc(moe_col, 1)
                V.tensor_copy(rcol[:, 3:6], gates[:, :, bass.ds(e, 1)].rearrange("p t e -> p (t e)")) \
                    .then_inc(moe_col, 1)
                dve.wait_ge(moe_col, n * 2 + 2)
                for t in range(TILES):
                    r = ROWS[t]
                    V.tensor_scalar(moe_G[0:r, t, :], C("iota")[0:r], rcol[0:r, t:t + 1], rcol[0:r, 3 + t:4 + t],
                                    ALU.is_equal, ALU.mult)
                for t in range(TILES):
                    r = ROWS[t]
                    ins = V.tensor_scalar(moe_P[0:r, t, :], C("iota")[0:r], rcol[0:r, t:t + 1], None, ALU.is_equal)
                ins.then_inc(moe_sel, 1)

                def weights_lo(b):
                    for i in (2 * b, 2 * b + 1):
                        dve.wait_ge(moe_hi, n * NPIECE + (i + 1))
                        V.tensor_tensor(low[i % PRING], raw[i % PRING], high[i % PRING].bitcast(F32), ALU.subtract) \
                            .then_inc(moe_lo, 1)

                def hidden(j):
                    dve.wait_ge(*used(n, 1, j))
                    dve.wait_ge(moe_silu, n * STAGES + (j + 1))
                    dve.wait_ge(moe_tr, n * STAGES + max(j - 1, 0))
                    V.tensor_tensor(moe_hid[j % 2], moe_sg[j % 2], bank[2 + j % 2][:, :], ALU.mult) \
                        .then_inc(moe_h, 1)

                def hidden_lo(j):
                    dve.wait_ge(moe_hThi, n * STAGES + (j + 1))
                    V.tensor_tensor(moe_hidT[1], bank[6][:, :], moe_hidT[0].bitcast(F32), ALU.subtract) \
                        .then_inc(moe_hT, 1)

                def add_last(pieces):
                    for i in pieces:
                        dve.wait_ge(moe_added, n * 6)
                        add_scattered(i, moe_scattered, n * 6 + (i + 1), moe_added)

                weights_lo(0)
                for half in range(2):
                    dve.wait_ge(moe_xhi, n * 2 + (half + 1))
                    V.tensor_tensor(moe_x[1][:, 4 * half:4 * half + 4, :], bank[7][:, :].rearrange("p (k c) -> p k c", k=4),
                                    moe_x[0][:, 4 * half:4 * half + 4, :].bitcast(F32), ALU.subtract) \
                        .then_inc(moe_xT, 1)
                weights_lo(1)
                for b, (m, j) in enumerate(PRODUCTS):
                    if b + 2 < len(PRODUCTS):
                        weights_lo(b + 2)
                    if m == 0 and j < 2:
                        add_last((0, 1) if j == 0 else (4, 5))
                    if m == 0 and j:
                        hidden_lo(j - 1)
                    if m == 1:
                        hidden(j)
                        if j == 0:
                            add_last((2, 3))
                    if m == 2 and j == 0:
                        dve.wait_ge(moe_GTr, n + 1)
                        V.tensor_copy(moe_GT[:, 0:T], bank[7][:, 0:T]).then_inc(moe_GTc, 1)
                hidden_lo(STAGES - 1)

            def expert_round(r):
                V.memset(moe_GT, 0.0).then_inc(moe_cleared, 1)
                V.memset(moe_y, 0.0).then_inc(moe_cleared, 1)
                dve.wait_ge(moe_cleared, r * 2 + 2)
                dve.sem_inc(moe_zero, 1)
                with dve.Fori(0, NE) as e:
                    expert(e + r * NE, e)
                dve.wait_ge(moe_added, (r + 1) * NE * 6)
                for i in range(6):
                    add_scattered(i, moe_scatteredE, r * 6 + (i + 1), moe_addedE)
                dve.wait_ge(moe_addedE, (r + 1) * 6)

            expert_round(0)
            most = dve.value_load(cmax_i[0:1, 0:1])
            with dve.If(most > CAP):
                with dve.Fori(1, ROUNDS) as r:
                    V.tensor_scalar(posr, posr, float(-CAP), None, ALU.add).then_inc(moe_shift, 1)
                    dve.wait_ge(moe_shift, r)
                    expert_round(r)
            dve.sem_inc(*sets("x_final"))
        out = {"marks": marks.table, "banks": banks.table, "releases": released}
    return out


OUTPUTS = (
    ("y_prompt", (1, SEQ, D)), ("y_sample", (NB, NS, D)),
    ("fox_k_p", (1, 1, SEQ, NH, HD)), ("fox_v_p", (1, 1, SEQ, NH, HD)), ("fox_logf_p", (1, 1, SEQ, NH)),
    ("sb_k_p", (1, 1, SEQ, NH, HD)), ("sb_v_p", (1, 1, SEQ, NH, HD)),
    ("pool_p", (1, 1, PBUF, HALF)), ("conv_p", (1, 1, CBUF, HALF)),
    ("mem_k_p", (2, 1, NMEM, XH, XHD)), ("mem_v_p", (2, 1, NMEM, XH, XHD)),
    ("fox_k_s", (1, NB, NS, NH, HD)), ("fox_v_s", (1, NB, NS, NH, HD)), ("fox_logf_s", (1, NB, NS, NH)),
    ("sb_k_s", (1, NB, NS, NH, HD)), ("sb_v_s", (1, NB, NS, NH, HD)),
    ("pool_s", (1, NB, PBUF, HALF)), ("conv_s", (1, NB, CBUF, HALF)),
)


def kernel(**inputs):
    import numpy as _np
    import concourse.bacc as _bacc
    from concourse import mybir as _mybir
    from concourse.bass_utils import run_bass_kernel_spmd as _run

    arrays = {f"in_{name}": _np.ascontiguousarray(x) for name, x in inputs.items()}
    arrays["in_const_table"] = constants()[0]
    known = {}
    for _ in range(2):
        nc = _bacc.Bacc("TRN2", target_bir_lowering=False, num_devices=1)
        a = {n[3:]: nc.dram_tensor(n, x.shape, _mybir.dt.from_np(x.dtype), kind="ExternalInput").ap()
             for n, x in arrays.items()}
        o = {n: nc.dram_tensor("out_" + n, shape, _mybir.dt.float32, kind="ExternalOutput").ap()
             for n, shape in OUTPUTS}
        known = decoder_step(nc, a, o, known)
    r = _run(nc, [arrays], core_ids=[0])
    return tuple(r.results[0]["out_" + n] for n, _ in OUTPUTS)
```

```python
from contextlib import ExitStack

import concourse.bass as bass
from concourse import mybir
import numpy as np

F32 = mybir.dt.float32
I32 = mybir.dt.int32
U32 = mybir.dt.uint32
F32R = mybir.dt.float32r
ALU = mybir.AluOpType
ACT = mybir.ActivationFunctionType
AX = mybir.AxisListType.X

P = 128
D = 1024
KD = D // P
SEQ = 256
NB, NS = 8, 8
PAST = 256
NPG = 2
HALF = 512
NH, HD = 8, 64
NCH = HALF // P
XH, XHD = 4, 128
NMEM = 256
DFF = 2816
NE = 8
DFE = 3584
EPS = 1e-6
WINDOWS = (2, 4, 8, 16)
PBUF = 15
CW = 31
CBUF = 30
NSAMP = NB * NS
T = SEQ + NSAMP
TILES = 3
ROWS = (P, P, NSAMP)
RING = 3
SLOT = 4096
XSLOTS = 7
FB = 512
STAGES = DFE // FB
AHEAD = (range(0, 5), range(5, 7), range(7, 8))
PRODUCTS = [(0, 0), (1, 0)] + [b for j in range(1, STAGES) for b in ((0, j), (1, j), (2, j - 1))] + [(2, STAGES - 1)]
PIECES = [(m, j, q) for m, j in PRODUCTS for q in range(2)]
NPIECE = len(PIECES)
PIECE = SLOT // 2
POOLED = [i for i, (m, j, q) in enumerate(PIECES) if m == 2 and q == 1]
PRING = 7
CAP = P
ROUNDS = -(-T // CAP)
NEG = -1e30
PSEG = PBUF + SEQ
SSEG = PBUF + NS
PFLAT = PSEG + NB * SSEG
CSEG = CBUF + SEQ
DSEG = CBUF + NS
CFLAT = CSEG + NB * DSEG


def constants():
    i, j = np.arange(P)[:, None], np.arange(P)[None, :]
    rb, rs = (np.arange(P) // 64)[:, None], (np.arange(P) % NS)[:, None]
    nb, ns = (np.arange(NSAMP) // NS), (np.arange(NSAMP) % NS)
    upto = (i <= j).astype(np.float32)
    one = np.ones((P, P), np.float32)
    own = [(nb[None, :] == 2 * g + rb) for g in range(4)]
    pad = lambda a: np.concatenate([a, np.zeros((P - a.shape[0], a.shape[1]), a.dtype)])
    parts = {
        "ident": np.eye(P, dtype=np.float32),
        "minus_half": np.full((P, 1), -0.5, np.float32),
        "upto": upto,
        "before": (i < j).astype(np.float32),
        "neg_upto": np.concatenate([-upto, -one], 1),
        "ones": one,
        "after": (i > j).astype(np.float32),
        "zeros": 0 * one,
        "causal": np.where(j <= i, 0, NEG).astype(np.float32),
        "new_upto": pad(-((nb[:, None] == nb[None, :]) & (ns[:, None] <= ns[None, :])).astype(np.float32)),
        "own_upto": pad(np.concatenate([((nb[:, None] == 2 * g + b) & (ns[:, None] <= np.arange(NS)[None, :]))
                                        for g in range(4) for b in range(2)], 1).astype(np.float32)),
        "own": pad(np.concatenate([(nb[:, None] == 2 * g + b) for g in range(4) for b in range(2)], 1)
                   .astype(np.float32)),
        "strict": (j < i).astype(np.float32),
        "new_causal": np.concatenate([np.where(o & (ns[None, :] <= rs), 0, NEG) for o in own], 1)
                        .astype(np.float32),
        "new_strict": np.concatenate([(o & (ns[None, :] < rs)) for o in own], 1).astype(np.float32),
        "inv_count": np.tile(np.concatenate([1.0 / np.minimum(np.arange(16) + 1, w) for w in WINDOWS])
                             .astype(np.float32), (P, 1)),
        "iota": np.tile(np.arange(P, dtype=np.float32), (P, 1)),
    }
    at, n = {}, 0
    for name, a in parts.items():
        at[name] = (n, a.shape[1])
        n += a.shape[1]
    return np.concatenate(list(parts.values()), 1).astype(np.float32), at


class Marks:

    def __init__(self, nc, ctx, known):
        self.nc, self.ctx, self.known = nc, ctx, known
        self.sems, self.table, self.count = {}, {}, {}

    def sem(self, name):
        if name not in self.sems:
            self.sems[name] = self.ctx.enter_context(self.nc.semaphore("m_" + name))
        return self.sems[name]

    def sets(self, name, *index, by=1):
        self.count[name] = self.count.get(name, 0) + by
        self.table[(name, *index)] = self.count[name]
        return self.sem(name), by

    def at(self, name, *index):
        return self.sem(name), self.known.get((name, *index), 1)

    def has(self, name, *index):
        return (name, *index) in self.known


class Banks:

    def __init__(self, known):
        self.known, self.table, self.n = known, {}, 0

    def open(self, *key):
        b, use = self.n % 8, self.n // 8
        self.n += 1
        self.table[key] = (b, use + 1)
        return b, use

    def of(self, *key):
        return self.known.get(key, (0, 1))

    def uses(self, b):
        return (self.n - b + 7) // 8


def units():
    out = []
    for l in range(2):
        out += [("mk", l, t) for t in range(2)]
        out += [(k, l, t) for k in ("q", "k") for t in range(TILES)]
        out += [("cq", l, t) for t in range(TILES)]
    return out


UNITS = units()
UNIT = {u: n for n, u in enumerate(UNITS)}


def decoder_step(nc, a, o, known):
    ctx = ExitStack()
    with ctx:
        marks = Marks(nc, ctx, known.get("marks", {}))
        banks = Banks(known.get("banks", {}))
        releases = known.get("releases", {})
        released = {}
        sets, at = marks.sets, marks.at

        at_byte, width = {}, {}

        def sb(name, cols, dt=F32):
            at_byte[name], width[name] = -(-nc.sbuf_base // 32) * 32, cols
            return ctx.enter_context(nc.sbuf_tensor(name, [P, cols], dt))

        def rounded(name):
            return nc.alloc_sbuf_tensor_at(name + "_r", [P, width[name]], F32R, offset=at_byte[name])

        def sem(name):
            return ctx.enter_context(nc.semaphore(name))

        small_ring = sb("small_ring", RING * SLOT)
        big = sb("big", (XSLOTS - RING) * SLOT)
        slots = [small_ring[:, s * SLOT:(s + 1) * SLOT] for s in range(RING)]
        slots += [big[:, s * SLOT:(s + 1) * SLOT] for s in range(XSLOTS - RING)]
        kT = big[:, 0:4096].rearrange("p (c b k) -> p c b k", c=NCH, b=4)
        vC = big[:, 4096:8192].rearrange("p (b g c) -> p b g c", b=4, g=NPG)
        qbd = big[:, 8192:12288]
        knat = big[:, 12288:14336].rearrange("p (s c) -> p s c", s=4)
        lb = big[:, 14336:16384].rearrange("p (b g c) -> p b g c", b=NB, g=NPG)

        x = sb("x", TILES * D)[:, :].rearrange("p (t d) -> p t d", t=TILES)
        hbuf = sb("h", TILES * D)
        h = hbuf[:, :].rearrange("p (t d) -> p t d", t=TILES)
        yT = hbuf[:, 0:8 * T].rearrange("p (c t) -> p c t", c=8)
        mem = hbuf[:, 0:2 * D].rearrange("p (t d) -> p t d", t=2)
        hTbuf = sb("hT", KD * T)
        hT = hTbuf[:, :].rearrange("p (c t) -> p c t", c=KD)
        lr = hTbuf[:, 0:2048].rearrange("p (t h c) -> p t h c", t=2, h=NH)
        poolF = big[:, 0:NCH * PFLAT].rearrange("p (c t) -> p c t", c=NCH)
        pool_new = big[:, NCH * PFLAT:NCH * (PFLAT + NSAMP)].rearrange("p (c t) -> p c t", c=NCH)
        conv_at = 4096
        conv = big[:, conv_at:conv_at + NCH * T].rearrange("p (c t) -> p c t", c=NCH)
        convF = big[:, conv_at + NCH * T:conv_at + NCH * (T + CFLAT)].rearrange("p (c t) -> p c t", c=NCH)
        conv_new = big[:, conv_at + NCH * (T + CFLAT):conv_at + NCH * (T + CFLAT + NSAMP)] \
            .rearrange("p (c t) -> p c t", c=NCH)
        taps = hbuf[:, 0:NSAMP * CW]
        squares = big[:, conv_at + NCH * T:conv_at + 2 * NCH * T].rearrange("p (c t) -> p c t", c=NCH)
        qz_t = sb("qz", NCH * 2 * SEQ)
        qz = qz_t[:, :].rearrange("p (c z t) -> p c z t", c=NCH, z=2)
        kN_t = sb("kN", NCH * T)
        kN = kN_t[:, :].rearrange("p (c t) -> p c t", c=NCH)
        v_t = sb("v", TILES * HALF)
        v = v_t[:, :].rearrange("p (t c) -> p t c", t=TILES)
        kM_t = sb("kM", XH * NMEM)
        kM = kM_t[:, :].rearrange("p (c t) -> p c t", c=XH)
        vM_t = sb("vM", 2 * HALF)
        vM = vM_t[:, :].rearrange("p (t c) -> p t c", t=2)
        S_t = sb("S", 640)
        L_t = sb("L", 640)
        Pr_t = sb("Pr", 1024)
        PT_t = sb("PT", 1024)
        stick_S = [hTbuf[:, 384 * i:384 * i + 384] for i in range(4)]
        stick_L = [big[:, 14336 + 384 * i:14336 + 384 * i + 384] for i in range(4)]
        stick_P = [Pr_t[:, 0:384], Pr_t[:, 512:896], hTbuf[:, 1536:1920], hTbuf[:, 1920:2304]]
        S = [S_t[:, 0:320], S_t[:, 320:640]]
        L = [L_t[:, 0:320], L_t[:, 320:640]]
        Pr = [Pr_t[:, 0:512], Pr_t[:, 512:1024]]
        PT = [PT_t[:, 0:512], PT_t[:, 512:1024]]
        osam = [hbuf[:, 8 * T:8 * T + 512], S_t[:, 0:512]]
        nbuf = [S_t[:, 0:512], L_t[:, 0:512]]
        gain = sb("gain", D)
        ctab, cat = constants()
        cbuf = sb("consts", ctab.shape[1])

        def C(name, lo=0, n=None):
            s, w = cat[name]
            return cbuf[:, s + lo:s + lo + (w - lo if n is None else n)]

        ident = C("ident")
        hg = sb("hg", 2 * (2 * HD + 2 * XHD))
        g_fq, g_fk = hg[:, 0:64], hg[:, 64:128]
        g_cq = [hg[:, 128:256], hg[:, 256:384]]
        hg2 = sb("hg2", XHD)
        g_ck = [hg[:, 384:512], hg2[:, :]]
        bf8 = sb("bf8", 2 * NH)
        b_f, b_r = bf8[:, 0:8], bf8[:, 8:16]
        wfl = sb("wfl", KD * NH)[:, :].rearrange("p (k n) -> p k n", k=KD)
        wrt = sb("wrt", KD * NE)[:, :].rearrange("p (k n) -> p k n", k=KD)
        wpg = sb("wpg", NCH * P)[:, :].rearrange("p (g n) -> p g n", g=NCH)
        chan_t = sb("chan", (4 + CW) * NCH)
        chan = chan_t[:, :].rearrange("p (c n) -> p n c", c=NCH)
        cw = chan[:, 4:4 + CW, :]
        pt = sb("pt", 16, I32)
        lf = sb("lf", 6 * 8)
        lf_y = lf[:, 0:24].rearrange("p (t h) -> p t h", t=3)
        logf = lf[:, 24:48].rearrange("p (t h) -> p t h", t=3)
        lfw = sb("lfw", 3 * 24)
        lf_a, lf_e, lf_l = (lfw[:, 24 * i:24 * i + 24].rearrange("p (t h) -> p t h", t=3) for i in range(3))
        lfp = sb("lfp", 16 * 8)[:, :].rearrange("p (b g h) -> p b g h", b=NB, g=NPG)
        Fq = sb("Fq", 16)[:, :].rearrange("p (t h) -> p t h", t=2)
        ln1_t = gain[:, 0:512]
        ln2_t = gain[:, 512:1024]
        route = sb("route", 9 * 24 + 24)
        lg, m8, pk1, pk2, picked, gates, posr = (route[:, 24 * i:24 * i + 24].rearrange("p (t e) -> p t e", t=3)
                                                 for i in range(7))
        idx = sb("idx", 24, U32)[:, :].rearrange("p (t e) -> p t e", t=3)
        idxf = route[:, 168:192].rearrange("p (t e) -> p t e", t=3)
        gw = route[:, 192:216].rearrange("p (t e) -> p t e", t=3)
        rcol = route[:, 216:222]
        cmax = route[:, 222:223]
        cmax_i = sb("cmax_i", 1, I32)
        ffn_s, ffn_hid = S, L
        ring_r, big_r, hT_r, Pr_r, PT_r = (rounded(n) for n in ("small_ring", "big", "hT", "Pr", "PT"))
        moe_x = [t[:, 0:1024].rearrange("p (k c) -> p k c", k=KD) for t in (hT_r, rounded("kM"))]
        moe_P = hTbuf[:, 1024:1408].rearrange("p (t c) -> p t c", t=3)
        moe_G = hTbuf[:, 1408:1792].rearrange("p (t c) -> p t c", t=3)
        moe_GT = hTbuf[:, 1792:2176]
        moe_y = qz_t[:, 0:1024]
        moe_hid = [qz_t[:, 1024:1536], qz_t[:, 1536:2048]]
        moe_sg = Pr
        gu_raw = [small_ring[:, (1 + b) * SLOT:(2 + b) * SLOT] for b in range(2)]
        gu_low = [ring_r[:, (1 + b) * SLOT:(2 + b) * SLOT] for b in range(2)]
        gu_high = [big_r[:, (2 + b) * SLOT:(3 + b) * SLOT] for b in range(2)]
        dn_raw = [big[:, b * SLOT:b * SLOT + PIECE] for b in range(2)]
        dn_low = [big_r[:, b * SLOT:b * SLOT + PIECE] for b in range(2)]
        dn_high = [big_r[:, b * SLOT + PIECE:(b + 1) * SLOT] for b in range(2)]
        ffn_x = hT_r[:, :].rearrange("p (k t) -> p k t", k=KD)
        ffn_xlo = [t[:, 0:4 * T].rearrange("p (k t) -> p k t", k=4) for t in (rounded("kN"), rounded("v"))]
        ffn_hhi = [Pr_r[:, 512 * i:512 * i + T] for i in range(2)]
        ffn_hlo = [PT_r[:, 512 * i:512 * i + T] for i in range(2)]
        moe_hidT = [PT_r[:, 0:512], PT_r[:, 512:1024]]

        def pieces_of(small, large):
            return [(small if s < RING else large)[:, (s % RING if s < RING else s - RING) * SLOT + q * PIECE:][:, 0:PIECE]
                    for s in (0, 1, 3, 4, 5, 6, 2) for q in range(2)]

        raw = pieces_of(small_ring, big)[:PRING]
        low = pieces_of(ring_r, big_r)[:PRING]
        high = pieces_of(ring_r, big_r)[PRING:]
        nst = sb("nst", 4 * TILES)
        n_ss, n_ms, n_rs = (nst[:, TILES * i:TILES * i + TILES] for i in range(3))
        lnst = sb("lnst", 2 * TILES)
        ln_var, ln_rs = lnst[:, 0:TILES], lnst[:, TILES:2 * TILES]
        ust = sb("ust", 2 * 24)
        u_ss = [ust[:, 24 * i:24 * i + 8] for i in range(2)]
        u_ms = [ust[:, 24 * i + 8:24 * i + 16] for i in range(2)]
        u_rs = [ust[:, 24 * i + 16:24 * i + 24] for i in range(2)]
        ast = sb("ast", 4 * 6)
        a_nm = [ast[:, 6 * i:6 * i + 2] for i in range(4)]
        a_sm = [ast[:, 6 * i + 2:6 * i + 4] for i in range(4)]
        a_rc = [ast[:, 6 * i + 4:6 * i + 6] for i in range(4)]

        bank = [ctx.enter_context(nc.psum_tensor(f"bank{b}", [P, 512], F32)) for b in range(8)]
        full = [sem(f"bank{b}_full") for b in range(8)]
        free = [sem(f"bank{b}_free") for b in range(8)]
        raw_full = [sem(f"raw{s}_full") for s in range(PRING)]
        moe_hi, moe_lo, moe_lo_pool, moe_used, moe_xhi, moe_hThi = (sem("moe_" + n) for n in (
            "weights_hi", "weights_lo", "weights_lo_pool", "weights_used", "tokens_hi", "hiddenT_hi"))
        slot_full = [sem(f"slot{s}_full") for s in range(XSLOTS)]
        knat_full = [sem(f"knat{s}_full") for s in range(4)]
        ffn_gate, ffn_up, ffn_silu, ffn_h, ffn_down, ffn_whi, ffn_wlo, ffn_hsplit, ffn_hlo_ready = (
            sem("ffn_" + n) for n in ("gate", "up", "silu", "hidden", "down", "weights_hi", "weights_lo",
                                      "hidden_hi", "hidden_lo"))
        (moe_sel, moe_gathered, moe_xT, moe_silu, moe_h, moe_tr, moe_hT, moe_yc,
         moe_scattered, moe_added, moe_GTr, moe_GTc, moe_zero, moe_scatteredE, moe_addedE) = (
            sem("moe_" + n) for n in (
                "selection", "gathered", "tokensT", "silu", "hidden", "transposed", "hiddenT", "output",
                "scattered", "added", "gatesT_psum", "gatesT", "zeroed", "scattered_last",
                "added_last"))
        moe_col, moe_cleared, moe_shift = sem("moe_columns"), sem("moe_cleared"), sem("moe_shifted")
        conv_p, conv_s = sem("conv_prompt_tap"), sem("conv_sample_sum")

        def primed(s, value):
            return s, value + 1

        prime = {"pe": (moe_used, moe_tr, moe_gathered, moe_GTr), "act": (moe_silu, moe_yc),
                 "dve": (moe_GTc, moe_xT, moe_h, moe_hT, moe_added)}

        def lo_parts(n, i):
            mine = i % NPIECE in POOLED
            rank = sum((p_ in POOLED) == mine for p_ in range(i % NPIECE))
            per = len(POOLED) if mine else NPIECE - len(POOLED)
            return moe_lo_pool if mine else moe_lo, n * per + (i // NPIECE * per + rank + 1)

        def used(n, m, j):
            return primed(moe_used, n * NPIECE + (2 * PRODUCTS.index((m, j)) + 2))

        def taken(*key):
            b, use = banks.of(*key)
            return free[b], use

        def view(ap, offset, dims):
            return bass.AP(ap.tensor, ap.offset + offset, [list(ap.ap[0])] + dims)

        def spread(src):
            return bass.AP(src.tensor, src.offset, [[0, P]] + [list(d) for d in src.ap])

        def w_stream():
            for l in range(2):
                yield ("ck", l), a["w_ck"][l].rearrange("(k p) n -> p k n", p=P)
                yield ("cv", l), a["w_cv"][l].rearrange("(k p) n -> p k n", p=P)
                w = a["w_in_e" if l == 0 else "w_in_o"][0].rearrange("(k p) n -> p k n", p=P)
                for n, name in ((1, "q"), (2, "k"), (3, "v"), (0, "p")) if l == 0 else \
                        ((0, "a"), (1, "g"), (2, "q"), (3, "k"), (4, "v")):
                    yield (name, l), w[:, :, n * HALF:(n + 1) * HALF]
                w = a["w_out_e" if l == 0 else "w_out_o"][0].rearrange("(k p) n -> p k n", p=P)
                for hf in range(2):
                    yield ("wo", l, hf), w[:, :, hf * HALF:(hf + 1) * HALF]
                yield ("cq", l), a["w_cq"][l].rearrange("(k p) n -> p k n", p=P)
                yield ("co", l), a["w_co"][l].rearrange("(k p) n -> p k n", p=P)

        stream = list(w_stream())
        place = {key: (n % RING, n // RING) for n, (key, _) in enumerate(stream)}
        FBLK = DFF // 256
        n0 = next(n for n, (key, _) in enumerate(stream) if key[1] == 1)
        extra = [0, 2 * (FBLK // 2 + 1), 2 * (FBLK // 2)]

        def uses_before(s, n):
            return len([m for m in range(n) if m % RING == s])

        def slot_of(key):
            s, use = place[key]
            n = next(m for m, (k, _) in enumerate(stream) if k == key)
            return s, use + 1 + (extra[s] if n >= n0 else 0)


        ZSEQ = [[(k, t) for k in ("q", "k", "v") for t in range(TILES)]] * 2
        block = ctx.enter_context(nc.Block())

        @block.tensor
        def _(pe):
            mm = nc.tensor.matmul
            tr = nc.tensor.transpose

            def open_bank(*key):
                b, use = banks.open(*key)
                if use:
                    pe.wait_ge(free[b], use)
                return b

            def slot(key):
                s, n = slot_of(key)
                pe.wait_ge(slot_full[s], 16 * n)
                return slots[s]

            def release(key, *last):
                released[key] = last

            def to_channel_major(j, src_ready, src, dst_tiles):
                for t in dst_tiles:
                    pe.wait_ge(*at(*src_ready(t)))
                    for kh in range(2):
                        b = open_bank("tc", j, t, kh)
                        for k in range(4):
                            ins = tr(bank[b][:, k * P:k * P + ROWS[t]],
                                     src[0:ROWS[t], t, (4 * kh + k) * P:(4 * kh + k + 1) * P],
                                     ident[0:ROWS[t], 0:ROWS[t]])
                        ins.then_inc(full[b], 1)

            def token_product(key, xT, w, nk, t, cols=HALF, col0=0):
                b = open_bank(*key)
                t0 = t * P
                for k in range(nk):
                    ins = mm(bank[b][0:ROWS[t], 0:cols], xT[:, k, t0:t0 + ROWS[t]], w[:, k, col0:col0 + cols],
                             start=k == 0, stop=k == nk - 1)
                ins.then_inc(full[b], 1)

            def unit_transpose(u):
                rows = ROWS[UNITS[u][2]]
                pe.wait_ge(*at("unit", u))
                b = open_bank("ut", u)
                for c in range(4):
                    ins = tr(bank[b][:, c * P:c * P + rows], nbuf[u % 2][0:rows, c * P:(c + 1) * P],
                             ident[0:rows, 0:rows])
                ins.then_inc(full[b], 1)

            def wait_hT(j, tiles=range(TILES)):
                for t in tiles:
                    for kh in range(2):
                        pe.wait_ge(*taken("tc", j, t, kh))

            def memory_keys_values(l):
                to_channel_major(("mem", l), lambda t: ("mem_in", l), mem, range(2))
                for t in range(2):
                    for kh in range(2):
                        pe.wait_ge(*taken("tc", ("mem", l), t, kh))
                w = slot(("ck", l)).rearrange("p (k n) -> p k n", k=KD)
                for t in range(2):
                    token_product(("z", "mk", l, t), hT, w, KD, t)
                release(("ck", l), "z", "mk", l, 1)
                w = slot(("cv", l)).rearrange("p (k n) -> p k n", k=KD)
                for t in range(2):
                    token_product(("z", "mv", l, t), hT, w, KD, t)
                    unit_transpose(UNIT["mk", l, t])
                release(("cv", l), "z", "mv", l, 1)

            def cache_transpose(stage, hf, j):
                n = (stage * 2 + hf) * 8 + j
                pe.wait_ge(knat_full[j % 4], 16 * (n // 4 + 1))
                b = open_bank("kt", stage, hf, j)
                for c in range(4):
                    ins = tr(bank[b][:, c * P:(c + 1) * P], knat[:, j % 4, c * P:(c + 1) * P], ident)
                ins.then_inc(full[b], 1)

            def stick_scores(hd):
                c = hd // 2
                b = open_bank("s", 1, hd)
                for qt in range(2):
                    ins = mm(bank[b][:, qt * P:(2 * qt + 1) * P], qz[:, c, hd % 2, qt * P:(qt + 1) * P],
                             kN[:, c, 0:(qt + 1) * P], start=True, stop=True)
                ins.then_inc(full[b], 1)

            def layernorm_sums():
                pe.wait_ge(*at("conv"))
                b = open_bank("lmean")
                for c in range(NCH):
                    ins = mm(bank[b][:, 0:T], C("ones"), conv[:, c, :], start=c == 0, stop=c == NCH - 1)
                ins.then_inc(full[b], 1)
                pe.wait_ge(*at("cent_sq"))
                b = open_bank("lvar")
                for t in range(TILES):
                    for c in range(NCH):
                        ins = mm(bank[b][0:ROWS[t], t:t + 1], squares[:, c, t * P:t * P + ROWS[t]], C("ones", 0, 1),
                                 start=c == 0, stop=c == NCH - 1)
                ins.then_inc(full[b], 1)

            def layernorm_spread():
                pe.wait_ge(*at("ln_diag"))
                b = open_bank("lrs")
                for t in range(TILES):
                    ins = mm(bank[b][:, t * P:t * P + ROWS[t]], C("ones")[0:ROWS[t]],
                             S_t[0:ROWS[t], t * P:t * P + ROWS[t]], start=True, stop=True)
                ins.then_inc(full[b], 1)

            def prompt_scores(l, hd):
                c = hd // 2
                for qt in range(2):
                    nk = (qt + 1) * P
                    b = open_bank("s", l, hd, qt)
                    out = bank[b][:, 0:nk]
                    ins = mm(out, qz[:, c, hd % 2, qt * P:(qt + 1) * P], kN[:, c, 0:nk],
                             start=True, stop=l == 1)
                    if l == 0:
                        ins = mm(out, lr[:, 0, hd, :], C("neg_upto", 0, nk), start=False, stop=qt == 0)
                        if qt == 1:
                            ins = mm(out[:, P:2 * P], lr[:, 1, hd, :], C("neg_upto", 0, P),
                                     start=False, stop=True)
                    ins.then_inc(full[b], 1)

            def prompt_values(l, hd, between):
                probs = Pr[hd % 2] if l == 0 else stick_P[hd % 4]
                for qt in range(2):
                    pe.wait_ge(*(at("probs", 0, "p", hd, qt) if l == 0 else at("probs", 1, "p", hd)))
                    if qt == 0:
                        b = open_bank("pt", l, hd)
                    for kt in range(qt + 1):
                        ins = tr(bank[b][:, (qt + kt) * P:(qt + kt + 1) * P],
                                 probs[:, (qt + kt) * P:(qt + kt + 1) * P], ident)
                ins.then_inc(full[b], 1)
                between()
                pe.wait_ge(*taken("pt", l, hd))
                c = hd // 2
                if hd % 2 == 0:
                    prompt_values.b = open_bank("o", l, c)
                out = bank[prompt_values.b][:, (hd % 2) * SEQ:(hd % 2 + 1) * SEQ]
                mm(out, v[:, 0, c * P:(c + 1) * P], PT[hd % 2][:, 0:SEQ], start=True, stop=False)
                ins = mm(out[:, P:SEQ], v[:, 1, c * P:(c + 1) * P], PT[hd % 2][:, SEQ:SEQ + P],
                         start=False, stop=True)
                if hd % 2 == 1:
                    ins.then_inc(full[prompt_values.b], 1)

            def sample_scores(l, g):
                b = open_bank("ss", l, g)
                q = qbd.rearrange("p (g b c r) -> p g b c r", g=4, b=2, c=NCH)
                old, new = bank[b][:, 0:PAST], bank[b][:, PAST:PAST + NSAMP]
                for b2 in range(2):
                    for c in range(NCH):
                        mm(old, q[:, g, b2, c, :], kT[:, c, 2 * (g % 2) + b2, :],
                           start=(b2, c) == (0, 0), stop=l == 1 and (b2, c) == (1, 3))
                if l == 0:
                    for b2 in range(2):
                        for pg in range(NPG):
                            mm(old, lb[:, 2 * g + b2, pg, :], C("after" if pg == 0 else "ones", 0, 2 * P),
                               start=False, stop=False)
                    mm(old, ln1_t[0:NSAMP, g * P:(g + 1) * P], view(C("ones")[0:NSAMP], 0, [[0, 2], [1, P]]),
                       start=False, stop=True)
                for b2 in range(2):
                    for c in range(NCH):
                        ins = mm(new, q[:, g, b2, c, :], kN[:, c, SEQ:T],
                                 start=(b2, c) == (0, 0), stop=l == 1 and (b2, c) == (1, 3))
                if l == 0:
                    mm(new, ln1_t[0:NSAMP, g * P:(g + 1) * P], C("ones", 0, NSAMP)[0:NSAMP],
                       start=False, stop=False)
                    ins = mm(new, ln2_t[0:NSAMP, g * P:(g + 1) * P], C("new_upto")[0:NSAMP],
                             start=False, stop=True)
                ins.then_inc(full[b], 1)

            def ahead(stage, hf, i):
                if hf == 0:
                    for j in AHEAD[i]:
                        cache_transpose(stage, 1, j)

            def sample_values(l, hf):
                gs = (2 * hf, 2 * hf + 1)
                for g in gs:
                    pe.wait_ge(*at("probs", l, "s", g))
                    b = open_bank("pts", l, g)
                    for kt in range(2):
                        tr(bank[b][:, kt * P:(kt + 1) * P], Pr[g % 2][:, kt * P:(kt + 1) * P], ident)
                    ins = tr(bank[b][0:NSAMP, 2 * P:3 * P], Pr[g % 2][:, 2 * P:2 * P + NSAMP], ident)
                    ins.then_inc(full[b], 1)
                ahead(2 * l, hf, 1)
                for g in gs:
                    pe.wait_ge(*taken("pts", l, g))
                    pe.wait_ge(*at("v_in", 2 * l, g // 2))
                    b = open_bank("os", l, g)
                    for b2 in range(2):
                        for pg in range(NPG):
                            mm(bank[b][64 * b2:64 * b2 + 64, :], PT[g % 2][:, pg * P + 64 * b2:pg * P + 64 * b2 + 64],
                               vC[:, 2 * (g % 2) + b2, pg, :], start=pg == 0, stop=False)
                    mm(bank[b][:, :], PT[g % 2][0:NSAMP, 2 * P:3 * P], v[0:NSAMP, 2, :], start=False, stop=True) \
                        .then_inc(full[b], 1)
                ahead(2 * l, hf, 2)
                for g in gs:
                    output_transpose(("ost", l, g), ("os", l, g), g % 2)

            def output_transpose(key, source, i):
                pe.wait_ge(*taken(*source))
                b = open_bank(*key)
                for c in range(4):
                    ins = tr(bank[b][:, c * P:(c + 1) * P], osam[i][:, c * P:(c + 1) * P], ident)
                ins.then_inc(full[b], 1)

            def self_attention(l):
                stage = 2 * l
                for t in range(TILES):
                    for k in ("q", "k"):
                        pe.wait_ge(*taken("ut", UNIT[k, l, t]))
                    pe.wait_ge(*taken("z", "v", l, t))
                if l == 0:
                    pe.wait_ge(*at("lr", 0))
                if l == 0:
                    prompt_scores(l, 0)
                    prompt_scores(l, 1)
                else:
                    for hd in range(4):
                        stick_scores(hd)
                    layernorm_sums()
                for hd in range(NH):
                    if l == 0 and hd + 2 < NH:
                        prompt_scores(l, hd + 2)
                    if l == 1 and hd % 2 == 0 and hd + 4 < NH:
                        stick_scores(hd + 4)
                        stick_scores(hd + 5)
                    prompt_values(l, hd, lambda: cache_transpose(stage, 0, hd))
                    if l == 1 and hd == 1:
                        layernorm_spread()
                for hf in range(2):
                    for j in range(8):
                        pe.wait_ge(*taken("kt", stage, hf, j))
                    if l == 0 and hf == 0:
                        pe.wait_ge(*at("lb", 0))
                    for g in (2 * hf, 2 * hf + 1):
                        sample_scores(l, g)
                    ahead(stage, hf, 0)
                    sample_values(l, hf)

            def out_projection(l):
                for c in range(NCH):
                    pe.wait_ge(*taken("ost", l, c))
                    pe.wait_ge(*taken("o", l, c))
                    pe.wait_ge(*(taken("pm", c) if l == 0 else at("y_mix", c)))
                for hf in range(2):
                    w = slot(("wo", l, hf)).rearrange("p (k n) -> p k n", k=KD)
                    for t in range(TILES):
                        token_product(("wo", l, hf, t), yT, w, KD, t)
                    release(("wo", l, hf), "wo", l, hf, 2)

            def cross_attention(l):
                stage = 2 * l + 1
                w = slot(("cq", l)).rearrange("p (k n) -> p k n", k=KD)
                wait_hT(3 * l + 1, range(2))
                for t in range(TILES):
                    if t == 2:
                        wait_hT(3 * l + 1, (2,))
                    token_product(("z", "cq", l, t), hT, w, KD, t)
                    if t == 0:
                        to_channel_major(3 * l + 1, lambda t: ("h", 3 * l + 1, t), h, (2,))
                    if t:
                        unit_transpose(UNIT["cq", l, t - 1])
                release(("cq", l), "z", "cq", l, 2)
                for t in range(2):
                    pe.wait_ge(*taken("ut", UNIT["cq", l, t]))
                    pe.wait_ge(*taken("ut", UNIT["mk", l, t]))
                    pe.wait_ge(*taken("z", "mv", l, t))

                def scores(hd):
                    b = open_bank("cs", l, hd)
                    for qt in range(2):
                        ins = mm(bank[b][:, qt * NMEM:(qt + 1) * NMEM], kN[:, hd, qt * P:(qt + 1) * P],
                                 kM[:, hd, :], start=True, stop=True)
                    ins.then_inc(full[b], 1)

                def values(hd):
                    pe.wait_ge(*at("probs", l, "cp", hd))
                    b = open_bank("cpt", l, hd)
                    for kt in range(2):
                        for qt in range(2):
                            ins = tr(bank[b][:, (2 * kt + qt) * P:(2 * kt + qt + 1) * P],
                                     Pr[hd % 2][:, qt * NMEM + kt * P:qt * NMEM + (kt + 1) * P], ident)
                    ins.then_inc(full[b], 1)
                    cache_transpose(stage, 0, 2 * hd)
                    cache_transpose(stage, 0, 2 * hd + 1)
                    pe.wait_ge(*taken("cpt", l, hd))
                    b = open_bank("co", l, hd)
                    for kt in range(2):
                        ins = mm(bank[b][:, 0:SEQ], vM[:, kt, hd * P:(hd + 1) * P],
                                 PT[hd % 2][:, kt * SEQ:(kt + 1) * SEQ], start=kt == 0, stop=kt == 1)
                    ins.then_inc(full[b], 1)

                scores(0)
                scores(1)
                unit_transpose(UNIT["cq", l, 2])
                pe.wait_ge(*taken("ut", UNIT["cq", l, 2]))
                for hd in range(XH):
                    if 2 <= hd + 1 < XH:
                        scores(hd + 1)
                    values(hd)
                q = qbd.rearrange("p (g b h r) -> p g b h r", g=2, b=4, h=XH)
                for hf in range(2):
                    for j in range(8):
                        pe.wait_ge(*taken("kt", stage, hf, j))
                    b = open_bank("css", l, hf)
                    for b4 in range(4):
                        for hd in range(XH):
                            ins = mm(bank[b][:, 0:NMEM], q[:, hf, b4, hd, :], kT[:, hd, b4, :],
                                     start=(b4, hd) == (0, 0), stop=(b4, hd) == (3, 3))
                    ins.then_inc(full[b], 1)
                    ahead(stage, hf, 0)
                    if hf:
                        output_transpose(("cost", l, 0), ("cos", l, 0), 0)
                    pe.wait_ge(*at("probs", l, "cs", hf))
                    b = open_bank("cpts", l, hf)
                    for kt in range(2):
                        ins = tr(bank[b][:, kt * P:(kt + 1) * P], Pr[hf][:, kt * P:(kt + 1) * P], ident)
                    ins.then_inc(full[b], 1)
                    ahead(stage, hf, 1)
                    pe.wait_ge(*taken("cpts", l, hf))
                    pe.wait_ge(*at("v_in", stage, hf))
                    b = open_bank("cos", l, hf)
                    for b4 in range(4):
                        for kt in range(2):
                            r0 = kt * P + b4 * 32
                            ins = mm(bank[b][32 * b4:32 * b4 + 32, :], PT[hf][:, r0:r0 + 32], vC[:, b4, kt, :],
                                     start=kt == 0, stop=kt == 1)
                    ins.then_inc(full[b], 1)
                    ahead(stage, hf, 2)
                output_transpose(("cost", l, 1), ("cos", l, 1), 1)
                for hf in range(2):
                    pe.wait_ge(*taken("cost", l, hf))
                for hd in range(XH):
                    pe.wait_ge(*taken("co", l, hd))
                w = slot(("co", l)).rearrange("p (k n) -> p k n", k=4)
                for hf in range(2):
                    for t in range(TILES):
                        token_product(("wc", l, hf, t), yT, w, 4, t, col0=hf * HALF)
                release(("co", l), "wc", l, 1, 2)

            for p_ in prime["pe"]:
                pe.sem_inc(p_, 1)
            pe.wait_ge(*at("head_in"))
            memory_keys_values(0)
            pe.wait_ge(*at("const_in"))
            pe.wait_ge(*at("table_in"))
            b = open_bank("chan")
            for c in range(NCH):
                ins = tr(bank[b][:, c * (4 + CW):(c + 1) * (4 + CW)], PT[1][0:4 + CW, c * P:(c + 1) * P],
                         ident[0:4 + CW, 0:4 + CW])
            ins.then_inc(full[b], 1)
            to_channel_major(0, lambda t: ("h", 0, t), h, range(TILES))
            wait_hT(0)
            lag = 2
            for n, (k, t) in enumerate(ZSEQ[0]):
                if t == 0:
                    w = slot((k, 0)).rearrange("p (k n) -> p k n", k=KD)
                token_product(("z", k, 0, t), hT, w, KD, t)
                if t == 2:
                    release((k, 0), "z", k, 0, 2)
                if n >= lag and ZSEQ[0][n - lag][0] != "v":
                    unit_transpose(UNIT[ZSEQ[0][n - lag][0], 0, ZSEQ[0][n - lag][1]])
            b = open_bank("fl")
            for t in range(TILES):
                for k in range(KD):
                    ins = mm(bank[b][0:ROWS[t], 8 * t:8 * t + 8], hT[:, k, t * P:t * P + ROWS[t]], wfl[:, k, :],
                             start=k == 0, stop=k == KD - 1)
            ins.then_inc(full[b], 1)
            pe.wait_ge(*at("pre_in"))
            b = open_bank("pre")
            for g in range(NCH):
                ins = tr(bank[b][:, g * 120:(g + 1) * 120], PT[0][0:120, g * P:(g + 1) * P], ident[0:120, 0:120])
            ins.then_inc(full[b], 1)
            w = slot(("p", 0)).rearrange("p (k n) -> p k n", k=KD)
            for g in range(NCH):
                b = open_bank("p", g)
                for k in range(KD):
                    ins = mm(bank[b][:, 0:T], w[:, k, g * P:(g + 1) * P], hT[:, k, :],
                             start=k == 0, stop=k == KD - 1)
                ins.then_inc(full[b], 1)
            release(("p", 0), "p", NCH - 1)
            pe.wait_ge(*at("logf"))
            b = open_bank("Fq")
            mm(bank[b][:, 0:8], C("upto"), logf[:, 0, :], start=True, stop=True)
            mm(bank[b][:, 8:16], C("ones"), logf[:, 0, :], start=True, stop=False)
            mm(bank[b][:, 8:16], C("upto"), logf[:, 1, :], start=False, stop=True).then_inc(full[b], 1)
            pe.wait_ge(*taken("p", NCH - 1))
            for n, (src, rows) in enumerate((("p", P), ("s", NSAMP))):
                b = open_bank("pst", src)
                for g in range(NCH):
                    t_in = poolF[:, g, PBUF + P:PBUF + SEQ] if n == 0 else \
                        pool_new[:, g, :]
                    ins = tr(bank[b][0:rows, g * P:(g + 1) * P], t_in, ident)
                ins.then_inc(full[b], 1)
            for g in range(NCH):
                pe.wait_ge(*at("pool_d", g))
                b = open_bank("pm", g)
                mm(bank[b][:, 0:T], wpg[:, g, :], L_t[:, (g % 2) * T:(g % 2 + 1) * T],
                   start=True, stop=True).then_inc(full[b], 1)
            self_attention(0)
            out_projection(0)
            to_channel_major(1, lambda t: ("h", 1, t), h, range(2))
            cross_attention(0)
            to_channel_major(2, lambda t: ("h", 2, t), h, range(TILES))
            wait_hT(2)

            for b in range(8):
                pe.wait_ge(free[b], banks.uses(b))

            def gate_up(blk, f2, ff, lo):
                w = [t[blk].rearrange("p (m k n) -> p m k n", m=2, k=KD) for t in (gu_high, gu_low)]
                for m, (bk, read, done) in enumerate(((6, ffn_silu, ffn_gate), (7, ffn_h, ffn_up))):
                    pe.wait_ge(ffn_wlo, lo + (m + 1))
                    pe.wait_ge(read, ff)
                    for k in range(KD):
                        for xa, wa in ((0, 0), (1, 0), (0, 1)):
                            ins = mm(bank[bk][:, 0:T], w[wa][:, m, k, f2 * P:(f2 + 1) * P],
                                     ffn_x[:, k, :] if xa == 0 else ffn_xlo[k // 4][:, k % 4, :],
                                     start=k == 0 and (xa, wa) == (0, 0), stop=k == KD - 1 and wa == 1)
                    ins.then_inc(done, 1)

            def down(blk, f2, ff, first=False, last=False):
                w = [t[blk].rearrange("p (f n) -> p f n", f=2) for t in (dn_high, dn_low)]
                pe.wait_ge(ffn_hlo_ready, ff + 1)
                for hf in range(2):
                    for t in range(TILES):
                        for xa, wa in ((0, 0), (1, 0), (0, 1)):
                            ins = mm(bank[3 * hf + t][0:ROWS[t], :],
                                     (ffn_hhi, ffn_hlo)[xa][f2][:, t * P:t * P + ROWS[t]],
                                     w[wa][:, f2, hf * HALF:(hf + 1) * HALF],
                                     start=first and (xa, wa) == (0, 0), stop=last and wa == 1)
                ins.then_inc(ffn_down, 1)

            def ffn_block(blk, i, first=False):
                gate_up(blk, 0, i * 2, i * 3)
                if not first:
                    down(1 - blk, 1, i * 2 - 1)
                gate_up(blk, 1, i * 2 + 1, i * 3)
                pe.wait_ge(ffn_wlo, i * 3 + 3)
                down(blk, 0, i * 2, first=first)

            ffn_block(0, 0, first=True)
            with pe.Fori(0, FBLK // 2) as i:
                ffn_block(1, i * 2 + 1)
                ffn_block(0, i * 2 + 2)
            down(0, 1, DFF // P - 1, last=True)
            for hf in range(2):
                for t in range(TILES):
                    pe.wait_ge(*at("ffn_out", hf, t))

            memory_keys_values(1)
            to_channel_major(3, lambda t: ("h", 3, t), h, range(TILES))
            wait_hT(3)
            for m, name in enumerate("ag"):
                w = slot((name, 1)).rearrange("p (k n) -> p k n", k=KD)
                for c in range(NCH):
                    b = open_bank(name, c)
                    for k in range(KD):
                        ins = mm(bank[b][:, 0:T], w[:, k, c * P:(c + 1) * P], hT[:, k, :],
                                 start=k == 0, stop=k == KD - 1)
                    ins.then_inc(full[b], 1)
                release((name, 1), name, NCH - 1)
                if m == 0:
                    pe.wait_ge(*at("cpre_in"))
                    for n in range(2):
                        b = open_bank("cpre", n)
                        for c in range(NCH):
                            ins = tr(bank[b][:, c * 120:(c + 1) * 120], PT[n][0:120, c * P:(c + 1) * P],
                                     ident[0:120, 0:120])
                        ins.then_inc(full[b], 1)
            for n, (k, t) in enumerate(ZSEQ[1]):
                if t == 0:
                    w = slot((k, 1)).rearrange("p (k n) -> p k n", k=KD)
                token_product(("z", k, 1, t), hT, w, KD, t)
                if t == 2:
                    release((k, 1), "z", k, 1, 2)
                if n >= lag and ZSEQ[1][n - lag][0] != "v":
                    unit_transpose(UNIT[ZSEQ[1][n - lag][0], 1, ZSEQ[1][n - lag][1]])
            pe.wait_ge(*taken("a", NCH - 1))
            for n, (src, rows) in enumerate((("p", P), ("s", NSAMP))):
                b = open_bank("cst", src)
                for c in range(NCH):
                    t_in = convF[:, c, CBUF + P:CBUF + SEQ] if n == 0 else \
                        conv_new[:, c, :]
                    ins = tr(bank[b][0:rows, c * P:(c + 1) * P], t_in, ident)
                ins.then_inc(full[b], 1)
            self_attention(1)
            out_projection(1)
            to_channel_major(4, lambda t: ("h", 4, t), h, range(2))
            cross_attention(1)
            to_channel_major(5, lambda t: ("h", 5, t), h, range(TILES))
            wait_hT(5)

            b = open_bank("rt")
            for t in range(TILES):
                for k in range(KD):
                    ins = mm(bank[b][0:ROWS[t], 8 * t:8 * t + 8], hT[:, k, t * P:t * P + ROWS[t]], wrt[:, k, :],
                             start=k == 0, stop=k == KD - 1)
            ins.then_inc(full[b], 1)
            pe.wait_ge(*at("picked"))
            b = open_bank("rank")
            for t in range(TILES):
                for s in range(t + 1):
                    mm(bank[b][0:ROWS[t], 8 * t:8 * t + 8], C("before" if s == t else "ones")[0:ROWS[s], 0:ROWS[t]],
                       picked[0:ROWS[s], s, :], start=s == 0, stop=s == t)
            for s in range(TILES):
                ins = mm(bank[b][:, 24:32], C("ones")[0:ROWS[s], :], picked[0:ROWS[s], s, :],
                         start=s == 0, stop=s == TILES - 1)
            ins.then_inc(full[b], 1)
            for b in range(8):
                pe.wait_ge(free[b], banks.uses(b))

            def split_product(n, m, j, out, x_hi_lo, chunks):
                for q in range(2):
                    i = 2 * PRODUCTS.index((m, j)) + q
                    pe.wait_ge(*lo_parts(n, i))
                    w = [t[i % PRING].rearrange("p (k n) -> p k n", k=chunks) for t in (high, low)]
                    for k in range(chunks):
                        kk = q * chunks + k
                        for xa, wa in ((0, 0), (1, 0), (0, 1)):
                            for dst, wcols in out(w[wa][:, k, :]):
                                ins = mm(dst, x_hi_lo[xa][kk], wcols,
                                         start=(m < 2 or j == 0) and kk == 0 and (xa, wa) == (0, 0),
                                         stop=(m < 2 or j == STAGES - 1) and kk == 2 * chunks - 1 and wa == 1)
                    ins.then_inc(moe_used, 1)

            def scatter(i, done):
                t, hf = i // 2, i % 2
                mm(bank[6 + i % 2][0:ROWS[t], :], moe_GT[:, t * P:t * P + ROWS[t]],
                   moe_y[:, hf * HALF:(hf + 1) * HALF], start=True, stop=True).then_inc(done, 1)

            def gather(n, first, r=None):
                pe.wait_ge(moe_sel, n + 1)
                if r is not None:
                    pe.wait_ge(moe_addedE, r * 6)
                pe.wait_ge(*primed(moe_GTc, n))
                for half in range(2):
                    if half and not first:
                        pe.wait_ge(*primed(moe_hT, n * STAGES - 1))
                    for k in range(4):
                        for t in range(TILES):
                            ins = mm(bank[7 - half][:, k * P:(k + 1) * P],
                                     h[0:ROWS[t], t, (4 * half + k) * P:(4 * half + k + 1) * P],
                                     moe_P[0:ROWS[t], t, :], start=t == 0, stop=t == TILES - 1)
                    ins.then_inc(moe_gathered, 1)

            def expert(n, last, r=None):
                if r is not None:
                    pe.wait_ge(moe_zero, r + 1)
                pe.wait_ge(*primed(moe_xT, n * 2 + 2))

                def product(m, j):
                    pe.wait_ge(*primed(moe_silu if m == 0 else moe_h, n * STAGES + max(j - 1, 0)))
                    split_product(n, m, j, lambda w: [(bank[2 * m + j % 2][:, :], w)],
                                  [[moe_x[i][:, k, :] for k in range(KD)] for i in range(2)], KD // 2)

                def hidden_transpose(j):
                    pe.wait_ge(*primed(moe_h, n * STAGES + (j + 1)))
                    if j:
                        pe.wait_ge(*primed(moe_hT, n * STAGES + j))
                    else:
                        pe.wait_ge(*primed(moe_added, n * 6 + 5))
                    if j == STAGES - 1 and not last:
                        pe.wait_ge(*primed(moe_xT, n * 2 + 4))
                    for c in range(4):
                        ins = tr(bank[6][:, c * P:(c + 1) * P], moe_hid[j % 2][:, c * P:(c + 1) * P], ident)
                    ins.then_inc(moe_tr, 1)

                def down_product(j):
                    pe.wait_ge(*primed(moe_hT, n * STAGES + (j + 1)))
                    if j == 0:
                        pe.wait_ge(*primed(moe_yc, n * 2))
                    split_product(n, 2, j,
                                  lambda w: [(bank[4 + hf][:, :], w[:, hf * HALF:(hf + 1) * HALF]) for hf in range(2)],
                                  [[moe_hidT[i][:, k * P:(k + 1) * P] for k in range(4)] for i in range(2)], 2)

                product(0, 0)
                pe.wait_ge(*primed(moe_yc, n * 2))
                pe.wait_ge(*primed(moe_hT, n * STAGES))
                scatter(0, moe_scattered)
                scatter(1, moe_scattered)
                product(1, 0)
                pe.wait_ge(*primed(moe_added, n * 6 + 1))
                scatter(2, moe_scattered)
                pe.wait_ge(*primed(moe_added, n * 6 + 2))
                scatter(3, moe_scattered)
                product(0, 1)
                pe.wait_ge(*primed(moe_added, n * 6 + 3))
                scatter(4, moe_scattered)
                pe.wait_ge(*primed(moe_added, n * 6 + 4))
                scatter(5, moe_scattered)
                hidden_transpose(0)
                product(1, 1)
                down_product(0)
                pe.wait_ge(*primed(moe_added, n * 6 + 6))
                for t in range(TILES):
                    ins = tr(bank[7][:, t * P:t * P + ROWS[t]], moe_G[0:ROWS[t], t, :],
                             ident[0:ROWS[t], 0:ROWS[t]])
                ins.then_inc(moe_GTr, 1)
                for j in range(1, STAGES):
                    if j + 1 < STAGES:
                        product(0, j + 1)
                    hidden_transpose(j)
                    if j + 1 < STAGES:
                        product(1, j + 1)
                        if j + 2 == STAGES and not last:
                            gather(n + 1, False)
                    down_product(j)

            def expert_round(r):
                if type(r) is int:
                    pe.wait_ge(moe_zero, r + 1)
                rr = None if type(r) is int else r
                gather(r * NE, True, rr)
                with pe.Fori(0, NE - 1) as e:
                    expert(e + r * NE, False, rr)
                expert(r * NE + (NE - 1), True, rr)
                pe.wait_ge(*primed(moe_yc, r * 16 + 16))
                for i in range(6):
                    if i >= 2:
                        pe.wait_ge(moe_addedE, r * 6 + (i - 1))
                    else:
                        pe.wait_ge(*(primed(moe_hT, (r + 1) * NE * STAGES) if i == 0 else primed(moe_GTc, (r + 1) * NE)))
                    scatter(i, moe_scatteredE)

            expert_round(0)
            pe.wait_ge(*at("cmax"))
            most = pe.value_load(cmax_i[0:1, 0:1])
            with pe.If(most > CAP):
                with pe.Fori(1, ROUNDS) as r:
                    expert_round(r)

        @block.sync
        def _(sp):
            def wait_group(*key):
                b, use = banks.of(*key)
                sp.wait_ge(full[b], use)

            def stream_load(n):
                key, src = stream[n]
                s = n % RING
                if n0 <= n < n0 + RING and s:
                    sp.wait_ge(ffn_up, 2 * FBLK if s == 1 else 2 * (FBLK - 1))
                elif n >= RING:
                    wait_group(*releases.get(stream[n - RING][0], ("fl",)))
                dst = slots[s].rearrange("p (k n) -> p k n", k=src.shape[1])
                sp.dma_start(dst, src).then_inc(slot_full[s], 16)

            def page(i):
                return sp.value_load(pt[0:1, i:i + 1], min_val=0, max_val=a["cache_fox_k"].shape[1] - 1)

            def key_load(stage, hf, j):
                n = (stage * 2 + hf) * 8 + j
                if n >= 4:
                    m = n - 4
                    wait_group("kt", m // 16, m // 8 % 2, m % 8)
                l, b, g = stage // 2, 4 * hf + j // 2, j % 2
                if stage % 2 == 0:
                    src = a["cache_fox_k" if l == 0 else "cache_sb_k"][0][page(2 * b + g), :, :, :]
                else:
                    src = a["cache_mem_k"][l, b, g * P:(g + 1) * P]
                sp.dma_start(knat[:, j % 4, :], src.rearrange("s h d -> s (h d)")).then_inc(knat_full[j % 4], 16)

            def value_loads(stage, hf):
                l = stage // 2
                for j in range(8):
                    b, g = 4 * hf + j // 2, j % 2
                    if stage % 2 == 0:
                        src = a["cache_fox_v" if l == 0 else "cache_sb_v"][0][page(2 * b + g), :, :, :]
                    else:
                        src = a["cache_mem_v"][l, b, g * P:(g + 1) * P]
                    sp.dma_start(vC[:, j // 2, g, :], src.rearrange("s h d -> s (h d)")) \
                        .then_inc(*sets("v_in", stage, hf, by=16))

            sp.dma_start(cbuf[:, 0:P + 1], a["const_table"][:, 0:P + 1]).then_inc(*sets("head_in", by=16))
            sp.dma_start(mem, a["mem_prompt"][0].rearrange("(t p) d -> p t d", p=P)).then_inc(*sets("mem_in", 0, by=16))
            stream_load(0)
            sp.dma_start(x[:, 0:2, :], a["x_prompt"][0].rearrange("(t p) d -> p t d", p=P)).then_inc(*sets("x_in", by=16))
            sp.dma_start(x[0:NSAMP, 2, :], a["x_sample"].rearrange("b s d -> (b s) d")).then_inc(*sets("x_in", by=16))
            stream_load(1)
            sp.dma_start(PT[0][0:NB * PBUF, :], a["state_pool"][0].rearrange("b j c -> (b j) c")) \
                .then_inc(*sets("pre_in", by=16))
            sp.dma_start(cbuf[:, P + 1:], a["const_table"][:, P + 1:]).then_inc(*sets("table_in", by=16))
            for n in range(2, 5):
                stream_load(n)
            sp.wait_ge(*at("pt_in"))
            for j in range(16):
                sp.dma_start(lfp[:, j // 2, j % 2, :], a["cache_fox_logf"][0][page(j), :, :]) \
                    .then_inc(*sets("lfp_in", by=16))
            for l in range(2):
                base = 0 if l == 0 else n0
                st = 2 * l
                if l == 1:
                    wait_group("tc", 2, 2, 1)
                    sp.dma_start(mem, a["mem_prompt"][0].rearrange("(t p) d -> p t d", p=P)) \
                        .then_inc(*sets("mem_in", 1, by=16))
                    stream_load(n0)
                    stream_load(n0 + 1)
                    stream_load(n0 + 2)
                    sp.wait_ge(ffn_down, 2 * FBLK)
                    for n in range(2):
                        sp.dma_start(PT[n][0:120, :],
                                     a["state_conv"][0, 4 * n:4 * n + 4].rearrange("b j c -> (b j) c")) \
                            .then_inc(*sets("cpre_in", by=16))
                    for n in range(3, 7):
                        stream_load(n0 + n)
                for j in range(4):
                    key_load(st, 0, j)
                if l == 0:
                    value_loads(st, 0)
                first = 5 if l == 0 else n0 + 7
                for n in range(first, first + (4 if l == 0 else 3)):
                    stream_load(n)
                for j in range(4, 8):
                    key_load(st, 0, j)
                if l == 1:
                    sp.wait_ge(*at("y_mix", NCH - 1))
                    value_loads(st, 0)
                for j in range(8):
                    key_load(st, 1, j)
                wait_group("os", l, 1)
                value_loads(st, 1)
                for j in range(4):
                    key_load(st + 1, 0, j)
                wait_group("os", l, 3)
                value_loads(st + 1, 0)
                stream_load(first + (4 if l == 0 else 3))
                for j in range(4, 8):
                    key_load(st + 1, 0, j)
                for j in range(8):
                    key_load(st + 1, 1, j)
                wait_group("cos", l, 0)
                value_loads(st + 1, 1)
                if l == 0:
                    wg = a["w_gate"][0].rearrange("(k p) (i n) -> i p k n", p=P, n=256)
                    wu = a["w_up"][0].rearrange("(k p) (i n) -> i p k n", p=P, n=256)
                    wd = a["w_down"][0].rearrange("(i f p) n -> i p f n", p=P, f=2)

                    def ffn_loads(blk, i):
                        half = slots[1 + blk].rearrange("p (m k n) -> p m k n", m=2, k=KD)
                        sp.dma_start(half[:, 0], wg[i]).then_inc(slot_full[1 + blk], 16)
                        sp.dma_start(half[:, 1], wu[i]).then_inc(slot_full[1 + blk], 16)

                    def down_load(blk, i):
                        dst = slots[3 + blk][:, 0:2 * D].rearrange("p (f n) -> p f n", f=2)
                        sp.dma_start(dst, wd[i]).then_inc(slot_full[3 + blk], 16)

                    for blk in range(2):
                        m = max(n for n in range(n0) if n % RING == 1 + blk)
                        wait_group(*releases.get(stream[m][0], ("fl",)))
                        ffn_loads(blk, blk)
                    wait_group("cos", 0, 1)
                    for blk in range(2):
                        down_load(blk, blk)
                    with sp.Fori(0, FBLK // 2 - 1) as i:
                        for blk in range(2):
                            sp.wait_ge(ffn_up, i * 4 + 2 * (blk + 1))
                            ffn_loads(blk, i * 2 + (2 + blk))
                            sp.wait_ge(ffn_down, i * 4 + 2 * (blk + 1))
                            down_load(blk, i * 2 + (2 + blk))
                    sp.wait_ge(ffn_up, 2 * (FBLK - 2))
                    ffn_loads(0, FBLK - 1)
                    sp.wait_ge(ffn_down, 2 * (FBLK - 2))
                    down_load(0, FBLK - 1)

            eg = a["we_gate"][0].rearrange("e (k p) (j n) -> e j p k n", p=P, n=FB)
            eu = a["we_up"][0].rearrange("e (k p) (j n) -> e j p k n", p=P, n=FB)
            ed = a["we_down"][0].rearrange("e (j k p) n -> e j p k n", p=P, k=4)

            def expert_loads(e, n, first=False):
                for i, (m, j, q) in enumerate(PIECES):
                    if i >= PRING or not first:
                        sp.wait_ge(*primed(moe_used, n * NPIECE + (i + 1 - PRING)))
                    elif i < 4:
                        wait_group(*releases.get(stream[max(p for p in range(len(stream))
                                                            if p % RING == i // 2)][0], ("fl",)))
                    else:
                        wait_group("cos", 1, 1)
                    w = (eg, eu, ed)[m]
                    chunks = 4 if m < 2 else 2
                    sp.dma_start(raw[i % PRING].rearrange("p (k n) -> p k n", k=chunks),
                                 w[e, j][:, q * chunks:(q + 1) * chunks, :]).then_inc(raw_full[i % PRING], 16)

            expert_loads(0, 0, first=True)
            with sp.Fori(1, NE) as e:
                expert_loads(e, e)
            sp.wait_ge(*at("cmax"))
            most = sp.value_load(cmax_i[0:1, 0:1])
            with sp.If(most > CAP):
                with sp.Fori(1, ROUNDS) as r:
                    with sp.Fori(0, NE) as e:
                        expert_loads(e, e + r * NE)
            sp.wait_ge(*at("x_final"))
            sp.dma_start(o["y_prompt"][0].rearrange("(t p) d -> p t d", p=P), x[:, 0:2, :]).then_inc(*sets("y_out", by=16))
            sp.dma_start(o["y_sample"].rearrange("b s d -> (b s) d"), x[0:NSAMP, 2, :]).then_inc(*sets("y_out", by=16))
            sp.wait_ge(*at("y_out"))

        @block.gpsimd
        def _(pool):
            tt, ts = nc.gpsimd.tensor_tensor, nc.gpsimd.tensor_scalar

            def after_group(*key):
                b, use = banks.of(*key)
                pool.wait_ge(full[b], use)

            pool.dma_start(pt[0:1, :], a["page_table"].rearrange("b g -> (b g)").rearrange("(o n) -> o n", o=1)) \
                .then_inc(*sets("pt_in", by=16))
            pool.dma_start(gain[:, :], spread(a["norm_mix"][0])).then_inc(*sets("gain", 0, by=16))
            nc.gpsimd.memset(qz_t[:, :], 0.0).then_inc(*sets("qz0"))
            nc.gpsimd.memset(qbd, 0.0).then_inc(*sets("qbd0", 0))
            nc.gpsimd.memset(big[:, 14336:16384], 0.0).then_inc(*sets("lb0"))
            pool.wait_ge(*at("head_in"))

            def unit_power(u):
                kind, l, t = UNITS[u]
                hd = HD if kind in "qk" else XHD
                nh = HALF // hd
                i = u % 2
                r = ROWS[t]
                pool.wait_ge(*at("u_ss", u))
                ts(u_ms[i][0:r, 0:nh], u_ss[i][0:r, 0:nh], 1.0 / hd, EPS, ALU.mult, ALU.add) \
                    .then_inc(*sets("u_ms", u))
                pool.wait_ge(*at("u_ms", u))
                tt(u_rs[i][0:r, 0:nh], u_ms[i][0:r, 0:nh], view(C("minus_half")[0:r], 0, [[0, nh]]), ALU.pow) \
                    .then_inc(*sets("u_rs", u))

            def unit_store(u, dst):
                pool.wait_ge(*at("unit", u))
                pool.dma_start(dst, nbuf[u % 2][0:ROWS[UNITS[u][2]], :]).then_inc(*sets(f"u_out{u % 2}", u, by=16))

            def norm_power(j):
                for t in range(TILES):
                    r = ROWS[t]
                    pool.wait_ge(*at("n_ss", j, t))
                    ts(n_ms[0:r, t:t + 1], n_ss[0:r, t:t + 1], 1.0 / D, EPS, ALU.mult, ALU.add) \
                        .then_inc(*sets("n_ms", j, t))
                    pool.wait_ge(*at("n_ms", j, t))
                    tt(n_rs[0:r, t:t + 1], n_ms[0:r, t:t + 1], C("minus_half", 0, 1)[0:r], ALU.pow) \
                        .then_inc(*sets("n_rs", j, t))

            def gain_load(j):
                src = a[("norm_mix", "norm_cross", "norm_ffn")[j % 3]][j // 3]
                pool.wait_ge(*at("h", j - 1, 2))
                pool.dma_start(gain[:, :], spread(src)).then_inc(*sets("gain", j, by=16))

            def memory(l):
                for t in range(2):
                    u = UNIT["mk", l, t]
                    unit_power(u)
                    unit_store(u, o["mem_k_p"][l, 0, t * P:(t + 1) * P].rearrange("s h d -> s (h d)"))
                for t in range(2):
                    pool.wait_ge(*taken("z", "mv", l, t))
                    pool.dma_start(o["mem_v_p"][l, 0, t * P:(t + 1) * P].rearrange("s h d -> s (h d)"), vM[:, t, :]) \
                        .then_inc(*sets("vM_out", l, t, by=16))

            def new_rows(name, t):
                if t < 2:
                    return o[name + "_p"][0, 0, t * P:(t + 1) * P].rearrange("s h d -> s (h d)")
                return o[name + "_s"][0].rearrange("b s h d -> (b s) (h d)")

            def state_stores(l, name, nbuf_, src):
                pool.wait_ge(*taken("pst" if l == 0 else "cst", "p"))
                pool.dma_start(o[name + "_p"][0, 0], PT[0][P - nbuf_:P, :]).then_inc(*sets("state_out", l, by=16))
                pool.wait_ge(*taken("pst" if l == 0 else "cst", "s"))
                for b in range(NB):
                    pool.dma_start(o[name + "_s"][0, b, nbuf_ - NS:nbuf_], PT[1][b * NS:(b + 1) * NS, :]) \
                        .then_inc(*sets("state_out", l, by=16))
                pool.dma_start(o[name + "_s"][0, :, 0:nbuf_ - NS], a[src][0, :, NS:nbuf_]) \
                    .then_inc(*sets("old_state_out", by=16))

            memory(0)
            pool.wait_ge(*at("const_in"))
            ts(hg[:, 0:64], hg[:, 0:64], HD ** -0.5, None, ALU.mult).then_inc(*sets("scaled_gain"))
            for l in range(2):
                ts(g_cq[l], g_cq[l], XHD ** -0.5, None, ALU.mult).then_inc(*sets("scaled_gain"))
            norm_power(0)
            for n, (k, t) in enumerate(ZSEQ[0]):
                if k != "v":
                    unit_power(UNIT[k, 0, t])
                if k == "k":
                    unit_store(UNIT[k, 0, t], new_rows("fox_k", t))
                if k == "v":
                    pool.wait_ge(*taken("z", "v", 0, t))
                    pool.dma_start(new_rows("fox_v", t), v[0:ROWS[t], t, :]).then_inc(*sets("v_out", 0, by=16))
            pool.wait_ge(*at("lb0"))
            pool.wait_ge(*at("lfp_in"))
            lfp_ap = lfp[:, 0, 0, :]
            for b2 in range(2):
                for pg in range(NPG):
                    nc.gpsimd.tensor_copy(
                        view(lb[:, 0, 0, :], (b2 * NPG + pg) * P + b2 * 64, [[2 * NPG * P, 4], [8, 8], [1, 8]]),
                        view(lfp_ap, (b2 * NPG + pg) * 8, [[2 * NPG * 8, 4], [1, 8], [0, 8]])) \
                        .then_inc(*sets("lb", 0))
            pool.wait_ge(*at("logf"))
            pool.wait_ge(*at("h", 0, 2))
            r = NSAMP
            for g in range(4):
                spread_f = view(logf[0:r, 2, :], 0, [[0, 2], [1, 8], [0, 8]])
                out1 = ln1_t[0:r, g * P:(g + 1) * P].rearrange("p (b h s) -> p b h s", b=2, h=8)
                out2 = ln2_t[0:r, g * P:(g + 1) * P].rearrange("p (b h s) -> p b h s", b=2, h=8)
                tt(out1, spread_f, view(C("own_upto")[0:r], g * 16, [[8, 2], [0, 8], [1, 8]]), ALU.mult) \
                    .then_inc(*sets("lb", 0))
                tt(out2, spread_f, view(C("own")[0:r], g * 2, [[1, 2], [0, 8], [0, 8]]), ALU.mult) \
                    .then_inc(*sets("lb", 0))
            pool.dma_start(o["fox_logf_p"][0, 0].rearrange("(t p) h -> p t h", p=P), logf[:, 0:2, :]) \
                .then_inc(*sets("logf_out", by=16))
            pool.dma_start(o["fox_logf_s"][0].rearrange("b s h -> (b s) h"), logf[0:NSAMP, 2, :]) \
                .then_inc(*sets("logf_out", by=16))
            state_stores(0, "pool", PBUF, "state_pool")
            for l in range(2):
                if l == 1:
                    pool.wait_ge(*at("ln_var"))
                    tt(ln_rs, ln_var, view(C("minus_half"), 0, [[0, TILES]]), ALU.pow).then_inc(*sets("ln_rs"))
                after_group("ss", l, 3)
                gain_load(3 * l + 1)
                nc.gpsimd.memset(qbd, 0.0).then_inc(*sets("qbd0", 2 * l + 1))
                norm_power(3 * l + 1)
                for t in range(TILES):
                    unit_power(UNIT["cq", l, t])
                gain_load(3 * l + 2)
                after_group("css", l, 1)
                norm_power(3 * l + 2)
                if l == 0:
                    pool.wait_ge(ffn_up, 2 * FBLK)
                    nc.gpsimd.memset(qbd, 0.0).then_inc(*sets("qbd0", 2))
                    gain_load(3)
                    memory(1)
                    norm_power(3)
                    pool.wait_ge(*taken("chan"))
                    for n in range(2):
                        pool.wait_ge(*taken("cpre", n))
                    for c in range(NCH):
                        pool.wait_ge(*taken("a", c))
                        if c:
                            pool.wait_ge(conv_s, c)
                        tt(taps.rearrange("p (b s j) -> p b s j", b=NB, s=NS),
                           view(convF[:, c, :], CSEG, [[DSEG, NB], [1, NS], [1, CW]]),
                           view(cw[:, 0, c:c + 1], 0, [[0, NB], [0, NS], [1, CW]]), ALU.mult).then_inc(*sets("taps", c))
                        if c == 1:
                            unit_store(UNIT["k", 1, 0], new_rows("sb_k", 0))
                    for t in (1, 2):
                        unit_store(UNIT["k", 1, t], new_rows("sb_k", t))
                    for t in range(TILES):
                        pool.wait_ge(*taken("z", "v", 1, t))
                        pool.dma_start(new_rows("sb_v", t), v[0:ROWS[t], t, :]).then_inc(*sets("v_out", 1, by=16))
                    state_stores(1, "conv", CBUF, "state_conv")
            def expert(n):
                for i in POOLED:
                    pool.wait_ge(moe_hi, n * NPIECE + (i + 1))
                    tt(low[i % PRING], raw[i % PRING], high[i % PRING].bitcast(F32), ALU.subtract) \
                        .then_inc(moe_lo_pool, 1)

            with pool.Fori(0, NE) as e:
                expert(e)
            pool.wait_ge(*at("cmax"))
            most = pool.value_load(cmax_i[0:1, 0:1])
            with pool.If(most > CAP):
                with pool.Fori(1, ROUNDS) as r:
                    with pool.Fori(0, NE) as e:
                        expert(e + r * NE)
            for name in ("u_out0", "u_out1", "vM_out", "v_out", "state_out", "old_state_out", "logf_out"):
                pool.wait_ge(marks.sem(name), marks.count[name])


        @block.scalar
        def _(act):
            A = nc.scalar.activation

            def take(*key):
                b, use = banks.of(*key)
                act.wait_ge(full[b], use)
                return b

            def copy(out, in_):
                return A(out, in_, ACT.Copy)

            def to_hT(j, tiles):
                for t in tiles:
                    b = take("tc", j, t, 0)
                    copy(hT[:, 0:4, t * P:t * P + ROWS[t]],
                         bank[b][:, :].rearrange("p (k c) -> p k c", k=4)[:, :, 0:ROWS[t]]).then_inc(free[b], 1)

            def unit_squares(u):
                kind, l, t = UNITS[u]
                if l == 1 and kind in "qk":
                    return
                b = take("z", kind, l, t)
                if u >= 2 and not (UNITS[u - 2][1] == 1 and UNITS[u - 2][0] in "qk"):
                    act.wait_ge(*at("u_ss", u - 2))
                A(Pr[u % 2][0:ROWS[t], :], bank[b][0:ROWS[t], :], ACT.Square).then_inc(*sets("u_sq", u))

            def unit_spread(u):
                kind, l, t = UNITS[u]
                b = take("ut", u)
                src = bank[b][:, :].rearrange("p (c r) -> p c r", c=4)[:, :, 0:ROWS[t]]
                if kind == "k":
                    ins = copy(kN[:, :, t * P:t * P + ROWS[t]], src)
                elif kind == "mk":
                    ins = copy(kM[:, :].rearrange("p c t -> p c t")[:, :, t * P:(t + 1) * P], src)
                elif kind == "q" and t < 2:
                    if t == 0 and l == 0:
                        act.wait_ge(*at("qz0"))
                    copy(qz[0:64, :, 0, t * P:(t + 1) * P], src[0:64])
                    ins = copy(qz[64:P, :, 1, t * P:(t + 1) * P], src[64:P])
                elif kind == "q":
                    act.wait_ge(*at("qbd0", 2 * l))
                    for z in range(2):
                        for b2 in range(2):
                            ins = copy(view(qbd[64 * z:64 * z + 64], b2 * (NCH * P + 64) + 8 * z,
                                            [[2 * NCH * P, 4], [P + 16, NCH], [1, NS]]),
                                       view(bank[b][64 * z:64 * z + 64, :], b2 * 8, [[16, 4], [P, NCH], [1, NS]]))
                elif t < 2:
                    ins = copy(kN[:, :, t * P:(t + 1) * P], src)
                else:
                    act.wait_ge(*at("qbd0", 2 * l + 1))
                    for g in range(2):
                        ins = copy(view(qbd, g * 16 * P, [[XH * P + 32, 4], [P + 8, XH], [1, NS]]),
                                   view(bank[b][:, :], g * 32, [[8, 4], [P, XH], [1, NS]]))
                ins.then_inc(free[b], 1)

            def norm_squares(j):
                for t in range(TILES):
                    act.wait_ge(*(at("x_in") if j == 0 else at("x", j, t)))
                    if j:
                        act.wait_ge(*at("n_rs", j - 1, t))
                    if j or t:
                        act.wait_ge(*at("n_ss", *((j, t - 1) if t else (j - 1, 2))))
                    A(Pr_t[0:ROWS[t], :], x[0:ROWS[t], t, :], ACT.Square,
                      accum_out=n_ss[0:ROWS[t], t:t + 1]).then_inc(*sets("n_ss", j, t))

            def memory(l):
                to_hT(("mem", l), range(2))
                for t in range(2):
                    unit_squares(UNIT["mk", l, t])
                for t in range(2):
                    b = take("z", "mv", l, t)
                    if l == 1:
                        act.wait_ge(*at("vM_out", 0, 1))
                    copy(vM[:, t, :], bank[b][:, :]).then_inc(free[b], 1)
                    unit_spread(UNIT["mk", l, t])

            def inputs(l):
                for n, (k, t) in enumerate(ZSEQ[l]):
                    if k == "v":
                        b = take("z", "v", l, t)
                        if l == 1:
                            act.wait_ge(*at("v_out", 0))
                        copy(v[0:ROWS[t], t, :], bank[b][0:ROWS[t], :]).then_inc(free[b], 1)
                    else:
                        unit_squares(UNIT[k, l, t])
                    if n >= 2 and ZSEQ[l][n - 2][0] != "v":
                        unit_spread(UNIT[ZSEQ[l][n - 2][0], l, ZSEQ[l][n - 2][1]])

            def keys_out(stage, hf, js):
                for j in js:
                    if j % 2 == 0:
                        b = take("kt", stage, hf, j)
                        copy(kT[:, :, j // 2, (j % 2) * P:(j % 2 + 1) * P],
                             bank[b][:, :].rearrange("p (c k) -> p c k", c=4)).then_inc(free[b], 1)

            def head_out(l, hd):
                b = take("pt", l, hd)
                if hd == 0:
                    act.wait_ge(*at("state_out", l))
                copy(PT[hd % 2][:, 0:3 * P], bank[b][:, 0:3 * P]).then_inc(free[b], 1)
                keys_out(2 * l, 0, [hd])
                if hd % 2:
                    c = hd // 2
                    b = take("o", l, c)
                    copy(yT[0:64, 4 + c, 0:SEQ], bank[b][0:64, 0:SEQ])
                    copy(yT[64:P, 4 + c, 0:SEQ], bank[b][64:P, SEQ:2 * SEQ]).then_inc(free[b], 1)

            def ahead(stage, hf, i):
                if hf == 0:
                    keys_out(stage, 1, AHEAD[i])

            def sample_out(l, hf):
                gs = (2 * hf, 2 * hf + 1)
                for g in gs:
                    b = take("pts", l, g)
                    copy(PT[g % 2][:, 0:2 * P], bank[b][:, 0:2 * P])
                    copy(PT[g % 2][0:NSAMP, 2 * P:3 * P], bank[b][0:NSAMP, 2 * P:3 * P]).then_inc(free[b], 1)
                ahead(2 * l, hf, 1)
                for g in gs:
                    b = take("os", l, g)
                    copy(osam[g % 2], bank[b][:, :]).then_inc(free[b], 1)
                ahead(2 * l, hf, 2)
                for g in gs:
                    b = take("ost", l, g)
                    for z in range(2):
                        ins = copy(view(yT[64 * z:64 * z + 64, 0, :], 4 * T + SEQ + 16 * g,
                                        [[T, NCH], [8, 2], [1, NS]]),
                                   view(bank[b][64 * z:64 * z + 64, :], 8 * z, [[P + 16, NCH], [64, 2], [1, NS]]))
                    ins.then_inc(free[b], 1)

            def softmax_exp(key, i, src, dst, col=0):
                act.wait_ge(*at("neg_max", *key))
                return A(dst, src, ACT.Exp, bias=a_nm[i % 4][:, col:col + 1], accum_out=a_sm[i % 4][:, col:col + 1])

            def forget_attention():
                for i in range(2 * NH):
                    hd, qt = i // 2, i % 2
                    if hd >= 2:
                        b, use = banks.of("pt", 0, hd - 2)
                        act.wait_ge(full[b], use)
                    nk = (qt + 1) * P
                    if i >= 4:
                        act.wait_ge(*at("probs", 0, "p", (i - 4) // 2, i % 2))
                    softmax_exp((0, "p", hd, qt), i, S[i % 2][:, 0:nk], Pr[hd % 2][:, qt * P:qt * P + nk]) \
                        .then_inc(*sets("exp", 0, "p", hd, qt))
                    if i % 2 and i >= 3:
                        head_out(0, hd - 1)
                head_out(0, NH - 1)
                for hf in range(2):
                    for g in (2 * hf, 2 * hf + 1):
                        b, use = banks.of("ss", 0, g)
                        i = 2 * NH + g
                        k, n = ("pt", NH - 2 + g) if g < 2 else ("pts", g - 2)
                        b2, use2 = banks.of(k, 0, n)
                        act.wait_ge(full[b2], use2)
                        act.wait_ge(*(at("probs", 0, "p", NH - 2 + g // 2, g % 2) if g < 4 else at("probs", 0, "s", g - 4)))
                        softmax_exp((0, "s", g), i, bank[b][:, 0:T], Pr[g % 2][:, 0:T]) \
                            .then_inc(*sets("exp", 0, "s", g))
                    ahead(0, hf, 0)
                    sample_out(0, hf)

            def stick_before(i, bkey, ukey, n, dst):
                b = take(*bkey)
                A(dst, bank[b][:, 0:n], ACT.Abs).then_inc(*sets("abs", *ukey))
                act.wait_ge(*at("abs", *ukey))
                A(dst, dst, ACT.Exp, scale=-1.0).then_inc(*sets("exp_abs", *ukey))
                act.wait_ge(*at("exp_abs", *ukey))
                A(L[i % 2][:, 0:n], dst, ACT.Ln, bias=1.0).then_inc(*sets("log1p", *ukey))

            def stick_exp(i, ukey, n, dst):
                act.wait_ge(*at("log_a", *ukey))
                A(dst, L[i % 2][:, 0:n], ACT.Exp, bias=a_nm[i % 4][:, 0:1]).then_inc(*sets("stick_exp", *ukey))

            def stick_attention():
                def log1p(pair):
                    heads = (2 * pair, 2 * pair + 1)
                    for hd in heads:
                        b = take("s", 1, hd)
                        A(stick_S[hd % 4], bank[b][:, 0:3 * P], ACT.Abs).then_inc(*sets("abs", hd))
                    for hd in heads:
                        act.wait_ge(*at("abs", hd))
                        A(stick_S[hd % 4], stick_S[hd % 4], ACT.Exp, scale=-1.0).then_inc(*sets("exp_abs", hd))
                    for hd in heads:
                        act.wait_ge(*at("exp_abs", hd))
                        A(stick_L[hd % 4], stick_S[hd % 4], ACT.Ln, bias=1.0).then_inc(*sets("log1p", hd))

                def weights(pair):
                    for hd in (2 * pair, 2 * pair + 1):
                        act.wait_ge(*at("log_a", hd))
                        for qt in range(2):
                            ins = A(stick_P[hd % 4][:, qt * P:(2 * qt + 1) * P],
                                    stick_L[hd % 4][:, qt * P:(2 * qt + 1) * P], ACT.Exp,
                                    bias=a_nm[hd % 4][:, qt:qt + 1])
                        ins.then_inc(*sets("stick_exp", hd))

                log1p(0)
                state_out("cst")
                act.wait_ge(*at("cent"))
                A(squares, conv, ACT.Square).then_inc(*sets("cent_sq"))
                log1p(1)
                for pair in range(NH // 2):
                    weights(pair)
                    if pair + 2 < NH // 2:
                        log1p(pair + 2)
                    head_out(1, 2 * pair)
                    head_out(1, 2 * pair + 1)
                    if pair == 3:
                        act.wait_ge(*at("scaled"))
                        for c in range(NCH):
                            A(yT[:, c, :], conv[:, c, :], ACT.Silu, bias=chan[:, 3, c:c + 1],
                              scale=chan[:, 2, c:c + 1]).then_inc(*sets("y_mix", c))
                for hf in range(2):
                    for g in (2 * hf, 2 * hf + 1):
                        k, n = ("pt", NH - 2 + g) if g < 2 else ("pts", g - 2)
                        b2, use2 = banks.of(k, 1, n)
                        act.wait_ge(full[b2], use2)
                        stick_before(g, ("ss", 1, g), ("s", g), T, Pr[g % 2][:, 0:T])
                    for g in (2 * hf, 2 * hf + 1):
                        stick_exp(g, ("s", g), T, Pr[g % 2][:, 0:T])
                    ahead(2, hf, 0)
                    sample_out(1, hf)

            def cross_attention(l):
                stage = 2 * l + 1
                for t in range(TILES):
                    unit_squares(UNIT["cq", l, t])
                    if t:
                        unit_spread(UNIT["cq", l, t - 1])
                unit_spread(UNIT["cq", l, 2])

                def exps(hd):
                    b = take("cs", l, hd)
                    if hd >= 2:
                        b2, use2 = banks.of("cpt", l, hd - 2)
                        act.wait_ge(full[b2], use2)
                    for qt in range(2):
                        ins = softmax_exp((l, "cp", hd), hd, bank[b][:, qt * NMEM:(qt + 1) * NMEM],
                                          Pr[hd % 2][:, qt * NMEM:(qt + 1) * NMEM], qt)
                    ins.then_inc(*sets("exp", l, "cp", hd))

                def cross_out(hf):
                    b = take("cost", l, hf)
                    copy(view(yT[:, 0, :], SEQ + 32 * hf, [[T, XH], [8, 4], [1, NS]]),
                         view(bank[b][:, :], 0, [[P + 8, XH], [32, 4], [1, NS]])).then_inc(free[b], 1)

                exps(0)
                for hd in range(XH):
                    if hd + 1 < XH:
                        exps(hd + 1)
                    b = take("cpt", l, hd)
                    copy(PT[hd % 2][:, :], bank[b][:, :]).then_inc(free[b], 1)
                    keys_out(stage, 0, [2 * hd, 2 * hd + 1])
                    b = take("co", l, hd)
                    copy(yT[:, hd, 0:SEQ], bank[b][:, 0:SEQ]).then_inc(free[b], 1)
                for hf in range(2):
                    b = take("css", l, hf)
                    softmax_exp((l, "cs", hf), hf, bank[b][:, 0:NMEM], Pr[hf][:, 0:NMEM]).then_inc(*sets("exp", l, "cs", hf))
                    if hf:
                        cross_out(0)
                    ahead(stage, hf, 0)
                    b = take("cpts", l, hf)
                    copy(PT[hf][:, 0:2 * P], bank[b][:, 0:2 * P]).then_inc(free[b], 1)
                    ahead(stage, hf, 1)
                    b = take("cos", l, hf)
                    copy(osam[hf], bank[b][:, :]).then_inc(free[b], 1)
                    ahead(stage, hf, 2)
                cross_out(1)

            def state_out(name):
                for n, (src, rows) in enumerate((("p", P), ("s", NSAMP))):
                    b = take(name, src)
                    copy(PT[n][0:rows, :], bank[b][0:rows, :]).then_inc(free[b], 1)

            for p_ in prime["act"]:
                act.sem_inc(p_, 1)

            def const_load(dst, src):
                act.dma_start(dst, src).then_inc(*sets("const_in", by=16))

            act.dma_start(hg[:, 384:512], spread(a["g_ck"][0])).then_inc(*sets("ck_gain_in", by=16))
            act.dma_start(hg2[:, :], spread(a["g_ck"][1])).then_inc(*sets("ck_gain_in", by=16))
            const_load(g_fq, spread(a["g_fq"][0]))
            const_load(hg[:, 64:128], spread(a["g_fk"][0]))
            for l in range(2):
                const_load(g_cq[l], spread(a["g_cq"][l]))
            const_load(b_f, spread(a["b_f"][0]))
            const_load(b_r, spread(a["b_router"][0]))
            const_load(wfl, a["w_in_e"][0].rearrange("(k p) n -> p k n", p=P)[:, :, 4 * HALF:4 * HALF + NH])
            const_load(wrt, a["w_router"][0].rearrange("(k p) n -> p k n", p=P))
            const_load(wpg, a["w_pool_grp"][0].rearrange("g c d -> c g d"))
            for n, name in enumerate(("pool_scale", "conv_b", "ln_g", "ln_b")):
                const_load(PT[1][n:n + 1, :], a[name])
            const_load(PT[1][4:4 + CW, :], a["conv_w"][0])
            memory(0)
            b = take("chan")
            copy(chan_t[:, :], bank[b][:, 0:(4 + CW) * NCH]).then_inc(free[b], 1)
            norm_squares(0)
            to_hT(0, range(TILES))
            inputs(0)
            act.wait_ge(*at("forget_abs"))
            A(lf_e, lf_a, ACT.Exp, scale=-1.0).then_inc(*sets("forget_exp"))
            act.wait_ge(*at("forget_exp"))
            A(lf_l, lf_e, ACT.Ln, bias=1.0).then_inc(*sets("forget_log"))
            for g in range(NCH):
                b = take("p", g)
                copy(poolF[:, g, PBUF:PSEG], bank[b][:, 0:SEQ])
                copy(pool_new[:, g, :], bank[b][:, SEQ:T])
                copy(view(poolF[:, g, :], PSEG + PBUF, [[SSEG, NB], [1, NS]]),
                     view(bank[b][:, :], SEQ, [[NS, NB], [1, NS]])).then_inc(free[b], 1)
            act.wait_ge(*at("logf"))
            for t in range(2):
                ins = copy(lr[:, t], view(logf[:, t, :], 0, [[1, NH], [0, P]]))
            ins.then_inc(*sets("lr", 0))
            state_out("pst")
            for g in range(NCH):
                b = take("pm", g)
                A(yT[:, g, :], bank[b][:, 0:T], ACT.Copy, scale=chan[:, 0, g:g + 1]).then_inc(free[b], 1)
            forget_attention()
            norm_squares(1)
            to_hT(1, range(TILES))
            cross_attention(0)
            norm_squares(2)
            for t in range(TILES):
                for kh in range(2):
                    b = take("tc", 2, t, kh)
                    copy(ffn_x[:, 4 * kh:4 * kh + 4, t * P:t * P + ROWS[t]],
                         bank[b][:, :].rearrange("p (k c) -> p k c", k=4)[:, :, 0:ROWS[t]]).then_inc(*sets("x_hi", t, kh))

            def ffn_silu_tile(f2, ff):
                act.wait_ge(ffn_gate, ff + 1)
                A(ffn_s[f2], bank[6][:, 0:T], ACT.Silu).then_inc(ffn_silu, 1)

            ub = [uses_before(1 + s, n0) for s in range(2)]

            def gate_up_hi(blk, i2):
                act.wait_ge(slot_full[1 + blk], i2 * 32 + 16 * (ub[blk] + 2))
                for m in range(2):
                    copy(gu_high[blk][:, m * PIECE:(m + 1) * PIECE], gu_raw[blk][:, m * PIECE:(m + 1) * PIECE]) \
                        .then_inc(ffn_whi, 1)

            def down_hi(blk, i2):
                act.wait_ge(slot_full[3 + blk], i2 * 16 + 16)
                copy(dn_high[blk], dn_raw[blk]).then_inc(ffn_whi, 1)

            def ffn_tiles(blk, ff, silu_read=None):
                for f2 in range(2):
                    if silu_read is not None:
                        act.wait_ge(ffn_h, silu_read + f2)
                    ffn_silu_tile(f2, ff + f2)
                    if f2 == 0 and blk is not None:
                        gate_up_hi(*blk)
                if blk is not None:
                    down_hi(*blk)

            gate_up_hi(0, 0)
            down_hi(0, 0)
            ffn_tiles((1, 0), 0)
            with act.Fori(0, FBLK // 2 - 1) as i:
                ffn_tiles((0, i + 1), i * 4 + 2, i * 4 + 1)
                ffn_tiles((1, i + 1), i * 4 + 4, i * 4 + 3)
            ffn_tiles((0, FBLK // 2), 2 * FBLK - 4, 2 * FBLK - 5)
            ffn_tiles(None, 2 * FBLK - 2, 2 * FBLK - 3)

            memory(1)
            norm_squares(3)
            to_hT(3, range(TILES))
            for t in range(2):
                act.wait_ge(*at(f"u_out{UNIT['mk', 1, t] % 2}", UNIT["mk", 1, t]))
            for c in range(NCH):
                b = take("g", c)
                if c >= 2:
                    act.wait_ge(*taken("a", c - 2))
                A(S[c % 2], bank[b][:, 0:T], ACT.Sigmoid).then_inc(free[b], 1)
            inputs(1)
            stick_attention()
            norm_squares(4)
            to_hT(4, range(TILES))
            cross_attention(1)
            norm_squares(5)
            to_hT(5, range(TILES))
            act.wait_ge(*at("gap"))
            A(gw[:, :, 1:2], gw[:, :, 0:1], ACT.Exp).then_inc(*sets("gap_exp"))

            def weights_hi(n, b):
                for i in (2 * b, 2 * b + 1):
                    act.wait_ge(raw_full[i % PRING], 16 * (n * (NPIECE // PRING) + (i // PRING + 1)))
                    copy(high[i % PRING], raw[i % PRING]).then_inc(moe_hi, 1)

            def tokens_hi(n):
                for half in range(2):
                    act.wait_ge(*primed(moe_gathered, n * 2 + (half + 1)))
                    copy(moe_x[0][:, 4 * half:4 * half + 4, :], bank[7 - half][:, :].rearrange("p (k c) -> p k c", k=4)) \
                        .then_inc(moe_xhi, 1)

            def expert(n, last):
                def silu(j):
                    act.wait_ge(*used(n, 0, j))
                    act.wait_ge(*primed(moe_h, n * STAGES + max(j - 1, 0)))
                    A(moe_sg[j % 2], bank[j % 2][:, :], ACT.Silu).then_inc(moe_silu, 1)

                def hidden_hi(j):
                    act.wait_ge(*primed(moe_tr, n * STAGES + (j + 1)))
                    if j:
                        act.wait_ge(*used(n, 2, j - 1))
                    else:
                        act.wait_ge(*primed(moe_used, n * NPIECE))
                    copy(moe_hidT[0], bank[6][:, :]).then_inc(moe_hThi, 1)

                for b, (m, j) in enumerate(PRODUCTS):
                    if b == len(PRODUCTS) - 1:
                        hidden_hi(STAGES - 1)
                    if b + 2 < len(PRODUCTS) or not last:
                        weights_hi(n, b + 2)
                    if m == 0:
                        silu(j)
                        if j:
                            hidden_hi(j - 1)
                    if (m, j) == (1, STAGES - 1) and not last:
                        tokens_hi(n + 1)
                act.wait_ge(*used(n, 2, STAGES - 1))
                act.wait_ge(moe_scattered, n * 6 + 6)
                for hf in range(2):
                    copy(moe_y[:, hf * HALF:(hf + 1) * HALF], bank[4 + hf][:, :]).then_inc(moe_yc, 1)

            def expert_round(r):
                act.wait_ge(moe_zero, r + 1)
                weights_hi(r * NE, 0)
                tokens_hi(r * NE)
                weights_hi(r * NE, 1)
                with act.Fori(0, NE - 1) as e:
                    expert(e + r * NE, False)
                expert(r * NE + (NE - 1), True)
                act.wait_ge(moe_scatteredE, (r + 1) * 6)

            expert_round(0)
            act.wait_ge(*at("cmax"))
            most = act.value_load(cmax_i[0:1, 0:1])
            with act.If(most > CAP):
                with act.Fori(1, ROUNDS) as r:
                    expert_round(r)

        @block.vector
        def _(dve):
            V = nc.vector
            steps = [0]
            dve_step = sem("dve_step")

            def step(ins):
                ins.then_inc(dve_step, 1)
                steps[0] += 1
                dve.wait_ge(dve_step, steps[0])

            def take(*key):
                b, use = banks.of(*key)
                dve.wait_ge(full[b], use)
                return b

            def to_hT(j, tiles):
                for t in tiles:
                    b = take("tc", j, t, 1)
                    V.tensor_copy(hT[:, 4:8, t * P:t * P + ROWS[t]],
                                  bank[b][:, :].rearrange("p (k c) -> p k c", k=4)[:, :, 0:ROWS[t]]) \
                        .then_inc(free[b], 1)

            def unit(u):
                kind, l, t = UNITS[u]
                r = ROWS[t]
                i = u % 2
                nb = nbuf[i][0:r, :]
                if l == 1 and kind in "qk":
                    b = take("z", kind, l, t)
                    unit_buffer_free(u)
                    V.tensor_scalar(nb, bank[b][0:r, :], HD ** -0.5 if kind == "q" else 1.0, None, ALU.mult) \
                        .then_inc(*sets("unit", u))
                    dve.wait_ge(*at("unit", u))
                    freed(b)
                    return
                hd = HD if kind in "qk" else XHD
                nh = HALF // hd
                b, use = banks.of("z", kind, l, t)
                dve.wait_ge(*at("u_sq", u))
                if u >= 2 and ("u_rs", u - 2) in marks.known:
                    dve.wait_ge(*at("u_ms", u - 2))
                V.tensor_reduce(u_ss[i][0:r, 0:nh], Pr[i][0:r, :].rearrange("p (h d) -> p h d", h=nh), AX, ALU.add) \
                    .then_inc(*sets("u_ss", u))
                unit_buffer_free(u)
                dve.wait_ge(*at("u_rs", u))
                V.tensor_tensor(nb.rearrange("p (h d) -> p h d", h=nh),
                                bank[b][0:r, :].rearrange("p (h d) -> p h d", h=nh),
                                view(u_rs[i][0:r, 0:nh], 0, [[1, nh], [0, hd]]), ALU.mult).then_inc(free[b], 1)
                dve.wait_ge(free[b], use)
                g = {"q": g_fq, "k": g_fk, "cq": g_cq[l], "mk": g_ck[l]}[kind]
                V.tensor_tensor(nb.rearrange("p (h d) -> p h d", h=nh), nb.rearrange("p (h d) -> p h d", h=nh),
                                view(g[0:r, :], 0, [[0, nh], [1, hd]]), ALU.mult).then_inc(*sets("unit", u))

            def freed(b):
                dve.sem_inc(free[b], 1)

            def unit_buffer_free(u):
                if u >= 2:
                    take("ut", u - 2)
                    name = f"u_out{u % 2}"
                    last = max([w for w in range(u - 1) if (name, w) in marks.known], default=None)
                    if last is not None:
                        dve.wait_ge(*at(name, last))

            def norm(j):
                for t in range(TILES):
                    r = ROWS[t]
                    if t == 0:
                        dve.wait_ge(*at("gain", j))
                        if j:
                            last = {1: ("wo", 0, 1, 2), 2: ("wc", 0, 1, 2), 3: ("tc", ("mem", 1), 1, 1),
                                    4: ("wo", 1, 1, 2), 5: ("wc", 1, 1, 2)}[j]
                        else:
                            last = ("tc", ("mem", 0), 1, 1)
                        take(*last)
                    dve.wait_ge(*at("n_rs", j, t))
                    V.scalar_tensor_tensor(h[0:r, t, :], x[0:r, t, :], n_rs[0:r, t:t + 1], gain[0:r, :],
                                           ALU.mult, ALU.mult).then_inc(*sets("h", j, t))

            def residual(name, l, j):
                for hf in range(2):
                    for t in range(TILES):
                        b = take(name, l, hf, t)
                        xs = x[0:ROWS[t], t, hf * HALF:(hf + 1) * HALF]
                        V.tensor_tensor(xs, xs, bank[b][0:ROWS[t], :], ALU.add).then_inc(free[b], 1)
                        if hf == 1:
                            dve.wait_ge(*taken(name, l, 1, t))
                            dve.sem_inc(*sets("x", j, t))

            def keys_out(stage, hf, js):
                for j in js:
                    if j % 2:
                        b = take("kt", stage, hf, j)
                        V.tensor_copy(kT[:, :, j // 2, (j % 2) * P:(j % 2 + 1) * P],
                                      bank[b][:, :].rearrange("p (c k) -> p c k", c=4)).then_inc(free[b], 1)

            def normalize(key, i, probs, ncol=1):
                dve.wait_ge(*at("exp", *key))
                step(V.reciprocal(a_rc[i % 4][:, 0:ncol], a_sm[i % 4][:, 0:ncol]))
                if ncol == 1:
                    return V.tensor_scalar(probs, probs, a_rc[i % 4][:, 0:1], None, ALU.mult)
                p3 = probs.rearrange("p (q k) -> p q k", q=2)
                return V.tensor_tensor(p3, p3, view(a_rc[i % 4], 0, [[1, 2], [0, NMEM]]), ALU.mult)

            def forget_attention():
                def scores(i):
                    hd, qt = i // 2, i % 2
                    nk = (qt + 1) * P
                    b = take("s", 0, hd, qt)
                    if i >= 2:
                        dve.wait_ge(*at("exp", 0, "p", (i - 2) // 2, qt))
                    V.scalar_tensor_tensor(S[qt][:, 0:nk], bank[b][:, 0:nk], Fq[:, qt, hd:hd + 1],
                                           C("causal" if qt == 0 else "zeros", 0, nk), ALU.add, ALU.add).then_inc(free[b], 1)
                    dve.wait_ge(*taken("s", 0, hd, qt))
                    V.reduce_max(a_nm[i % 4][:, 0:1], S[qt][:, 0:nk], AX, negate=True) \
                        .then_inc(*sets("neg_max", 0, "p", hd, qt))

                def finish(i):
                    hd, qt = i // 2, i % 2
                    normalize((0, "p", hd, qt), i, Pr[hd % 2][:, qt * P:(2 * qt + 1) * P]) \
                        .then_inc(*sets("probs", 0, "p", hd, qt))

                for i in range(2 * NH):
                    scores(i)
                    if i >= 2:
                        finish(i - 2)
                    if i % 2 and i >= 3:
                        keys_out(0, 0, [i // 2 - 1])
                finish(2 * NH - 2)
                finish(2 * NH - 1)
                keys_out(0, 0, [NH - 1])
                for hf in range(2):
                    for g in (2 * hf, 2 * hf + 1):
                        b = take("ss", 0, g)
                        i = 2 * NH + g
                        new = bank[b][:, PAST:T]
                        step(V.tensor_tensor(new, new, C("new_causal", g * NSAMP, NSAMP), ALU.add))
                        V.reduce_max(a_nm[i % 4][:, 0:1], bank[b][:, 0:T], AX, negate=True) \
                            .then_inc(*sets("neg_max", 0, "s", g))
                    for g in (2 * hf, 2 * hf + 1):
                        normalize((0, "s", g), 2 * NH + g, Pr[g % 2][:, 0:T]).then_inc(*sets("probs", 0, "s", g))
                        freed(banks.of("ss", 0, g)[0])
                    if not hf:
                        keys_out(0, 1, range(8))

            def stick(i, bkey, ukey, n, probs, masked, mask):
                b, use = banks.of(*bkey)
                dve.wait_ge(*at("log1p", *ukey))
                Sn, Ln = S[i % 2][:, 0:n], L[i % 2][:, 0:n]
                step(V.scalar_tensor_tensor(Sn, bank[b][:, 0:n], 0.0, Ln, ALU.max, ALU.add))
                m = Sn[:, masked:n]
                V.scalar_tensor_tensor(Ln, bank[b][:, 0:n], 0.0, Ln, ALU.min, ALU.subtract).then_inc(free[b], 1)
                step(V.tensor_tensor(m, m, mask, ALU.mult))
                step(V.tensor_tensor_scan(probs, Sn, Sn, 0.0, ALU.add, ALU.bypass))
                step(V.tensor_tensor(Ln, Ln, probs, ALU.add))
                V.tensor_scalar(a_nm[i % 4][:, 0:1], probs[:, n - 1:n], -1.0, None, ALU.mult) \
                    .then_inc(*sets("log_a", *ukey))

            def stick_finish(ukey, probs, masked, mask, key):
                dve.wait_ge(*at("stick_exp", *ukey))
                m = probs[:, masked:]
                V.tensor_tensor(m, m, mask, ALU.mult).then_inc(*sets("probs", 1, *key))

            def stick_attention():
                strict2 = view(C("strict"), 0, [[0, 2], [1, P]])

                def diagonal(a384):
                    return view(a384, 0, [[2 * P, 2], [1, P]])

                def log_weights(pair):
                    heads = (2 * pair, 2 * pair + 1)
                    for hd in heads:
                        b, _use = banks.of("s", 1, hd)
                        z, Sn, Ln = bank[b][:, 0:3 * P], stick_S[hd % 4], stick_L[hd % 4]
                        dve.wait_ge(*at("log1p", hd))
                        V.scalar_tensor_tensor(Sn, z, 0.0, Ln, ALU.max, ALU.add).then_inc(*sets("softplus", hd))
                        dve.wait_ge(*at("softplus", hd))
                        V.scalar_tensor_tensor(Ln, z, 0.0, Ln, ALU.min, ALU.subtract).then_inc(free[b], 1)
                    for hd in heads:
                        m = diagonal(stick_S[hd % 4])
                        V.tensor_tensor(m, m, strict2, ALU.mult).then_inc(*sets("masked", hd))
                    for hd in heads:
                        if hd >= 4:
                            take("pt", 1, hd - 4)
                        dve.wait_ge(*at("masked", hd))
                        V.tensor_tensor_scan(stick_P[hd % 4], stick_S[hd % 4], stick_S[hd % 4], 0.0,
                                             ALU.add, ALU.bypass).then_inc(*sets("summed", hd))
                    for hd in heads:
                        dve.wait_ge(*at("summed", hd))
                        V.tensor_scalar(a_nm[hd % 4][:, 0:2], view(stick_P[hd % 4], P - 1, [[2 * P, 2]]), -1.0, None,
                                        ALU.mult)
                        V.tensor_tensor(stick_L[hd % 4], stick_L[hd % 4], stick_P[hd % 4], ALU.add) \
                            .then_inc(*sets("log_a", hd))

                def finish(pair):
                    for hd in (2 * pair, 2 * pair + 1):
                        dve.wait_ge(*at("stick_exp", hd))
                        m = diagonal(stick_P[hd % 4])
                        V.tensor_tensor(m, m, strict2, ALU.mult).then_inc(*sets("probs", 1, "p", hd))

                log_weights(0)
                for u in (UNIT["k", 1, 1], UNIT["k", 1, 2]):
                    unit_buffer_free(u + 2)
                b = take("lvar")
                step(V.memset(ln_var, 1.0))
                V.tensor_scalar(ln_var[:, 0:2], bank[b][:, 0:2], 1.0 / HALF, EPS, ALU.mult, ALU.add)
                V.tensor_scalar(ln_var[0:NSAMP, 2:3], bank[b][0:NSAMP, 2:3], 1.0 / HALF, EPS, ALU.mult, ALU.add) \
                    .then_inc(free[b], 1)
                dve.wait_ge(*taken("lvar"))
                dve.sem_inc(*sets("ln_var"))
                log_weights(1)
                dve.wait_ge(*at("ln_rs"))
                for t in range(TILES):
                    r = ROWS[t]
                    ins = V.tensor_scalar(S_t[0:r, t * P:t * P + r], ident[0:r, 0:r], ln_rs[0:r, t:t + 1], None, ALU.mult)
                ins.then_inc(*sets("ln_diag"))
                for pair in range(NH // 2):
                    finish(pair)
                    if pair + 2 < NH // 2:
                        log_weights(pair + 2)
                    keys_out(2, 0, [2 * pair, 2 * pair + 1])
                    if pair == 0:
                        b = take("lrs")
                        V.tensor_tensor(conv, conv, view(bank[b][:, :], 0, [[0, NCH], [1, T]]), ALU.mult).then_inc(free[b], 1)
                        dve.wait_ge(*taken("lrs"))
                        dve.sem_inc(*sets("scaled"))
                for hf in range(2):
                    gs = (2 * hf, 2 * hf + 1)
                    for g in gs:
                        stick(g, ("ss", 1, g), ("s", g), T, Pr[g % 2][:, 0:T], PAST, C("new_strict", g * NSAMP, NSAMP))
                    for g in gs:
                        stick_finish(("s", g), Pr[g % 2][:, 0:T], PAST, C("new_strict", g * NSAMP, NSAMP), ("s", g))
                    if not hf:
                        keys_out(2, 1, range(8))

            def cross_attention(l):
                stage = 2 * l + 1
                for t in range(TILES):
                    unit(UNIT["cq", l, t])

                def scores(hd):
                    b = take("cs", l, hd)
                    V.reduce_max(a_nm[hd % 4], bank[b][:, :].rearrange("p (q k) -> p q k", q=2), AX, negate=True) \
                        .then_inc(*sets("neg_max", l, "cp", hd))

                scores(0)
                for hd in range(XH):
                    if hd + 1 < XH:
                        scores(hd + 1)
                    normalize((l, "cp", hd), hd, Pr[hd % 2], 2).then_inc(*sets("probs", l, "cp", hd))
                    freed(banks.of("cs", l, hd)[0])
                    keys_out(stage, 0, [2 * hd, 2 * hd + 1])
                for hf in range(2):
                    b = take("css", l, hf)
                    V.reduce_max(a_nm[hf][:, 0:1], bank[b][:, 0:NMEM], AX, negate=True) \
                        .then_inc(*sets("neg_max", l, "cs", hf))
                    normalize((l, "cs", hf), hf, Pr[hf][:, 0:NMEM]).then_inc(*sets("probs", l, "cs", hf))
                    freed(b)
                    if not hf:
                        keys_out(stage, 1, range(8))

            def memory(l):
                to_hT(("mem", l), range(2))
                for t in range(2):
                    unit(UNIT["mk", l, t])

            for p_ in prime["dve"]:
                dve.sem_inc(p_, 1)
            dve.wait_ge(*at("ck_gain_in"))
            step(V.memset(lf[:, :], 0.0))
            step(V.memset(route[:, :], 0.0))
            step(V.memset(poolF[:, :, 0:PBUF], 0.0))
            memory(0)
            norm(0)
            to_hT(0, range(TILES))
            dve.wait_ge(*at("scaled_gain"))
            dve.wait_ge(*at("const_in"))
            dve.wait_ge(*at("table_in"))
            for n, (k, t) in enumerate(ZSEQ[0]):
                if k != "v":
                    unit(UNIT[k, 0, t])
            b = take("fl")
            for t in range(TILES):
                r = ROWS[t]
                ins = V.tensor_tensor(lf_y[0:r, t, :], bank[b][0:r, 8 * t:8 * t + 8], b_f[0:r, :], ALU.add)
            ins.then_inc(free[b], 1)
            dve.wait_ge(*taken("fl"))
            V.scalar_tensor_tensor(lf_a, lf_y, -1.0, lf_y, ALU.mult, ALU.max).then_inc(*sets("forget_abs"))
            b = take("pre")
            V.tensor_copy(view(poolF[:, 0, :], PSEG, [[PFLAT, NCH], [SSEG, NB], [1, PBUF]]),
                          view(bank[b][:, :], 0, [[120, NCH], [PBUF, NB], [1, PBUF]])).then_inc(free[b], 1)
            dve.wait_ge(*at("forget_log"))
            V.scalar_tensor_tensor(logf, lf_y, 0.0, lf_l, ALU.min, ALU.subtract).then_inc(*sets("logf"))
            dve.wait_ge(*taken("pre"))
            for u in (UNIT["k", 0, 1], UNIT["k", 0, 2]):
                unit_buffer_free(u + 2)
            for g, w in enumerate(WINDOWS):
                dve.wait_ge(*taken("p", g))
                f = poolF[:, g, :]
                src, lo = f, 0
                for i in range(g + 1):
                    dst = (S_t[:, 0:PFLAT], Pr_t[:, 0:PFLAT])[i % 2]
                    d = 1 << i
                    step(V.tensor_tensor(dst[:, lo + d:], src[:, lo + d:], src[:, lo:PFLAT - d], ALU.add))
                    src, lo = dst, lo + d
                if g >= 2:
                    take("pm", g - 2)
                out = L_t[:, (g % 2) * T:(g % 2 + 1) * T]
                new = lambda q: view(q, PSEG + PBUF, [[SSEG, NB], [1, NS]])
                V.scalar_tensor_tensor(out[:, SEQ:T].rearrange("p (b s) -> p b s", b=NB), new(src), 1.0 / w, new(f),
                                       ALU.mult, ALU.subtract)
                V.scalar_tensor_tensor(out[:, 16:SEQ], src[:, PBUF + 16:PSEG], 1.0 / w, f[:, PBUF + 16:PSEG],
                                       ALU.mult, ALU.subtract)
                step(V.tensor_tensor(out[:, 0:16], src[:, PBUF:PBUF + 16], C("inv_count", 16 * g, 16), ALU.mult))
                V.tensor_tensor(out[:, 0:16], out[:, 0:16], f[:, PBUF:PBUF + 16], ALU.subtract) \
                    .then_inc(*sets("pool_d", g))
                dve.wait_ge(*at("pool_d", g))
            b = take("Fq")
            V.tensor_copy(Fq, bank[b][:, 0:16].rearrange("p (t h) -> p t h", t=2)).then_inc(free[b], 1)
            dve.wait_ge(*taken("Fq"))
            forget_attention()
            residual("wo", 0, 1)
            norm(1)
            to_hT(1, range(TILES))
            cross_attention(0)
            residual("wc", 0, 2)
            norm(2)
            dve.wait_ge(*at("v_out", 0))
            for t in range(TILES):
                for kh in range(2):
                    b, _use = banks.of("tc", 2, t, kh)
                    dve.wait_ge(*at("x_hi", t, kh))
                    cols = slice(t * P, t * P + ROWS[t])
                    V.tensor_tensor(ffn_xlo[kh][:, :, cols],
                                    bank[b][:, :].rearrange("p (k c) -> p k c", k=4)[:, :, 0:ROWS[t]],
                                    ffn_x[:, 4 * kh:4 * kh + 4, cols].bitcast(F32), ALU.subtract).then_inc(free[b], 1)

            def ffn_mul(f2, ff):
                dve.wait_ge(ffn_up, ff + 1)
                dve.wait_ge(ffn_silu, ff + 1)
                V.tensor_tensor(ffn_hid[f2], ffn_s[f2], bank[7][:, 0:T], ALU.mult).then_inc(ffn_h, 1)
                dve.wait_ge(ffn_h, ff + 1)
                V.tensor_copy(ffn_hhi[f2], ffn_hid[f2]).then_inc(ffn_hsplit, 1)
                dve.wait_ge(ffn_hsplit, ff + 1)
                V.tensor_tensor(ffn_hlo[f2], ffn_hid[f2], ffn_hhi[f2].bitcast(F32), ALU.subtract) \
                    .then_inc(ffn_hlo_ready, 1)

            def gate_up_lo(blk, parts):
                for m in range(2):
                    dve.wait_ge(ffn_whi, parts + (m + 1))
                    cols = slice(m * PIECE, (m + 1) * PIECE)
                    V.tensor_tensor(gu_low[blk][:, cols], gu_raw[blk][:, cols], gu_high[blk][:, cols].bitcast(F32),
                                    ALU.subtract).then_inc(ffn_wlo, 1)

            def down_lo(blk, parts):
                dve.wait_ge(ffn_whi, parts + 3)
                V.tensor_tensor(dn_low[blk], dn_raw[blk], dn_high[blk].bitcast(F32), ALU.subtract) \
                    .then_inc(ffn_wlo, 1)

            def ffn_tiles(blk, parts, ff, hidden_used=None):
                for f2 in range(2):
                    if hidden_used is not None:
                        dve.wait_ge(ffn_down, hidden_used + f2)
                    ffn_mul(f2, ff + f2)
                    if f2 == 0 and blk is not None:
                        gate_up_lo(blk, parts)
                if blk is not None:
                    down_lo(blk, parts)

            gate_up_lo(0, 0)
            down_lo(0, 0)
            ffn_tiles(1, 3, 0)
            with dve.Fori(0, FBLK // 2 - 1) as i:
                ffn_tiles(0, i * 6 + 6, i * 4 + 2, i * 4 + 1)
                ffn_tiles(1, i * 6 + 9, i * 4 + 4, i * 4 + 3)
            ffn_tiles(0, 3 * FBLK - 3, 2 * FBLK - 4, 2 * FBLK - 5)
            ffn_tiles(None, None, 2 * FBLK - 2, 2 * FBLK - 3)
            dve.wait_ge(ffn_down, 2 * FBLK)
            for hf in range(2):
                for t in range(TILES):
                    xs = x[0:ROWS[t], t, hf * HALF:(hf + 1) * HALF]
                    V.tensor_tensor(xs, xs, bank[3 * hf + t][0:ROWS[t], :], ALU.add).then_inc(*sets("ffn_out", hf, t))
            for t in range(TILES):
                dve.wait_ge(*at("ffn_out", 1, t))
                dve.sem_inc(*sets("x", 3, t))

            memory(1)
            norm(3)
            to_hT(3, range(TILES))
            step(V.memset(convF[:, :, 0:CBUF], 0.0))
            for n in range(2):
                b = take("cpre", n)
                V.tensor_copy(view(convF[:, 0, :], CSEG + 4 * n * DSEG, [[CFLAT, NCH], [DSEG, 4], [1, CBUF]]),
                              view(bank[b][:, :], 0, [[120, NCH], [CBUF, 4], [1, CBUF]])).then_inc(free[b], 1)
            for c in range(NCH):
                dve.wait_ge(*taken("g", c))
                b = take("a", c)
                V.tensor_tensor(convF[:, c, CBUF:CSEG], bank[b][:, 0:SEQ], S[c % 2][:, 0:SEQ], ALU.mult)
                V.tensor_tensor(conv_new[:, c, :], bank[b][:, SEQ:T], S[c % 2][:, SEQ:T], ALU.mult)
                V.tensor_tensor(view(convF[:, c, :], CSEG + CBUF, [[DSEG, NB], [1, NS]]),
                                view(bank[b][:, :], SEQ, [[NS, NB], [1, NS]]),
                                S[c % 2][:, SEQ:T].rearrange("p (b s) -> p b s", b=NB), ALU.mult).then_inc(free[b], 1)
            for n in range(2):
                dve.wait_ge(*taken("cpre", n))
            order = [UNIT[k, 1, t] for k, t in ZSEQ[1] if k != "v"]
            for c in range(NCH):
                dve.wait_ge(*taken("a", c))
                accp = conv[:, c, 0:SEQ]
                inp = lambda j: view(convF[:, c, :], j, [[1, SEQ]])
                V.tensor_scalar(accp, inp(0), cw[:, 0, c:c + 1], chan[:, 1, c:c + 1], ALU.mult, ALU.add) \
                    .then_inc(conv_p, 1)
                for j in range(1, CW):
                    dve.wait_ge(conv_p, c * CW + j)
                    V.scalar_tensor_tensor(accp, inp(j), cw[:, j, c:c + 1], accp, ALU.mult, ALU.add) \
                        .then_inc(conv_p, 1)
                for u in order[2 * c:2 * c + 2]:
                    unit(u)
                dve.wait_ge(*at("taps", c))
                V.tensor_reduce(conv[:, c, SEQ:T], taps.rearrange("p (t j) -> p t j", j=CW), AX, ALU.add) \
                    .then_inc(conv_s, 1)
                dve.wait_ge(conv_s, c + 1)
                V.tensor_scalar(conv[:, c, SEQ:T], conv[:, c, SEQ:T], chan[:, 1, c:c + 1], None, ALU.add) \
                    .then_inc(*sets("conv_bias", c))
            dve.wait_ge(*at("conv_bias", NCH - 1))
            dve.wait_ge(conv_p, NCH * CW)
            dve.sem_inc(*sets("conv"))
            b = take("lmean")
            V.scalar_tensor_tensor(conv, view(bank[b][:, :], 0, [[0, NCH], [1, T]]), -1.0 / HALF, conv, ALU.mult, ALU.add).then_inc(free[b], 1)
            dve.wait_ge(*taken("lmean"))
            dve.sem_inc(*sets("cent"))
            stick_attention()
            residual("wo", 1, 4)
            norm(4)
            to_hT(4, range(TILES))
            cross_attention(1)
            residual("wc", 1, 5)
            norm(5)
            to_hT(5, range(TILES))

            b = take("rt")
            for t in range(TILES):
                r = ROWS[t]
                ins = V.tensor_tensor(lg[0:r, t, :], bank[b][0:r, 8 * t:8 * t + 8], b_r[0:r, :], ALU.add)
            ins.then_inc(free[b], 1)
            dve.wait_ge(*taken("rt"))
            for t in range(TILES):
                ins = V.max(m8[:, t, :], lg[:, t, :])
            step(ins)
            for t in range(TILES):
                ins = V.max_index(idx[:, t, :], m8[:, t, :], lg[:, t, :])
            step(ins)
            V.tensor_tensor(gw[:, :, 0:1], m8[:, :, 1:2], m8[:, :, 0:1], ALU.subtract).then_inc(*sets("gap"))
            step(V.tensor_copy(idxf, idx))
            iota8 = view(C("iota"), 0, [[0, 3], [1, NE]])
            V.tensor_tensor(pk1, iota8, view(idxf[:, 0, :], 0, [[8, 3], [0, NE]]), ALU.is_equal)
            step(V.tensor_tensor(pk2, iota8, view(idxf[:, 0, :], 1, [[8, 3], [0, NE]]), ALU.is_equal))
            V.tensor_tensor(picked, pk1, pk2, ALU.add).then_inc(*sets("picked"))
            dve.wait_ge(*at("gap_exp"))
            step(V.tensor_scalar(gw[:, :, 2:3], gw[:, :, 1:2], 1.0, None, ALU.add))
            step(V.reciprocal(gw[:, :, 3:4], gw[:, :, 2:3]))
            step(V.tensor_tensor(gw[:, :, 4:5], gw[:, :, 3:4], gw[:, :, 1:2], ALU.mult))
            step(V.tensor_tensor(pk1, pk1, view(gw[:, 0, :], 3, [[8, 3], [0, NE]]), ALU.mult))
            step(V.tensor_tensor(pk2, pk2, view(gw[:, 0, :], 4, [[8, 3], [0, NE]]), ALU.mult))
            step(V.tensor_tensor(gates, pk1, pk2, ALU.add))
            b = take("rank")
            FAR = 1048576.0
            for t in range(TILES):
                r = ROWS[t]
                ins = V.scalar_tensor_tensor(posr[0:r, t, :], bank[b][0:r, 8 * t:8 * t + 8], FAR, picked[0:r, t, :],
                                             ALU.add, ALU.mult)
            step(ins)
            step(V.tensor_scalar(posr, posr, -FAR, None, ALU.add))
            V.reduce_max(cmax, bank[b][:, 24:32], AX).then_inc(free[b], 1)
            dve.wait_ge(*taken("rank"))
            V.tensor_copy(cmax_i[:, :], cmax).then_inc(*sets("cmax"))
            dve.wait_ge(*at("cmax"))

            def add_scattered(i, scattered, n, done):
                t, hf = i // 2, i % 2
                dve.wait_ge(scattered, n)
                xs = x[0:ROWS[t], t, hf * HALF:(hf + 1) * HALF]
                V.tensor_tensor(xs, xs, bank[6 + i % 2][0:ROWS[t], :], ALU.add).then_inc(done, 1)

            def select(n, e):
                dve.wait_ge(*primed(moe_gathered, n * 2))
                dve.wait_ge(*primed(moe_GTr, n))
                V.tensor_copy(rcol[:, 0:3], posr[:, :, bass.ds(e, 1)].rearrange("p t e -> p (t e)")) \
                    .then_inc(moe_col, 1)
                V.tensor_copy(rcol[:, 3:6], gates[:, :, bass.ds(e, 1)].rearrange("p t e -> p (t e)")) \
                    .then_inc(moe_col, 1)
                dve.wait_ge(moe_col, n * 2 + 2)
                for t in range(TILES):
                    r = ROWS[t]
                    V.tensor_scalar(moe_G[0:r, t, :], C("iota")[0:r], rcol[0:r, t:t + 1], rcol[0:r, 3 + t:4 + t],
                                    ALU.is_equal, ALU.mult)
                for t in range(TILES):
                    r = ROWS[t]
                    ins = V.tensor_scalar(moe_P[0:r, t, :], C("iota")[0:r], rcol[0:r, t:t + 1], None, ALU.is_equal)
                ins.then_inc(moe_sel, 1)

            def weights_lo(n, b):
                for i in (2 * b, 2 * b + 1):
                    if i % NPIECE in POOLED:
                        continue
                    dve.wait_ge(moe_hi, n * NPIECE + (i + 1))
                    V.tensor_tensor(low[i % PRING], raw[i % PRING], high[i % PRING].bitcast(F32), ALU.subtract) \
                        .then_inc(moe_lo, 1)

            def tokens_lo(n):
                for half in range(2):
                    dve.wait_ge(moe_xhi, n * 2 + (half + 1))
                    V.tensor_tensor(moe_x[1][:, 4 * half:4 * half + 4, :], bank[7 - half][:, :].rearrange("p (k c) -> p k c", k=4),
                                    moe_x[0][:, 4 * half:4 * half + 4, :].bitcast(F32), ALU.subtract) \
                        .then_inc(moe_xT, 1)

            def expert(n, e, last):
                def hidden(j):
                    dve.wait_ge(*used(n, 1, j))
                    dve.wait_ge(*primed(moe_silu, n * STAGES + (j + 1)))
                    dve.wait_ge(*primed(moe_tr, n * STAGES + max(j - 1, 0)))
                    V.tensor_tensor(moe_hid[j % 2], moe_sg[j % 2], bank[2 + j % 2][:, :], ALU.mult) \
                        .then_inc(moe_h, 1)

                def hidden_lo(j):
                    dve.wait_ge(moe_hThi, n * STAGES + (j + 1))
                    V.tensor_tensor(moe_hidT[1], bank[6][:, :], moe_hidT[0].bitcast(F32), ALU.subtract) \
                        .then_inc(moe_hT, 1)

                def add_last(pieces):
                    for i in pieces:
                        dve.wait_ge(*primed(moe_added, n * 6))
                        add_scattered(i, moe_scattered, n * 6 + (i + 1), moe_added)

                for b, (m, j) in enumerate(PRODUCTS):
                    if b == len(PRODUCTS) - 1:
                        hidden_lo(STAGES - 1)
                    if b + 2 < len(PRODUCTS) or not last:
                        weights_lo(n, b + 2)
                    if m == 0 and j < 2:
                        add_last((0, 1) if j == 0 else (4, 5))
                    if m == 0 and j:
                        hidden_lo(j - 1)
                    if m == 1:
                        hidden(j)
                        if j == 0:
                            add_last((2, 3))
                    if m == 2 and j == 0:
                        dve.wait_ge(*primed(moe_GTr, n + 1))
                        V.tensor_copy(moe_GT[:, 0:T], bank[7][:, 0:T]).then_inc(moe_GTc, 1)
                    if (m, j) == (2, 1) and not last:
                        select(n + 1, e + 1)
                    if (m, j) == (1, STAGES - 1) and not last:
                        tokens_lo(n + 1)

            def expert_round(r):
                V.memset(moe_GT, 0.0).then_inc(moe_cleared, 1)
                V.memset(moe_y, 0.0).then_inc(moe_cleared, 1)
                dve.wait_ge(moe_cleared, r * 2 + 2)
                dve.sem_inc(moe_zero, 1)
                select(r * NE, 0)
                weights_lo(r * NE, 0)
                tokens_lo(r * NE)
                weights_lo(r * NE, 1)
                with dve.Fori(0, NE - 1) as e:
                    expert(e + r * NE, e, False)
                expert(r * NE + (NE - 1), NE - 1, True)
                dve.wait_ge(*primed(moe_added, (r + 1) * NE * 6))
                for i in range(6):
                    add_scattered(i, moe_scatteredE, r * 6 + (i + 1), moe_addedE)
                dve.wait_ge(moe_addedE, (r + 1) * 6)

            expert_round(0)
            most = dve.value_load(cmax_i[0:1, 0:1])
            with dve.If(most > CAP):
                with dve.Fori(1, ROUNDS) as r:
                    V.tensor_scalar(posr, posr, float(-CAP), None, ALU.add).then_inc(moe_shift, 1)
                    dve.wait_ge(moe_shift, r)
                    expert_round(r)
            dve.sem_inc(*sets("x_final"))
        out = {"marks": marks.table, "banks": banks.table, "releases": released}
    return out


OUTPUTS = (
    ("y_prompt", (1, SEQ, D)), ("y_sample", (NB, NS, D)),
    ("fox_k_p", (1, 1, SEQ, NH, HD)), ("fox_v_p", (1, 1, SEQ, NH, HD)), ("fox_logf_p", (1, 1, SEQ, NH)),
    ("sb_k_p", (1, 1, SEQ, NH, HD)), ("sb_v_p", (1, 1, SEQ, NH, HD)),
    ("pool_p", (1, 1, PBUF, HALF)), ("conv_p", (1, 1, CBUF, HALF)),
    ("mem_k_p", (2, 1, NMEM, XH, XHD)), ("mem_v_p", (2, 1, NMEM, XH, XHD)),
    ("fox_k_s", (1, NB, NS, NH, HD)), ("fox_v_s", (1, NB, NS, NH, HD)), ("fox_logf_s", (1, NB, NS, NH)),
    ("sb_k_s", (1, NB, NS, NH, HD)), ("sb_v_s", (1, NB, NS, NH, HD)),
    ("pool_s", (1, NB, PBUF, HALF)), ("conv_s", (1, NB, CBUF, HALF)),
)


def kernel(**inputs):
    import numpy as _np
    import concourse.bacc as _bacc
    from concourse import mybir as _mybir
    from concourse.bass_utils import run_bass_kernel_spmd as _run

    arrays = {f"in_{name}": _np.ascontiguousarray(x) for name, x in inputs.items()}
    arrays["in_const_table"] = constants()[0]
    known = {}
    for _ in range(2):
        nc = _bacc.Bacc("TRN2", target_bir_lowering=False, num_devices=1)
        a = {n[3:]: nc.dram_tensor(n, x.shape, _mybir.dt.from_np(x.dtype), kind="ExternalInput").ap()
             for n, x in arrays.items()}
        o = {n: nc.dram_tensor("out_" + n, shape, _mybir.dt.float32, kind="ExternalOutput").ap()
             for n, shape in OUTPUTS}
        known = decoder_step(nc, a, o, known)
    r = _run(nc, [arrays], core_ids=[0])
    return tuple(r.results[0]["out_" + n] for n, _ in OUTPUTS)
```
